# Optimizing a Trainium2 kernel written in Bass

```python
import math
import jax, jax.numpy as jnp
from jax import lax
import numpy as np

D_MODEL = 1024
BATCH = 1
SEQ = 256
DEPTH = 2

MEM_LEN = 256
HEAD_DIM = 64
DIFF_HEADS = 4
DIFF_QK = 32
DIFF_V = 2 * DIFF_QK
MLA_HEADS = 4
MLA_Q_RANK = 256
MLA_KV_RANK = 128
MLA_NOPE = 64
MLA_ROPE = 32
MLA_V = 64
SWA_Q_HEADS = 8
SWA_KV_HEADS = 2
SWA_GROUP = SWA_Q_HEADS // SWA_KV_HEADS
SWA_WINDOW = 128
D_MIX = DIFF_HEADS * DIFF_V + MLA_HEADS * MLA_V + SWA_Q_HEADS * HEAD_DIM
IN_SIZES = [DIFF_HEADS * 2 * DIFF_QK, DIFF_HEADS * 2 * DIFF_QK, DIFF_HEADS * DIFF_V,
            MLA_Q_RANK, MLA_KV_RANK, MLA_ROPE,
            SWA_Q_HEADS * HEAD_DIM, SWA_KV_HEADS * HEAD_DIM, SWA_KV_HEADS * HEAD_DIM]
D_IN = sum(IN_SIZES)
IN_SPLITS = [int(v) for v in np.cumsum(IN_SIZES)[:-1]]
X_HEADS = 4
X_HEAD_DIM = D_MODEL // X_HEADS
D_FF = -(-8 * D_MODEL // (3 * 256)) * 256

N_ALIBI = DIFF_HEADS + SWA_Q_HEADS
QBLK = 128
ROPE_THETA = 10000.0
EPS = 1e-6


def rmsnorm(x, g):
    xf = x.astype(jnp.float32)
    y = xf * lax.rsqrt(jnp.mean(xf * xf, axis=-1, keepdims=True) + EPS)
    return (y * g.astype(jnp.float32)).astype(x.dtype)

def rope(x, pos):
    half = x.shape[-1] // 2
    inv = ROPE_THETA ** (-jnp.arange(half, dtype=jnp.float32) / half)
    ang = pos.astype(jnp.float32)[..., None] * inv
    ang = ang.reshape(ang.shape[:2] + (1,) * (x.ndim - 3) + (half,))
    cos, sin = jnp.cos(ang), jnp.sin(ang)
    xf = x.astype(jnp.float32)
    x1, x2 = xf[..., :half], xf[..., half:]
    return jnp.concatenate([x1 * cos - x2 * sin, x1 * sin + x2 * cos], axis=-1).astype(x.dtype)

def alibi_slopes():
    return 2.0 ** (-8.0 * jnp.arange(1, N_ALIBI + 1, dtype=jnp.float32) / N_ALIBI)

def diff_attention(q, k, v, pos, slopes, lam):
    B, S, H, _ = q.shape
    nblk = S // QBLK
    scale = 1.0 / math.sqrt(DIFF_QK)
    qb = q.reshape(B, nblk, QBLK, H, 2, DIFF_QK).swapaxes(0, 1)
    pb = pos.reshape(B, nblk, QBLK).swapaxes(0, 1)
    k2 = k.reshape(B, S, H, 2, DIFF_QK)

    def one_block(args):
        qi, pi = args
        s = jnp.einsum('bqhmd,bshmd->bmhqs', qi, k2).astype(jnp.float32) * scale
        dist = jnp.abs(pi[:, :, None] - pos[:, None, :]).astype(jnp.float32)
        s = s - slopes[None, None, :, None, None] * dist[:, None, None]
        p = jax.nn.softmax(s, axis=-1)
        a = p[:, 0] - lam * p[:, 1]
        return jnp.einsum('bhqs,bshd->bqhd', a.astype(v.dtype), v)

    out = lax.map(one_block, (qb, pb))
    return out.swapaxes(0, 1).reshape(B, S, H, DIFF_V)

def mla_attention(q, k, v):
    B, S, H, D = q.shape
    nblk = S // QBLK
    scale = 1.0 / math.sqrt(D)
    qb = q.reshape(B, nblk, QBLK, H, D).swapaxes(0, 1)

    def one_block(qi):
        s = jnp.einsum('bqhd,bshd->bhqs', qi, k).astype(jnp.float32) * scale
        p = jax.nn.softmax(s, axis=-1)
        return jnp.einsum('bhqs,bshd->bqhd', p.astype(v.dtype), v)

    out = lax.map(one_block, qb)
    return out.swapaxes(0, 1).reshape(B, S, H * MLA_V)

def swa_attention(q, k, v, pos, slopes, sinks):
    B, S = q.shape[:2]
    W = SWA_WINDOW
    nblk = S // W
    scale = 1.0 / math.sqrt(HEAD_DIM)

    def band(t):
        pad = [(0, 0), (W, W)] + [(0, 0)] * (t.ndim - 2)
        tp = jnp.pad(t, pad).reshape((t.shape[0], nblk + 2, W) + t.shape[2:])
        return jnp.concatenate([tp[:, :-2], tp[:, 1:-1], tp[:, 2:]], axis=2)

    kb, vb, pkb = band(k), band(v), band(pos)
    valid = band(jnp.ones((1, S), dtype=bool))
    qg = q.reshape(B, nblk, W, SWA_KV_HEADS, SWA_GROUP, HEAD_DIM)
    s = jnp.einsum('bnqkgd,bnskd->bnkgqs', qg, kb).astype(jnp.float32) * scale
    pq = pos.reshape(B, nblk, W)
    dist = jnp.abs(pq[..., :, None] - pkb[..., None, :]).astype(jnp.float32)
    s = s - slopes.reshape(SWA_KV_HEADS, SWA_GROUP)[:, :, None, None] * dist[:, :, None, None]
    offs = jnp.arange(3 * W)[None, :] - W - jnp.arange(W)[:, None]
    mask = (jnp.abs(offs) <= W)[None, None] & valid[:, :, None, :]
    s = jnp.where(mask[:, :, None, None], s, jnp.finfo(jnp.float32).min)
    sink = sinks.astype(jnp.float32).reshape(SWA_KV_HEADS, SWA_GROUP)[:, :, None, None]
    m = jnp.maximum(jnp.max(s, axis=-1, keepdims=True), sink)
    e = jnp.exp(s - m)
    p = e / (jnp.sum(e, axis=-1, keepdims=True) + jnp.exp(sink - m))
    o = jnp.einsum('bnkgqs,bnskd->bnqkgd', p.astype(v.dtype), vb)
    return o.reshape(B, S, SWA_Q_HEADS * HEAD_DIM)

def cross_attention(h, mem_n, w_q, w_kv, w_o):
    B, S, _ = h.shape
    M = mem_n.shape[1]
    q = (h @ w_q).reshape(B, S, X_HEADS, X_HEAD_DIM)
    k, v = jnp.split(mem_n @ w_kv, 2, axis=-1)
    k = k.reshape(B, M, X_HEADS, X_HEAD_DIM)
    v = v.reshape(B, M, X_HEADS, X_HEAD_DIM)
    s = jnp.einsum('bqhd,bmhd->bhqm', q, k).astype(jnp.float32) / math.sqrt(X_HEAD_DIM)
    p = jax.nn.softmax(s, axis=-1)
    o = jnp.einsum('bhqm,bmhd->bqhd', p.astype(v.dtype), v).reshape(B, S, D_MODEL)
    return o @ w_o

def first_inputs(seed: int = 0) -> dict:
    key = jax.random.key(seed)
    ks = jax.random.split(key, 32)
    f32 = jnp.float32

    def w(k, shape, fan_in):
        return jax.random.normal(k, shape, f32) * fan_in ** -0.5

    def gain(k, shape):
        return 1.0 + 0.02 * jax.random.normal(k, shape, f32)

    offset = jax.random.randint(ks[2], (BATCH, 1), 0, 1024, dtype=jnp.int32)
    positions = offset + jnp.arange(SEQ, dtype=jnp.int32)[None, :]
    return {
        "x": jax.random.normal(ks[0], (BATCH, SEQ, D_MODEL), f32),
        "mem": jax.random.normal(ks[1], (BATCH, MEM_LEN, D_MODEL), f32),
        "positions": positions,
        "g_mix_pre": gain(ks[3], (DEPTH, D_MODEL)),
        "g_mix_post": gain(ks[4], (DEPTH, D_MODEL)),
        "w_in": w(ks[5], (DEPTH, D_MODEL, D_IN), D_MODEL),
        "diff_lambda": 0.1 * jax.random.normal(ks[6], (DEPTH, 4, DIFF_QK), f32),
        "diff_head_g": gain(ks[7], (DEPTH, DIFF_V)),
        "mla_q_norm_g": gain(ks[8], (DEPTH, MLA_Q_RANK)),
        "mla_w_q_up": w(ks[9], (DEPTH, MLA_Q_RANK, MLA_HEADS * (MLA_NOPE + MLA_ROPE)), MLA_Q_RANK),
        "mla_kv_norm_g": gain(ks[10], (DEPTH, MLA_KV_RANK)),
        "mla_w_kv_up": w(ks[11], (DEPTH, MLA_KV_RANK, MLA_HEADS * (MLA_NOPE + MLA_V)), MLA_KV_RANK),
        "swa_sinks": 0.5 * jax.random.normal(ks[12], (DEPTH, SWA_Q_HEADS), f32),
        "w_out": w(ks[13], (DEPTH, D_MIX, D_MODEL), D_MIX),
        "g_x_pre": gain(ks[14], (DEPTH, D_MODEL)),
        "g_x_mem": gain(ks[15], (DEPTH, D_MODEL)),
        "g_x_post": gain(ks[16], (DEPTH, D_MODEL)),
        "w_xq": w(ks[17], (DEPTH, D_MODEL, D_MODEL), D_MODEL),
        "w_xkv": w(ks[18], (DEPTH, D_MODEL, 2 * D_MODEL), D_MODEL),
        "w_xo": w(ks[19], (DEPTH, D_MODEL, D_MODEL), D_MODEL),
        "g_ffn_pre": gain(ks[20], (DEPTH, D_MODEL)),
        "g_ffn_post": gain(ks[21], (DEPTH, D_MODEL)),
        "w_ffn_in": w(ks[22], (DEPTH, D_MODEL, 2 * D_FF), D_MODEL),
        "w_ffn_out": w(ks[23], (DEPTH, D_FF, D_MODEL), D_FF),
    }

def first_block(x, mem, positions, g_mix_pre, g_mix_post, w_in, diff_lambda, diff_head_g,
              mla_q_norm_g, mla_w_q_up, mla_kv_norm_g, mla_w_kv_up, swa_sinks, w_out,
              g_x_pre, g_x_mem, g_x_post, w_xq, w_xkv, w_xo,
              g_ffn_pre, g_ffn_post, w_ffn_in, w_ffn_out):
    B, S, _ = x.shape
    slopes = alibi_slopes()
    swa_slopes = slopes[:SWA_Q_HEADS]
    diff_slopes = slopes[SWA_Q_HEADS:]

    for l in range(DEPTH):
        h = rmsnorm(x, g_mix_pre[l])
        (a_q, a_k, a_v, b_cq, b_ckv, b_kr, c_q, c_k, c_v) = jnp.split(h @ w_in[l], IN_SPLITS, axis=-1)

        lam_init = 0.8 - 0.6 * math.exp(-0.3 * l)
        lp = diff_lambda[l].astype(jnp.float32)
        lam = jnp.exp(jnp.sum(lp[0] * lp[1])) - jnp.exp(jnp.sum(lp[2] * lp[3])) + lam_init
        o_a = diff_attention(a_q.reshape(B, S, DIFF_HEADS, 2 * DIFF_QK),
                             a_k.reshape(B, S, DIFF_HEADS, 2 * DIFF_QK),
                             a_v.reshape(B, S, DIFF_HEADS, DIFF_V),
                             positions, diff_slopes, lam)
        o_a = (rmsnorm(o_a, diff_head_g[l]) * (1.0 - lam_init)).reshape(B, S, DIFF_HEADS * DIFF_V)

        qb = (rmsnorm(b_cq, mla_q_norm_g[l]) @ mla_w_q_up[l]).reshape(B, S, MLA_HEADS, MLA_NOPE + MLA_ROPE)
        qb = jnp.concatenate([qb[..., :MLA_NOPE], rope(qb[..., MLA_NOPE:], positions)], axis=-1)
        kvb = (rmsnorm(b_ckv, mla_kv_norm_g[l]) @ mla_w_kv_up[l]).reshape(B, S, MLA_HEADS, MLA_NOPE + MLA_V)
        k_rope = jnp.broadcast_to(rope(b_kr, positions)[:, :, None, :], (B, S, MLA_HEADS, MLA_ROPE))
        kb = jnp.concatenate([kvb[..., :MLA_NOPE], k_rope], axis=-1)
        o_b = mla_attention(qb, kb, kvb[..., MLA_NOPE:])

        o_c = swa_attention(c_q.reshape(B, S, SWA_Q_HEADS, HEAD_DIM),
                            c_k.reshape(B, S, SWA_KV_HEADS, HEAD_DIM),
                            c_v.reshape(B, S, SWA_KV_HEADS, HEAD_DIM),
                            positions, swa_slopes, swa_sinks[l])

        mix = jnp.concatenate([o_a, o_b, o_c], axis=-1) @ w_out[l]
        x = x + rmsnorm(mix, g_mix_post[l])

        xo = cross_attention(rmsnorm(x, g_x_pre[l]), rmsnorm(mem, g_x_mem[l]), w_xq[l], w_xkv[l], w_xo[l])
        x = x + rmsnorm(xo, g_x_post[l])

        gate, up = jnp.split(rmsnorm(x, g_ffn_pre[l]) @ w_ffn_in[l], 2, axis=-1)
        f = (jax.nn.silu(gate) * up) @ w_ffn_out[l]
        x = x + rmsnorm(f, g_ffn_post[l])

    return x


DEPTH_2 = 1

GRID_W = 64
NORM_EPS = 1e-6
RWKV_HEADS = 8
RWKV_HEAD = 64
RWKV_W = RWKV_HEADS * RWKV_HEAD
DECAY_LORA = 64
ICLR_LORA = 64
GATE_LORA = 128
VRES_LORA = 32
RWKV_LN_EPS = 64e-5
N_DIR = 2
RWKV_COLS = 3 * RWKV_W + N_DIR * DECAY_LORA + N_DIR * ICLR_LORA + GATE_LORA
POOL_WINDOWS = (2, 4, 8, 16)
POOL_GROUPS = len(POOL_WINDOWS)
POOL_GROUP_W = 128
POOL_W = POOL_GROUPS * POOL_GROUP_W
ATT_HEADS = 8
ATT_KV_HEADS = 2
ATT_GROUP = ATT_HEADS // ATT_KV_HEADS
ATT_HEAD = 64
ATT_W = ATT_HEADS * ATT_HEAD
ATT_COLS = (ATT_HEADS + 2 * ATT_KV_HEADS) * ATT_HEAD
ROPE_AXIS_DIM = ATT_HEAD // 2
Q_BLOCK = 128
N_BRANCH = 3
GATE_COLS = N_BRANCH * D_MODEL
N_PROJ = RWKV_COLS + POOL_W + ATT_COLS + GATE_COLS
N_EXPERTS = 16
EXPERT_FF = 1024
CAPACITY_FACTOR = 2


def rms_norm(x, g, eps=NORM_EPS):
    xf = x.astype(jnp.float32)
    y = xf * lax.rsqrt(jnp.mean(xf * xf, axis=-1, keepdims=True) + eps)
    return (y * g.astype(jnp.float32)).astype(x.dtype)

def centred_token_shift(p, mu_prev, mu_next):
    zero = jnp.zeros_like(p[:, :1])
    p_prev = jnp.concatenate([zero, p[:, :-1]], axis=1)
    p_next = jnp.concatenate([p[:, 1:], zero], axis=1)
    return p + mu_prev * (p_prev - p) + mu_next * (p_next - p)

def _heads(z):
    return z.reshape(z.shape[:-1] + (RWKV_HEADS, RWKV_HEAD))

def rwkv7_bidir(p, hn, vres, v_first, w0, w2, a0, a2, g2, k_k, k_a, r_k, ln_w, ln_b):
    B, S, _ = p.shape
    f32 = jnp.float32
    dt = p.dtype
    pf = p.astype(f32)
    offs = np.cumsum([RWKV_W, RWKV_W, RWKV_W, N_DIR * DECAY_LORA, N_DIR * ICLR_LORA]).tolist()
    r, k, v, wd, ad, gd = jnp.split(pf, offs, axis=-1)
    wd = wd.reshape(B, S, N_DIR, DECAY_LORA)
    ad = ad.reshape(B, S, N_DIR, ICLR_LORA)
    w_raw = w0.astype(f32) + jnp.einsum('bsel,elc->bsec', jnp.tanh(wd), w2.astype(f32))
    decay = jnp.exp(-jnp.exp(-jax.nn.softplus(-w_raw) - 0.5))
    a = jax.nn.sigmoid(a0.astype(f32) + jnp.einsum('bsel,elc->bsec', ad, a2.astype(f32)))
    g = jnp.einsum('bsl,lc->bsc', jax.nn.sigmoid(gd), g2.astype(f32))
    if v_first is None:
        v_first = v
    else:
        v0, v1, v2 = vres
        mix = jax.nn.sigmoid(v0.astype(f32) + jnp.einsum('bsd,dl,lc->bsc', hn.astype(f32), v1.astype(f32), v2.astype(f32)))
        v = v + (v_first - v) * mix
    kk = _heads(k * k_k.astype(f32))
    kk = kk / jnp.maximum(jnp.linalg.norm(kk, axis=-1, keepdims=True), 1e-12)
    k_dir = k[:, :, None, :] * (1.0 + (a - 1.0) * k_a.astype(f32))

    def both(z):
        return jnp.stack([z, jnp.flip(z, 1)], axis=2)

    def per_dir(z):
        return jnp.stack([z[:, :, 0], jnp.flip(z[:, :, 1], 1)], axis=2)

    def time_major(z):
        return _heads(z).transpose(1, 2, 0, 3, 4)

    inputs = (time_major(both(r)), time_major(per_dir(decay)), time_major(per_dir(k_dir)),
              time_major(both(v)), both(kk).transpose(1, 2, 0, 3, 4), time_major(per_dir(a)))

    def step(state, inp):
        r_t, w_t, k_t, v_t, kk_t, a_t = inp
        sa = jnp.einsum('dbhij,dbhj->dbhi', state, -kk_t)
        state = (state * w_t[..., None, :] + sa[..., :, None] * (kk_t * a_t)[..., None, :]
                 + v_t[..., :, None] * k_t[..., None, :])
        return state, jnp.einsum('dbhij,dbhj->dbhi', state, r_t)

    state0 = jnp.zeros((N_DIR, B, RWKV_HEADS, RWKV_HEAD, RWKV_HEAD), f32)
    _, ys = lax.scan(step, state0, inputs)
    y = (ys[:, 0] + jnp.flip(ys[:, 1], 0)).transpose(1, 0, 2, 3)
    mu = jnp.mean(y, axis=-1, keepdims=True)
    var = jnp.mean(jnp.square(y - mu), axis=-1, keepdims=True)
    yn = (y - mu) * lax.rsqrt(var + RWKV_LN_EPS) * _heads(ln_w.astype(f32)) + _heads(ln_b.astype(f32))
    bonus = jnp.sum(_heads(r) * _heads(k_dir.sum(axis=2)) * _heads(r_k.astype(f32)), axis=-1, keepdims=True) * _heads(v)
    out = (yn + bonus).reshape(B, S, RWKV_W) * g
    return out.astype(dt), v_first

def multiscale_pool(z, pool_w, pool_scale):
    B, S, _ = z.shape
    zg = z.astype(jnp.float32).reshape(B, S, POOL_GROUPS, POOL_GROUP_W)
    csum = jnp.concatenate([jnp.zeros((B, 1, POOL_GROUPS, POOL_GROUP_W), jnp.float32), jnp.cumsum(zg, axis=1)], axis=1)
    t = jnp.arange(S)
    outs = []
    for gi, w in enumerate(POOL_WINDOWS):
        lo = w // 2
        hi = w - lo - 1
        start = jnp.clip(t - lo, 0, S)
        end = jnp.clip(t + hi + 1, 0, S)
        cnt = (end - start).astype(jnp.float32)
        outs.append((csum[:, end, gi] - csum[:, start, gi]) / cnt[None, :, None] - zg[:, :, gi])
    pooled = jnp.stack(outs, axis=2)
    y = jnp.einsum('bsgc,gcd->bsgd', pooled, pool_w.astype(jnp.float32)).reshape(B, S, POOL_W)
    return (y * pool_scale.astype(jnp.float32)).astype(z.dtype)

def axial_rope(seq):
    rows = seq // GRID_W
    row = jnp.repeat(jnp.arange(rows, dtype=jnp.float32), GRID_W)
    col = jnp.tile(jnp.arange(GRID_W, dtype=jnp.float32), rows)
    freqs = ROPE_THETA ** (-jnp.arange(0, ROPE_AXIS_DIM, 2, dtype=jnp.float32) / ROPE_AXIS_DIM)
    ang = jnp.concatenate([row[:, None] * freqs, col[:, None] * freqs], axis=-1)
    return jnp.cos(ang), jnp.sin(ang)

def apply_rope(x, cos, sin):
    xp = x.reshape(x.shape[:-1] + (ATT_HEAD // 2, 2))
    x0, x1 = xp[..., 0], xp[..., 1]
    c = cos[None, :, None, :]
    s = sin[None, :, None, :]
    return jnp.stack([x0 * c - x1 * s, x0 * s + x1 * c], axis=-1).reshape(x.shape)

def gqa_axial(p_att, q_norm, k_norm):
    B, S, _ = p_att.shape
    dt = p_att.dtype
    q, k, v = jnp.split(p_att, [ATT_W, ATT_W + ATT_KV_HEADS * ATT_HEAD], axis=-1)
    q = rms_norm(q.reshape(B, S, ATT_HEADS, ATT_HEAD), q_norm).astype(jnp.float32)
    k = rms_norm(k.reshape(B, S, ATT_KV_HEADS, ATT_HEAD), k_norm).astype(jnp.float32)
    cos, sin = axial_rope(S)
    q = (apply_rope(q, cos, sin) * (ATT_HEAD ** -0.5)).astype(dt)
    k = apply_rope(k, cos, sin).astype(dt)
    v = v.reshape(B, S, ATT_KV_HEADS, ATT_HEAD)
    n_blocks = S // Q_BLOCK
    q_blocks = q.reshape(B, n_blocks, Q_BLOCK, ATT_KV_HEADS, ATT_GROUP, ATT_HEAD).transpose(1, 0, 3, 4, 2, 5)
    k_t = k.transpose(0, 2, 1, 3)
    v_t = v.transpose(0, 2, 1, 3)

    def block(qb):
        s = jnp.einsum('bkgqd,bksd->bkgqs', qb, k_t).astype(jnp.float32)
        pr = jax.nn.softmax(s, axis=-1).astype(dt)
        return jnp.einsum('bkgqs,bksd->bkgqd', pr, v_t)

    o = lax.map(block, q_blocks)
    return o.transpose(1, 0, 4, 2, 3, 5).reshape(B, S, ATT_W)

def expert_choice_ffn(h, router, w_gate, w_up, w_down):
    B, S, D = h.shape
    cap = CAPACITY_FACTOR * S // N_EXPERTS
    aff = jax.nn.softmax(jnp.einsum('bsd,de->bse', h, router).astype(jnp.float32), axis=-1)
    vals, idx = lax.top_k(aff.transpose(0, 2, 1), cap)
    xg = jax.vmap(lambda hb, ib: hb[ib])(h, idx)
    hid = jax.nn.silu(jnp.einsum('becd,edf->becf', xg, w_gate)) * jnp.einsum('becd,edf->becf', xg, w_up)
    y = jnp.einsum('becf,efd->becd', hid, w_down) * vals[..., None].astype(h.dtype)
    return jax.vmap(lambda ib, yb: jnp.zeros((S, D), yb.dtype).at[ib.reshape(-1)].add(yb.reshape(-1, D)))(idx, y)

def second_inputs(seed: int = 0) -> dict:
    key = jax.random.key(seed)
    ks = iter(jax.random.split(key, 40))

    def nrm(shape, scale):
        return jax.random.normal(next(ks), shape, jnp.float32) * scale

    def uni(shape, lo, hi):
        return jax.random.uniform(next(ks), shape, jnp.float32, lo, hi)

    L = DEPTH_2
    Lv = DEPTH_2 - 1
    return {
        'x': nrm((BATCH, SEQ, D_MODEL), 1.0),
        'norm_mix': 1.0 + nrm((L, D_MODEL), 0.05),
        'w_in': nrm((L, D_MODEL, N_PROJ), D_MODEL ** -0.5),
        'shift_prev': uni((L, RWKV_COLS), 0.0, 0.5),
        'shift_next': uni((L, RWKV_COLS), 0.0, 0.5),
        'rwkv_w0': uni((L, N_DIR, RWKV_W), -5.0, 1.0),
        'rwkv_w2': nrm((L, N_DIR, DECAY_LORA, RWKV_W), 0.5 * DECAY_LORA ** -0.5),
        'rwkv_a0': nrm((L, N_DIR, RWKV_W), 0.5),
        'rwkv_a2': nrm((L, N_DIR, ICLR_LORA, RWKV_W), ICLR_LORA ** -0.5),
        'rwkv_g2': nrm((L, GATE_LORA, RWKV_W), GATE_LORA ** -0.5),
        'rwkv_k_k': 0.85 + nrm((L, RWKV_W), 0.05),
        'rwkv_k_a': 1.0 + nrm((L, RWKV_W), 0.05),
        'rwkv_r_k': nrm((L, RWKV_W), 0.1),
        'rwkv_ln_w': 1.0 + nrm((L, RWKV_W), 0.05),
        'rwkv_ln_b': nrm((L, RWKV_W), 0.02),
        'vres_v0': 0.5 + nrm((Lv, RWKV_W), 0.3),
        'vres_w1': nrm((Lv, D_MODEL, VRES_LORA), D_MODEL ** -0.5),
        'vres_w2': nrm((Lv, VRES_LORA, RWKV_W), VRES_LORA ** -0.5),
        'pool_w': nrm((L, POOL_GROUPS, POOL_GROUP_W, POOL_GROUP_W), POOL_GROUP_W ** -0.5),
        'pool_scale': 1.0 + nrm((L, POOL_W), 0.1),
        'q_norm': 1.0 + nrm((L, ATT_HEAD), 0.05),
        'k_norm': 1.0 + nrm((L, ATT_HEAD), 0.05),
        'w_branch_rwkv': nrm((L, RWKV_W, D_MODEL), RWKV_W ** -0.5),
        'w_branch_pool': nrm((L, POOL_W, D_MODEL), POOL_W ** -0.5),
        'w_branch_attn': nrm((L, ATT_W, D_MODEL), ATT_W ** -0.5),
        'w_out': nrm((L, D_MODEL, D_MODEL), D_MODEL ** -0.5),
        'norm_ffn': 1.0 + nrm((L, D_MODEL), 0.05),
        'router': nrm((L, D_MODEL, N_EXPERTS), D_MODEL ** -0.5),
        'exp_gate': nrm((L, N_EXPERTS, D_MODEL, EXPERT_FF), D_MODEL ** -0.5),
        'exp_up': nrm((L, N_EXPERTS, D_MODEL, EXPERT_FF), D_MODEL ** -0.5),
        'exp_down': nrm((L, N_EXPERTS, EXPERT_FF, D_MODEL), EXPERT_FF ** -0.5),
        'norm_final': 1.0 + nrm((D_MODEL,), 0.05),
    }

def second_block(x, norm_mix, w_in, shift_prev, shift_next, rwkv_w0, rwkv_w2, rwkv_a0, rwkv_a2, rwkv_g2,
              rwkv_k_k, rwkv_k_a, rwkv_r_k, rwkv_ln_w, rwkv_ln_b, vres_v0, vres_w1, vres_w2,
              pool_w, pool_scale, q_norm, k_norm, w_branch_rwkv, w_branch_pool, w_branch_attn, w_out,
              norm_ffn, router, exp_gate, exp_up, exp_down, norm_final):
    B, S, D = x.shape
    split_at = [RWKV_COLS, RWKV_COLS + POOL_W, RWKV_COLS + POOL_W + ATT_COLS]
    v_first = None
    for l in range(DEPTH_2):
        hn = rms_norm(x, norm_mix[l])
        proj = jnp.einsum('bsd,dn->bsn', hn, w_in[l])
        p_rwkv, p_pool, p_att, p_gate = jnp.split(proj, split_at, axis=-1)
        p_rwkv = centred_token_shift(p_rwkv, shift_prev[l], shift_next[l])
        vres = None if l == 0 else (vres_v0[l - 1], vres_w1[l - 1], vres_w2[l - 1])
        y_a, v_first = rwkv7_bidir(p_rwkv, hn, vres, v_first, rwkv_w0[l], rwkv_w2[l], rwkv_a0[l], rwkv_a2[l],
                                   rwkv_g2[l], rwkv_k_k[l], rwkv_k_a[l], rwkv_r_k[l], rwkv_ln_w[l], rwkv_ln_b[l])
        y_b = multiscale_pool(p_pool, pool_w[l], pool_scale[l])
        y_c = gqa_axial(p_att, q_norm[l], k_norm[l])
        gates = jax.nn.sigmoid(p_gate).reshape(B, S, N_BRANCH, D)
        merged = (gates[:, :, 0] * (y_a @ w_branch_rwkv[l]) + gates[:, :, 1] * (y_b @ w_branch_pool[l])
                  + gates[:, :, 2] * (y_c @ w_branch_attn[l]))
        x = x + merged @ w_out[l]
        x = x + expert_choice_ffn(rms_norm(x, norm_ffn[l]), router[l], exp_gate[l], exp_up[l], exp_down[l])
    return rms_norm(x, norm_final)


def setup_inputs(seed=0):
    out = dict(first_inputs(seed))
    for name, value in second_inputs(seed + 1).items():
        if name != "x":
            out[name + "_2"] = value
    return out


def reference(
    x, mem, positions, g_mix_pre, g_mix_post, w_in, diff_lambda, diff_head_g, mla_q_norm_g,
    mla_w_q_up, mla_kv_norm_g, mla_w_kv_up, swa_sinks, w_out, g_x_pre, g_x_mem, g_x_post, w_xq,
    w_xkv, w_xo, g_ffn_pre, g_ffn_post, w_ffn_in, w_ffn_out, norm_mix_2, w_in_2, shift_prev_2,
    shift_next_2, rwkv_w0_2, rwkv_w2_2, rwkv_a0_2, rwkv_a2_2, rwkv_g2_2, rwkv_k_k_2, rwkv_k_a_2,
    rwkv_r_k_2, rwkv_ln_w_2, rwkv_ln_b_2, vres_v0_2, vres_w1_2, vres_w2_2, pool_w_2,
    pool_scale_2, q_norm_2, k_norm_2, w_branch_rwkv_2, w_branch_pool_2, w_branch_attn_2,
    w_out_2, norm_ffn_2, router_2, exp_gate_2, exp_up_2, exp_down_2, norm_final_2,
):
    x = first_block(
        x, mem, positions, g_mix_pre, g_mix_post, w_in, diff_lambda, diff_head_g, mla_q_norm_g,
        mla_w_q_up, mla_kv_norm_g, mla_w_kv_up, swa_sinks, w_out, g_x_pre, g_x_mem, g_x_post,
        w_xq, w_xkv, w_xo, g_ffn_pre, g_ffn_post, w_ffn_in, w_ffn_out,
    )
    return second_block(
        x, norm_mix_2, w_in_2, shift_prev_2, shift_next_2, rwkv_w0_2, rwkv_w2_2, rwkv_a0_2,
        rwkv_a2_2, rwkv_g2_2, rwkv_k_k_2, rwkv_k_a_2, rwkv_r_k_2, rwkv_ln_w_2, rwkv_ln_b_2,
        vres_v0_2, vres_w1_2, vres_w2_2, pool_w_2, pool_scale_2, q_norm_2, k_norm_2,
        w_branch_rwkv_2, w_branch_pool_2, w_branch_attn_2, w_out_2, norm_ffn_2, router_2,
        exp_gate_2, exp_up_2, exp_down_2, norm_final_2,
    )


_drawn_inputs = setup_inputs


def setup_inputs(seed=0):
    import zlib

    import numpy as np

    out = dict(_drawn_inputs(seed))
    spreads = {}
    factors = {'diff_head_g': 2.912,
     'mla_q_norm_g': 8.0,
     'mla_kv_norm_g': 8.0,
     'g_x_pre': 3.194,
     'g_x_post': 3.032,
     'g_ffn_pre': 2.807,
     'g_ffn_post': 3.758,
     'norm_mix_2': 3.557,
     'rwkv_w2_2': 5.322,
     'rwkv_ln_w_2': 8.0,
     'rwkv_ln_b_2': 33.948,
     'pool_scale_2': 3.527,
     'q_norm_2': 8.0,
     'k_norm_2': 8.0,
     'norm_ffn_2': 4.948,
     'rwkv_k_k_2': 3.418}
    for name, (base, spread) in spreads.items():
        noise = np.random.default_rng([zlib.crc32(name.encode()), seed]).standard_normal(out[name].shape)
        drawn = base * np.exp(spread * noise) if base else spread * noise
        out[name] = __import__('jax').numpy.asarray(drawn.astype(out[name].dtype))
    for name, factor in factors.items():
        out[name] = (out[name] * factor).astype(out[name].dtype)
    return out
```

```python
import math

import numpy as np
import concourse.bass as bass
from concourse import mybir

F32 = mybir.dt.float32
I32 = mybir.dt.int32
ALU = mybir.AluOpType
ACT = mybir.ActivationFunctionType
AX = mybir.AxisListType.X

P = 128
S = 256
NB = S // P
D = 1024
KC = D // P
DEPTH = 2
FF = 2816
FC = FF // P
UNIT = 2048
SLOTS = 8
EXPERT_SLOTS = 12
E_N = 16
CAP = 32
G_N = 4
GE = E_N // G_N
EF = 1024
HEADS2 = 8
PAIRS = 4
CH = 64
NCH = S // CH
EPS = 1e-6
LN_EPS = 64e-5
FAR = 1e30
LAYER_UNITS = 64
BLOCK2_UNITS = 40
GROUP_UNITS = 48
DENSE_UNITS = DEPTH * LAYER_UNITS + BLOCK2_UNITS
EXPERT_UNITS = G_N * GROUP_UNITS
DECAY = math.exp(-0.5)
SLOPES = [2.0 ** (-8.0 * (i + 1) / 12) for i in range(12)]


def columns(*parts):
    at, out = 0, {}
    for name, width in parts:
        out[name] = (at, at + width)
        at += width
    return out, at


CONST, CONST_W = columns(
    ("ident", 128), ("inv", 16), ("swa_far", 512), ("headsum", 128), ("eye64", 64),
    ("causal", 256), ("level", 6 * 128), ("scan_keep", 256),
    ("cos", 64), ("sin", 64), ("pool_cnt", 1024), ("iota", 32), ("eps", 1), ("ln_eps", 1), ("half_pi", 1),
)
LAYER, LAYER_W = columns(
    ("g_mix_pre", 8), ("g_x_pre", 8), ("g_x_mem", 8), ("g_ffn_pre", 8), ("g_q", 2), ("g_kv", 1),
    ("g_diff", 1), ("sinks", 8), ("lambda", 128), ("lam_init", 1), ("lam_rest", 1), ("kv_up", 512),
    ("q_up", 768), ("g_mix_post", 1024), ("g_x_post", 1024), ("g_ffn_post", 1024),
)
SECOND, SECOND_W = columns(
    ("g_mix", 8), ("mu_prev", 15), ("mu_next", 15), ("w0", 8), ("a0", 8), ("k_k", 4), ("k_a", 4),
    ("r_k", 4), ("ln_w", 4), ("ln_b", 4), ("pool_scale", 4), ("g_ffn", 8), ("q_norm", 64),
    ("k_norm", 64), ("router", 128), ("w2", 512), ("a2", 512), ("g2", 512), ("pool_w", 512),
    ("g_final", 1024),
)


class Engine:

    def __init__(self, prog, eng, name):
        self.prog, self.e, self.name = prog, eng, name
        self.steps = prog.sem(f"{name}_steps")
        self.n = 0
        self.mine = {f"{name}_steps"}

    def step(self):
        self.n += 1
        return self.steps

    def event(self, event):
        self.mine.add(event)
        return self.prog.sem(event)

    def finish(self, scope, turn):
        if self.n:
            self.e.wait_ge(self.steps, self.n)
        met = self.prog.sem(f"{scope}_met")
        self.e.drain().then_inc(met, 1)
        self.e.wait_ge(met, turn * 8 + 4)
        self.e.sem_inc(self.prog.sem("passed"), 1)
        for name in sorted(self.mine):
            self.e.sem_clear(self.prog.sem(name))
        self.e.drain().then_inc(met, 1)
        self.e.wait_ge(met, turn * 8 + 8)
        self.n = 0
        self.mine = {f"{self.name}_steps"}


class TileRing:

    def __init__(self, prog, name, banks):
        self.full, self.drained = prog.sem(f"{name}_tile_full"), prog.sem(f"{name}_tile_drained")
        self.names = (f"{name}_tile_full", f"{name}_tile_drained")
        self.banks, self.size = banks, len(banks)
        self.opened = 0
        self.taken = {}

    def open(self, pe):
        pe.mine.add(self.names[0])
        self.opened += 1
        return self.banks[(self.opened - 1) % self.size]

    def turn(self, eng):
        return self.taken.get(eng.name, 0) + 1

    def take(self, eng):
        if eng.name != "act" or self.names[1] != "both_tile_drained":
            eng.mine.add(self.names[1])
        self.taken[eng.name] = self.turn(eng)
        return self.banks[(self.taken[eng.name] - 1) % self.size]

    def reset(self, name):
        if name == "pe":
            self.opened = 0
        self.taken[name] = 0


class Weights:

    def __init__(self, prog, pe):
        self.prog, self.pe = prog, pe
        self.owed = 0

    def start(self, base, slots, loaded, free):
        self.n, self.base = 0, base
        self.slots, self.loaded, self.free = slots, loaded, free

    def next(self):
        s, r = self.n % len(self.slots), self.n // len(self.slots)
        self.n += 1
        self.pe.e.wait_ge(self.loaded[s], self.base + 16 * (r + 1))
        return self.slots[s]

    def used(self, n=1):
        self.owed += n

    def mm(self, out, lhsT, rhs, start=True, stop=True):
        ins = self.pe.e.matmul(out, lhsT, rhs, start=start, stop=stop)
        return self._tell(ins)

    def transpose(self, out, in_, identity):
        return self._tell(self.pe.e.transpose(out, in_, identity))

    def _tell(self, ins):
        if self.owed:
            ins.then_inc(self.free, self.owed)
            self.owed = 0
        return ins

    def flush(self):
        if self.owed:
            self.pe.e.drain().then_inc(self.free, self.owed)
            self.owed = 0


class Program:
    def __init__(self, nc, ctx, io):
        self.nc, self.ctx, self.io = nc, ctx, io
        self.sems = {}
        self.count = {}
        self.mark = {}
        self.slots_free = self.sem("slots_free")
        self.slot_loaded = [self.sem(f"slot_loaded_{s}") for s in range(SLOTS)]
        ring = self.sb("ring", SLOTS * UNIT)
        self.slots = [ring[:, s * UNIT:(s + 1) * UNIT] for s in range(SLOTS)]
        self.expert_slot_loaded = [self.sem(f"expert_slot_loaded_{s}") for s in range(EXPERT_SLOTS)]
        self.expert_slots_used = self.sem("expert_slots_used")
        self.const = self.sb("const", CONST_W)
        self.par = self.sb("par", max(LAYER_W, SECOND_W))
        self.x = self.sb("x", NB * D)[:, :].rearrange("p (b d) -> p b d", b=NB)
        self.small = self.sb("small", 256)
        self.arena_w = 26240
        self.arena = self.sb("arena", self.arena_w)
        self.at = 0
        tail = [self.arena[:, self.arena_w - (j + 1) * UNIT:self.arena_w - j * UNIT]
                for j in range(EXPERT_SLOTS - SLOTS)]
        self.expert_slots = self.slots + tail
        self.ps = [ctx.enter_context(nc.psum_tensor(f"ps{i}", [P, 512], F32)) for i in range(8)]
        b = [t[:, :] for t in self.ps]
        self.act_tiles = TileRing(self, "act", b[0:2])
        self.dve_tiles = TileRing(self, "dve", b[2:6])
        self.both_tiles = TileRing(self, "both", b[6:8])

    def sem(self, name):
        if name not in self.sems:
            self.sems[name] = self.ctx.enter_context(self.nc.semaphore(name))
        return self.sems[name]

    def sb(self, name, width, dt=F32):
        return self.ctx.enter_context(self.nc.sbuf_tensor(name, [P, width], dt))

    def take(self, *shape):
        width = int(np.prod(shape))
        ap = self.arena[:, self.at:self.at + width]
        self.at += width
        assert self.at <= self.arena_w, self.at
        return shaped(ap, *shape)

    def c(self, name, *shape):
        a, b = CONST[name]
        return shaped(self.const[:, a:b], *shape)

    def lp(self, name, *shape):
        a, b = LAYER[name]
        return shaped(self.par[:, a:b], *shape)

    def sp(self, name, *shape):
        a, b = SECOND[name]
        return shaped(self.par[:, a:b], *shape)

    def reset_rings(self, name):
        for r in (self.act_tiles, self.dve_tiles, self.both_tiles):
            r.reset(name)


def shaped(ap, *shape):
    if len(shape) < 2:
        return ap
    names = "abcd"[:len(shape)]
    spec = f"p ({' '.join(names)}) -> p {' '.join(names)}"
    return ap.rearrange(spec, **{n: s for n, s in zip(names[:-1], shape[:-1])})


def spread(ap, axis, n):
    u = ap.unsqueeze(axis)
    shape = list(u.shape)
    shape[axis] = n
    return u.to_broadcast(shape)



def norm_stats(p, act, src, width, out, tag):
    for b in range(NB):
        act.e.activation(p.junk_act[:, 0:width], src[:, b, 0:width], ACT.Square,
                                accum_out=p.small_act[:, b:b + 1]).then_inc(act.step(), 1)
        act.e.wait_ge(act.steps, act.n)
    act.e.activation(p.small_act[:, 2:4], p.small_act[:, 0:2], ACT.Ln,
                            scale=1.0 / width, bias=p.c("eps")).then_inc(act.step(), 1)
    act.e.wait_ge(act.steps, act.n)
    act.e.activation(out, p.small_act[:, 2:4], ACT.Exp, scale=-0.5).then_inc(act.event(tag), 1)


def norm_rows(p, dve, src, rstd, dst, width, tag, n):
    dve.e.wait_ge(p.sem(tag), n)
    for b in range(NB):
        ins = dve.e.tensor_scalar(dst[:, b, 0:width], src[:, b, 0:width], rstd[:, b:b + 1], None, ALU.mult)
        if b == NB - 1:
            ins.then_inc(dve.event(tag + "_rows"), 1)
        else:
            ins.then_inc(dve.step(), 1)


def rows_to_columns_pe(p, pe, w, src, chunks, tag, n):
    pe.e.wait_ge(p.sem(tag + "_rows"), n)
    ident = p.c("ident")
    for j in range((chunks + 1) // 2):
        tiles = p.act_tiles if j % 2 == 0 else p.dve_tiles
        if tiles.opened >= tiles.size:
            pe.e.wait_ge(tiles.drained, tiles.opened - tiles.size + 1)
        bank = tiles.open(pe)
        for c in range(2 * j, min(2 * j + 2, chunks)):
            for b in range(NB):
                o = (c - 2 * j) * S + b * P
                ins = w.transpose(bank[:, o:o + P], src[:, b, c * P:(c + 1) * P], ident) if not (
                    c == min(2 * j + 2, chunks) - 1 and b == NB - 1) else pe.e.transpose(
                        bank[:, o:o + P], src[:, b, c * P:(c + 1) * P], ident)
        ins.then_inc(tiles.full, 1)


def rows_to_columns_evac(p, eng, dst, gain, chunks, mine):
    for j in range((chunks + 1) // 2):
        if (j % 2 == 0) != mine:
            continue
        tiles = p.act_tiles if mine else p.dve_tiles
        eng.e.wait_ge(tiles.full, tiles.turn(eng))
        bank = tiles.take(eng)
        cs = range(2 * j, min(2 * j + 2, chunks))
        for c in cs:
            o = (c - 2 * j) * S
            g = 1.0 if gain is None else gain[:, c:c + 1]
            if mine:
                ins = eng.e.activation(dst[:, c, :], bank[:, o:o + S], ACT.Copy, scale=g)
            else:
                ins = eng.e.tensor_scalar(dst[:, c, :], bank[:, o:o + S], g, None, ALU.mult)
            if c == cs[-1]:
                ins.then_inc(tiles.drained, 1)
            else:
                ins.then_inc(eng.step(), 1)


def columns_ready(p, pe):
    pe.e.wait_ge(p.act_tiles.drained, p.act_tiles.opened)
    pe.e.wait_ge(p.dve_tiles.drained, p.dve_tiles.opened)



def project_columns(p, pe, w, src, tiles, n=2):
    u = w.next()
    if tiles.opened >= tiles.size:
        pe.e.wait_ge(tiles.drained, tiles.opened - tiles.size + 1)
    bank = tiles.open(pe)
    for c in range(n):
        for k in range(KC):
            o = (c * KC + k) * P
            last = c == n - 1 and k == KC - 1
            ins = (pe.e.matmul if last else w.mm)(bank[:, c * S:(c + 1) * S], u[:, o:o + P], src[:, k, :],
                                                  start=k == 0, stop=k == KC - 1)
    ins.then_inc(tiles.full, 1)
    w.used()


def project_rows(p, pe, w, src, tiles, width, split=2):
    kn = KC // split
    banks = []
    for _ in range(NB):
        if tiles.opened >= tiles.size:
            pe.e.wait_ge(tiles.drained, tiles.opened - tiles.size + 1)
        bank = tiles.open(pe)
        banks.append(bank)
    for h in range(split):
        u = w.next()
        for b in range(NB):
            for k in range(kn):
                kk = h * kn + k
                last = h == split - 1 and k == kn - 1
                ins = (pe.e.matmul if last else w.mm)(banks[b][:, 0:width], src[:, kk, b * P:(b + 1) * P],
                                                      u[:, k * width:(k + 1) * width],
                                                      start=kk == 0, stop=kk == KC - 1)
                if last:
                    ins.then_inc(tiles.full, 1)
        w.used()



def first_buffers(p):
    p.at = 0
    p.hrow = p.take(NB, D)
    p.hT = p.take(KC, S)
    p.memT = p.take(KC, S)
    p.memgT = shaped(p.hrow.rearrange("p b d -> p (b d)"), KC, S)
    p.mla = p.take(NB, 416)
    p.v_row = p.take(NB, 384)
    p.qk = p.take(10, S)
    p.xqT = p.qk[:, 0:8, :]
    p.xkT = p.take(KC, S)
    p.xv = p.take(NB, D)
    p.mixT = p.hT
    p.dist = p.take(NB, S)
    p.dist_swa = p.take(NB, S)
    p.rot = p.take(2, NB, 16)
    mark = p.at
    p.cq = p.take(NB, 384)
    p.cqT = p.take(3, S)
    p.q_mla = p.take(NB, 4, 96)
    p.k_mla = shaped(p.cq.rearrange("p b d -> p (b d)"), NB, 4, 96)
    p.kv = p.take(NB, 512)
    p.qT_mla = p.qk[:, 0:4, :]
    p.kT_mla = p.take(4, S)
    p.o_diff = p.take(NB, 256)
    p.sc = [p.take(NB, S) for _ in range(4)]
    p.pr = [p.take(NB, S) for _ in range(4)]
    p.junk_act = p.arena[:, p.at - 1024:p.at]
    p.pT = [p.take(NB, S) for _ in range(2)]
    p.junk_dve = p.take(512)
    end = p.at
    p.at = mark
    p.h1T = p.take(FC, S)
    p.silu = p.take(2, S)
    p.at = max(p.at, end)
    p.small_act = p.small[:, 0:8]
    p.rstd = p.small[:, 8:10]
    p.lam = p.small[:, 10:16]
    p.mx = p.small[:, 16:48]
    p.sums = p.small[:, 48:112]
    p.diff_ss = p.small[:, 112:136]


HEAD_ITEMS = ([("diff", h, m) for h in range(4) for m in range(2)]
              + [("swa", h, 0) for j in range(4) for h in (j, j + 4)]
              + [("mla", h, 0) for h in range(4)])
X_ITEMS = [("x", h, 0) for h in range(4)]
GQA_ITEMS = [("gqa", h, 0) for j in range(4) for h in (j, j + 4)]
SCALE = {"gqa": 64 ** -0.5, "diff": 32 ** -0.5, "swa": 64 ** -0.5, "mla": 96 ** -0.5, "x": 256 ** -0.5}


def beside(item, i):
    kind, h, m = item
    if kind == "gqa":
        return i
    i = i - 1 if kind == "diff" else i
    return i // 2 if i % 2 == 0 and i < 16 else None


def scores_pe(p, pe, w, i, item):
    kind, h, m = item
    if p.both_tiles.opened >= p.both_tiles.size:
        pe.e.wait_ge(p.both_tiles.drained, p.both_tiles.opened - p.both_tiles.size + 1)
    bank = p.both_tiles.open(pe)
    for b in range(NB):
        q = slice(b * P, (b + 1) * P)
        if kind == "diff":
            r = slice(64 * (h % 2) + 32 * m, 64 * (h % 2) + 32 * m + 32)
            parts = [(p.qk[r, h // 2, q], p.qk[r, 2 + h // 2, :])]
        elif kind == "swa":
            r = slice(64 * (h // 4), 64 * (h // 4) + 64)
            parts = [(p.qk[r, 4 + h % 4, q], p.qk[r, 8, :])]
        elif kind == "gqa":
            r = slice(64 * (h // 4), 64 * (h // 4) + 64)
            parts = [(p.qk2[r, h % 4, q], p.qk2[r, 4, :])]
        elif kind == "mla":
            parts = [(p.qT_mla[0:96, h, q], p.kT_mla[0:96, h, :])]
        else:
            parts = [(p.xqT[:, 2 * h + c, q], p.xkT[:, 2 * h + c, :]) for c in range(2)]
        for j, (a, k) in enumerate(parts):
            ins = pe.e.matmul(bank[:, b * S:(b + 1) * S], a, k, start=j == 0, stop=j == len(parts) - 1)
    ins.then_inc(p.both_tiles.full, 1)


def softmax_max_dve(p, dve, i, item):
    kind, h, m = item
    scale = SCALE[kind]
    dve.e.wait_ge(p.both_tiles.full, p.both_tiles.turn(dve))
    bank = shaped(p.both_tiles.take(dve), NB, S)
    sc, mx = p.sc[i % 4], p.mx[:, 2 * (i % 8):2 * (i % 8) + 2]
    nm = p.mx[:, 16 + 2 * (i % 8):18 + 2 * (i % 8)]
    if i >= 4:
        dve.e.wait_ge(p.sem("probs_made"), i - 3)
    if kind in ("diff", "swa"):
        slope = SLOPES[h + 8] if kind == "diff" else SLOPES[h]
        dist = p.dist if kind == "diff" else p.dist_swa
        dve.e.scalar_tensor_tensor(sc, dist, -slope / scale, bank, ALU.mult, ALU.add).then_inc(p.both_tiles.drained, 1)
    else:
        dve.e.tensor_copy(sc, bank).then_inc(p.both_tiles.drained, 1)
    dve.e.wait_ge(p.both_tiles.drained, p.both_tiles.taken["dve"])
    dve.e.tensor_reduce(mx, sc, AX, ALU.max).then_inc(dve.step(), 1)
    dve.e.wait_ge(dve.steps, dve.n)
    if kind == "swa":
        dve.e.tensor_scalar(mx, mx, scale, p.lp("sinks")[:, h:h + 1], ALU.mult, ALU.max).then_inc(dve.step(), 1)
        dve.e.wait_ge(dve.steps, dve.n)
        dve.e.tensor_scalar(nm, mx, -1.0, None, ALU.mult).then_inc(dve.event("max_found"), 1)
    else:
        dve.e.tensor_scalar(nm, mx, -scale, None, ALU.mult).then_inc(dve.event("max_found"), 1)


def softmax_exp_act(p, act, i, item):
    kind, h, m = item
    act.e.wait_ge(p.sem("max_found"), i + 1)
    if i >= 4:
        act.e.wait_ge(p.sem("probs_scaled"), i - 3)
    nm = p.mx[:, 16 + 2 * (i % 8):18 + 2 * (i % 8)]
    sums = p.sums[:, 4 * (i % 8):4 * (i % 8) + 4]
    if kind == "swa":
        act.e.activation(sums[:, 2:4], nm, ACT.Exp, bias=p.lp("sinks")[:, h:h + 1]).then_inc(act.step(), 1)
    for b in range(NB):
        ins = act.e.activation(p.pr[i % 4][:, b, :], p.sc[i % 4][:, b, :], ACT.Exp,
                               bias=nm[:, b:b + 1], scale=SCALE[kind], accum_out=sums[:, b:b + 1])
        if b == NB - 1:
            ins.then_inc(act.event("probs_made"), 1)
        else:
            ins.then_inc(act.step(), 1)


def softmax_scale_dve(p, dve, i, item):
    kind, h, m = item
    dve.e.wait_ge(p.sem("probs_made"), i + 1)
    sums = p.sums[:, 4 * (i % 8):4 * (i % 8) + 4]
    pr = p.pr[i % 4]
    if kind == "swa":
        dve.e.tensor_tensor(sums[:, 0:2], sums[:, 0:2], sums[:, 2:4], ALU.add).then_inc(dve.step(), 1)
        dve.e.wait_ge(dve.steps, dve.n)
    dve.e.reciprocal(sums[:, 0:2], sums[:, 0:2]).then_inc(dve.step(), 1)
    dve.e.wait_ge(dve.steps, dve.n)
    if kind == "diff" and m == 1:
        dve.e.tensor_scalar(sums[:, 0:2], sums[:, 0:2], p.lam[:, 0:1], None, ALU.mult).then_inc(dve.step(), 1)
        dve.e.wait_ge(dve.steps, dve.n)
    for b in range(NB):
        ins = dve.e.tensor_scalar(pr[:, b, :], pr[:, b, :], sums[:, b:b + 1], None, ALU.mult)
        if kind == "diff" and m == 1 or b < NB - 1:
            ins.then_inc(dve.step(), 1)
        else:
            ins.then_inc(dve.event("probs_scaled"), 1)
    if kind == "diff" and m == 1:
        dve.e.wait_ge(p.sem("probs_scaled"), i)
        dve.e.wait_ge(dve.steps, dve.n)
        dve.e.tensor_tensor(p.pr[(i - 1) % 4], p.pr[(i - 1) % 4], pr, ALU.subtract).then_inc(dve.event("probs_scaled"), 1)


def probs_source(p, i, item):
    return p.pr[(i - 1) % 4] if item[0] == "diff" else p.pr[i % 4]


def has_output(item):
    return not (item[0] == "diff" and item[2] == 0)


def probs_transpose_pe(p, pe, w, i, item):
    pe.e.wait_ge(p.sem("probs_scaled"), i + 1)
    src = probs_source(p, i, item)
    if p.act_tiles.opened >= p.act_tiles.size:
        pe.e.wait_ge(p.act_tiles.drained, p.act_tiles.opened - p.act_tiles.size + 1)
    bank = p.act_tiles.open(pe)
    for kb in range(NB):
        for b in range(NB):
            o = kb * S + b * P
            ins = pe.e.transpose(bank[:, o:o + P], src[:, b, kb * P:(kb + 1) * P], p.c("ident"))
    ins.then_inc(p.act_tiles.full, 1)


def values_pe(p, pe, w, i, item, nth):
    kind, h, m = item
    pe.e.wait_ge(p.act_tiles.drained, p.act_tiles.opened)
    pT = p.pT[nth % 2]
    if kind == "diff":
        if p.act_tiles.opened >= p.act_tiles.size:
            pe.e.wait_ge(p.act_tiles.drained, p.act_tiles.opened - p.act_tiles.size + 1)
        bank = p.act_tiles.open(pe)
        for b in range(NB):
            for kb in range(NB):
                ins = pe.e.matmul(bank[:, b * 64:b * 64 + 64], pT[:, kb, b * P:(b + 1) * P],
                                  p.v_row[:, kb, h * 64:h * 64 + 64], start=kb == 0, stop=kb == NB - 1)
        ins.then_inc(p.act_tiles.full, 1)
    elif kind == "x":
        if p.act_tiles.opened >= p.act_tiles.size:
            pe.e.wait_ge(p.act_tiles.drained, p.act_tiles.opened - p.act_tiles.size + 1)
        bank = p.act_tiles.open(pe)
        for c in range(2):
            for kb in range(NB):
                o = h * 256 + c * P
                ins = pe.e.matmul(bank[:, c * S:(c + 1) * S], p.xv[:, kb, o:o + P], pT[:, kb, :],
                                  start=kb == 0, stop=kb == NB - 1)
        ins.then_inc(p.act_tiles.full, 1)
    else:
        half = h % 2 if kind == "mla" else h // 4
        if p.act_tiles.opened >= p.act_tiles.size:
            pe.e.wait_ge(p.act_tiles.drained, p.act_tiles.opened - p.act_tiles.size + 1)
        bank = p.act_tiles.open(pe)
        for kb in range(NB):
            v = (p.att[:, kb, 640 + 64 * half:704 + 64 * half] if kind == "gqa" else
                 p.kv[:, kb, h * P + 64:h * P + 128] if kind == "mla"
                 else p.v_row[:, kb, 256 + 64 * (h // 4):320 + 64 * (h // 4)])
            ins = pe.e.matmul(bank[64 * half:64 * half + 64, 0:S], v, pT[:, kb, :],
                              start=kb == 0, stop=kb == NB - 1)
        ins.then_inc(p.act_tiles.full, 1)


def attention_pe(p, pe, w, items, memory=None):
    nth = 0
    for t in range(len(items) + 2):
        if t < len(items):
            if items[t][0] == "mla" and (t == 0 or items[t - 1][0] != "mla"):
                mla_columns_pe(p, pe, w)
            scores_pe(p, pe, w, t, items[t])
        if t >= 2 and has_output(items[t - 2]):
            probs_transpose_pe(p, pe, w, t - 2, items[t - 2])
            u = beside(items[t - 2], t - 2)
            if memory is not None and u is not None:
                memory(u)
            values_pe(p, pe, w, t - 2, items[t - 2], nth)
            nth += 1
            if items[t - 2] == ("diff", 3, 1):
                p.mark["diff"] = p.act_tiles.opened


def attention_dve(p, dve, items, before=None):
    for t in range(len(items) + 1):
        if t < len(items):
            if before and t in before:
                before[t]()
            softmax_max_dve(p, dve, t, items[t])
        if t >= 1:
            softmax_scale_dve(p, dve, t - 1, items[t - 1])


def attention_act(p, act, items, dst, memory=None, before=None):
    nth = 0
    for t in range(len(items) + 2):
        if t < len(items):
            if before and t in before:
                before[t]()
            softmax_exp_act(p, act, t, items[t])
        if t >= 2 and has_output(items[t - 2]):
            i, item = t - 2, items[t - 2]
            kind, h, m = item
            act.e.wait_ge(p.act_tiles.full, p.act_tiles.turn(act))
            bank = shaped(p.act_tiles.take(act), NB, S)
            act.e.activation(p.pT[nth % 2], bank, ACT.Copy).then_inc(p.act_tiles.drained, 1)
            u = beside(item, i)
            if memory is not None and u is not None:
                memory(u)
            act.e.wait_ge(p.act_tiles.full, p.act_tiles.turn(act))
            bank = p.act_tiles.take(act)
            if kind == "diff":
                out = p.o_diff[:, :, h * 64:h * 64 + 64]
                act.e.activation(out, shaped(bank[:, 0:128], NB, 64), ACT.Copy).then_inc(p.act_tiles.drained, 1)
            elif kind == "x":
                act.e.activation(dst[:, 2 * h:2 * h + 2, :], shaped(bank, 2, S), ACT.Copy).then_inc(p.act_tiles.drained, 1)
            else:
                half = h % 2 if kind == "mla" else h // 4
                c = h % 4 if kind == "gqa" else 2 + h // 2 if kind == "mla" else 4 + h % 4
                r = slice(64 * half, 64 * half + 64)
                act.e.activation(dst[r, c, :], bank[r, 0:S], ACT.Copy).then_inc(p.act_tiles.drained, 1)
            nth += 1


def mla_columns_pe(p, pe, w):
    rows_to_columns_pe(p, pe, w, p.cq, 3, "latent", 1)
    columns_ready(p, pe)
    for b in range(NB):
        if p.dve_tiles.opened >= p.dve_tiles.size:
            pe.e.wait_ge(p.dve_tiles.drained, p.dve_tiles.opened - p.dve_tiles.size + 1)
        bank = p.dve_tiles.open(pe)
        for c in range(2):
            ins = pe.e.matmul(bank[:, 0:384], p.cqT[:, c, b * P:(b + 1) * P],
                              p.lp("q_up")[:, c * 384:(c + 1) * 384], start=c == 0, stop=c == 1)
        ins.then_inc(p.dve_tiles.full, 1)
    for b in range(NB):
        if p.dve_tiles.opened >= p.dve_tiles.size:
            pe.e.wait_ge(p.dve_tiles.drained, p.dve_tiles.opened - p.dve_tiles.size + 1)
        bank = p.dve_tiles.open(pe)
        ins = pe.e.matmul(bank[:, 0:512], p.cqT[:, 2, b * P:(b + 1) * P], p.lp("kv_up"))
        ins.then_inc(p.dve_tiles.full, 1)
    pe.e.wait_ge(p.sem("mla_rows"), 1)
    for src in (p.q_mla, p.k_mla):
        for j in range(2):
            if p.dve_tiles.opened >= p.dve_tiles.size:
                pe.e.wait_ge(p.dve_tiles.drained, p.dve_tiles.opened - p.dve_tiles.size + 1)
            bank = p.dve_tiles.open(pe)
            for c in range(2):
                for b in range(NB):
                    o = c * S + b * P
                    ins = pe.e.transpose(bank[0:96, o:o + P], src[:, b, 2 * j + c, :], p.c("ident"))
            ins.then_inc(p.dve_tiles.full, 1)
    pe.e.wait_ge(p.dve_tiles.drained, p.dve_tiles.opened)


def latent_stats_act(p, act):
    act.e.wait_ge(p.dve_tiles.drained, p.mark["mla"])
    for b in range(NB):
        act.e.activation(p.junk_act[:, 0:256], p.mla[:, b, 0:256], ACT.Square,
                                accum_out=p.small_act[:, b:b + 1]).then_inc(act.step(), 1)
        act.e.wait_ge(act.steps, act.n)
        act.e.activation(p.junk_act[:, 0:128], p.mla[:, b, 256:384], ACT.Square,
                                accum_out=p.small_act[:, 2 + b:3 + b]).then_inc(act.step(), 1)
        act.e.wait_ge(act.steps, act.n)
    act.e.activation(p.small_act[:, 4:6], p.small_act[:, 0:2], ACT.Ln, scale=1.0 / 256, bias=p.c("eps")).then_inc(act.step(), 1)
    act.e.wait_ge(act.steps, act.n)
    act.e.activation(p.small_act[:, 6:8], p.small_act[:, 2:4], ACT.Ln, scale=1.0 / 128, bias=p.c("eps")).then_inc(act.step(), 1)
    act.e.wait_ge(act.steps, act.n)
    act.e.activation(p.lam[:, 2:6], p.small_act[:, 4:8], ACT.Exp, scale=-0.5).then_inc(act.event("latent_rstd"), 1)


def rotate(p, dve, dst, x1, x2, cos, sin, tmp):
    d1, d2 = dst
    t1, t2, t3, t4 = tmp
    dve.e.tensor_tensor(t1, x1, cos, ALU.mult).then_inc(dve.step(), 1)
    dve.e.tensor_tensor(t2, x2, sin, ALU.mult).then_inc(dve.step(), 1)
    dve.e.tensor_tensor(t3, x1, sin, ALU.mult).then_inc(dve.step(), 1)
    dve.e.tensor_tensor(t4, x2, cos, ALU.mult).then_inc(dve.step(), 1)
    dve.e.wait_ge(dve.steps, dve.n)
    dve.e.tensor_tensor(d1, t1, t2, ALU.subtract).then_inc(dve.step(), 1)
    dve.e.tensor_tensor(d2, t3, t4, ALU.add).then_inc(dve.step(), 1)


def mla_dve(p, dve):
    dve.e.wait_ge(p.sem("latent_rstd"), 1)
    for b in range(NB):
        dve.e.tensor_scalar(p.cq[:, b, 0:256], p.mla[:, b, 0:256], p.lam[:, 2 + b:3 + b], None, ALU.mult).then_inc(dve.step(), 1)
        ins = dve.e.tensor_scalar(p.cq[:, b, 256:384], p.mla[:, b, 256:384], p.lam[:, 4 + b:5 + b], None, ALU.mult)
        if b == NB - 1:
            ins.then_inc(dve.event("latent_rows"), 1)
        else:
            ins.then_inc(dve.step(), 1)
    dve.e.wait_ge(p.dve_tiles.full, p.dve_tiles.turn(dve))
    bank = p.dve_tiles.take(dve)
    dve.e.tensor_scalar(p.cqT[:, 2, :], bank[:, 0:S], p.lp("g_kv"), None, ALU.mult).then_inc(p.dve_tiles.drained, 1)
    tmp = [shaped(p.junk_dve[:, j * 64:(j + 1) * 64], 4, 16) for j in range(4)]
    for b in range(NB):
        dve.e.wait_ge(p.dve_tiles.full, p.dve_tiles.turn(dve))
        bank = shaped(p.dve_tiles.take(dve)[:, 0:384], 4, 96)
        dve.e.tensor_copy(p.q_mla[:, b], bank).then_inc(p.dve_tiles.drained, 1)
    dve.e.wait_ge(p.dve_tiles.drained, p.dve_tiles.taken["dve"])
    for b in range(NB):
        dve.e.wait_ge(p.dve_tiles.full, p.dve_tiles.turn(dve))
        bank = p.dve_tiles.take(dve)
        dve.e.tensor_copy(p.kv[:, b, :], bank).then_inc(p.dve_tiles.drained, 1)
    dve.e.wait_ge(p.dve_tiles.drained, p.dve_tiles.taken["dve"])
    for b in range(NB):
        cos, sin = spread(p.rot[:, 0, b, :], 1, 4), spread(p.rot[:, 1, b, :], 1, 4)
        rotate(p, dve, (p.q_mla[:, b, :, 64:80], p.q_mla[:, b, :, 80:96]),
               p.q_mla[:, b, :, 64:80], p.q_mla[:, b, :, 80:96], cos, sin, tmp)
        dve.e.wait_ge(dve.steps, dve.n)
        t = [x[:, 0, :] for x in tmp]
        kr = p.mla[:, b, 384:416]
        rotate(p, dve, (kr[:, 0:16], kr[:, 16:32]), kr[:, 0:16], kr[:, 16:32],
               p.rot[:, 0, b, :], p.rot[:, 1, b, :], t)
        dve.e.wait_ge(dve.steps, dve.n)
        dve.e.tensor_copy(p.k_mla[:, b, :, 0:64], shaped(p.kv[:, b, :], 4, 128)[:, :, 0:64]).then_inc(dve.step(), 1)
        ins = dve.e.tensor_copy(p.k_mla[:, b, :, 64:96], spread(kr, 1, 4))
        if b == NB - 1:
            ins.then_inc(dve.event("mla_rows"), 1)
        else:
            ins.then_inc(dve.step(), 1)
    for dst in (p.qT_mla, p.kT_mla):
        for j in range(2):
            dve.e.wait_ge(p.dve_tiles.full, p.dve_tiles.turn(dve))
            bank = shaped(p.dve_tiles.take(dve), 2, S)
            dve.e.tensor_copy(dst[0:96, 2 * j:2 * j + 2, :], bank[0:96]).then_inc(p.dve_tiles.drained, 1)


def mla_act(p, act):
    act.e.wait_ge(p.act_tiles.full, p.act_tiles.turn(act))
    bank = p.act_tiles.take(act)
    act.e.activation(p.cqT[:, 0, :], bank[:, 0:S], ACT.Copy, scale=p.lp("g_q")[:, 0:1]).then_inc(act.step(), 1)
    act.e.activation(p.cqT[:, 1, :], bank[:, S:2 * S], ACT.Copy, scale=p.lp("g_q")[:, 1:2]).then_inc(p.act_tiles.drained, 1)


def post_stats_act(p, act, n):
    act.e.wait_ge(p.dve_tiles.drained, p.mark[f"mix{n}"])
    norm_stats(p, act, p.hrow, D, p.rstd, "rstd")


def residual_dve(p, dve, gain, n_copy, n_rstd):
    for half in range(2):
        for b in range(NB):
            dve.e.wait_ge(p.dve_tiles.full, p.dve_tiles.turn(dve))
            bank = p.dve_tiles.take(dve)
            dve.e.tensor_copy(p.hrow[:, b, half * 512:(half + 1) * 512], bank).then_inc(p.dve_tiles.drained, 1)
    dve.e.wait_ge(p.dve_tiles.drained, p.dve_tiles.taken["dve"])
    dve.e.wait_ge(p.sem("rstd"), n_rstd)
    for b in range(NB):
        dve.e.scalar_tensor_tensor(p.hrow[:, b, :], p.hrow[:, b, :], p.rstd[:, b:b + 1],
                                           gain, ALU.mult, ALU.mult).then_inc(dve.step(), 1)
    dve.e.wait_ge(dve.steps, dve.n)
    for b in range(NB):
        ins = dve.e.tensor_tensor(p.x[:, b, :], p.x[:, b, :], p.hrow[:, b, :], ALU.add)
        if b == NB - 1:
            ins.then_inc(dve.event("x_ready"), 1)
        else:
            ins.then_inc(dve.step(), 1)
    dve.e.wait_ge(p.sem("x_ready"), n_copy)



def layer_pe(p, pe, w):
    pe.e.wait_ge(p.sem("layer_params"), 16)
    rows_to_columns_pe(p, pe, w, p.hrow, KC, "rstd", 1)
    columns_ready(p, pe)
    project_rows(p, pe, w, p.hT, p.dve_tiles, 416)
    p.mark["mla"] = p.dve_tiles.opened
    project_rows(p, pe, w, p.hT, p.dve_tiles, 384)
    for j in range(5):
        project_columns(p, pe, w, p.hT, p.act_tiles, 2 if j < 4 else 1)
    columns_ready(p, pe)
    pe.e.wait_ge(p.sem("memory_gained"), 1)

    def memory(u):
        if u < 4:
            project_columns(p, pe, w, p.memgT, p.dve_tiles)
        elif u in (4, 6):
            project_rows(p, pe, w, p.memgT, p.dve_tiles, 512)
    attention_pe(p, pe, w, HEAD_ITEMS, memory)
    rows_to_columns_pe(p, pe, w, p.o_diff, 2, "diff", 1)
    columns_ready(p, pe)
    for _ in range(2):
        project_rows(p, pe, w, p.mixT, p.dve_tiles, 512)
    p.mark["mix1"] = p.dve_tiles.opened
    rows_to_columns_pe(p, pe, w, p.hrow, KC, "rstd", 2)
    columns_ready(p, pe)
    for _ in range(4):
        project_columns(p, pe, w, p.hT, p.act_tiles)
    columns_ready(p, pe)
    attention_x(p, "pe", pe, w)
    columns_ready(p, pe)
    for _ in range(2):
        project_rows(p, pe, w, p.mixT, p.dve_tiles, 512)
    p.mark["mix2"] = p.dve_tiles.opened
    rows_to_columns_pe(p, pe, w, p.hrow, KC, "rstd", 3)
    columns_ready(p, pe)
    acc = []
    for _ in range(4):
        if p.dve_tiles.opened >= p.dve_tiles.size:
            pe.e.wait_ge(p.dve_tiles.drained, p.dve_tiles.opened - p.dve_tiles.size + 1)
        bank = p.dve_tiles.open(pe)
        acc.append(bank)
    p.mark["hidden"] = p.both_tiles.opened

    def down(j):
        u = w.next()
        pe.e.wait_ge(p.both_tiles.drained, p.mark["hidden"] + 2 * j + 2)
        for c in range(2):
            f = 2 * j + c
            for half in range(2):
                for b in range(NB):
                    last = f == FC - 1
                    o = c * D + half * 512
                    ins = (pe.e.matmul if last else w.mm)(acc[half * NB + b], p.h1T[:, f, b * P:(b + 1) * P],
                                                          u[:, o:o + 512], start=f == 0, stop=last)
                    if last:
                        closing[half * NB + b] = ins
        w.used()
    closing = {}
    for j in range(FC // 2):
        for _ in range(2):
            project_columns(p, pe, w, p.hT, p.both_tiles)
        if j:
            down(j - 1)
    down(FC // 2 - 1)
    for k in range(4):
        closing[k].then_inc(p.dve_tiles.full, 1)
    p.mark["mix3"] = p.dve_tiles.opened
    for _ in range(LAYER_UNITS - w.n):
        w.next()
        w.used()
    w.flush()


def attention_x(p, name, eng, w=None):
    items = X_ITEMS
    n0 = len(HEAD_ITEMS)
    if name == "pe":
        for t in range(len(items) + 2):
            if t < len(items):
                scores_pe(p, eng, w, n0 + t, items[t])
            if t >= 2:
                probs_transpose_pe(p, eng, w, n0 + t - 2, items[t - 2])
                values_pe(p, eng, w, n0 + t - 2, items[t - 2], t)
    elif name == "dve":
        for t in range(len(items) + 1):
            if t < len(items):
                softmax_max_dve(p, eng, n0 + t, items[t])
            if t >= 1:
                softmax_scale_dve(p, eng, n0 + t - 1, items[t - 1])
    else:
        for t in range(len(items) + 2):
            if t < len(items):
                softmax_exp_act(p, eng, n0 + t, items[t])
            if t >= 2:
                h = items[t - 2][1]
                eng.e.wait_ge(p.act_tiles.full, p.act_tiles.turn(eng))
                bank = shaped(p.act_tiles.take(eng), NB, S)
                eng.e.activation(p.pT[t % 2], bank, ACT.Copy).then_inc(p.act_tiles.drained, 1)
                eng.e.wait_ge(p.act_tiles.full, p.act_tiles.turn(eng))
                bank = shaped(p.act_tiles.take(eng), 2, S)
                eng.e.activation(p.mixT[:, 2 * h:2 * h + 2, :], bank, ACT.Copy).then_inc(p.act_tiles.drained, 1)


def layer_act(p, act):
    act.e.wait_ge(p.sem("layer_params"), 16)
    norm_stats(p, act, p.x, D, p.rstd, "rstd")
    act.e.wait_ge(p.sem("lambda_sums"), 1)
    act.e.activation(p.lam[:, 0:2], p.lam[:, 0:2], ACT.Exp).then_inc(act.event("lambda_exps"), 1)
    rows_to_columns_evac(p, act, p.hT, p.lp("g_mix_pre"), KC, True)
    for j in range(5):
        act.e.wait_ge(p.act_tiles.full, p.act_tiles.turn(act))
        bank = p.act_tiles.take(act)
        n = 2 if j < 4 else 1
        act.e.activation(p.qk[:, 2 * j:2 * j + n, :], shaped(bank[:, 0:n * S], n, S), ACT.Copy).then_inc(p.act_tiles.drained, 1)
    latent_stats_act(p, act)
    attention_act(p, act, HEAD_ITEMS, p.mixT, None, {16: lambda: mla_act(p, act)})
    act.e.wait_ge(p.sem("diff_squares"), 1)
    act.e.activation(p.diff_ss[:, 8:16], p.diff_ss[:, 0:8], ACT.Ln, scale=1.0 / 64, bias=p.c("eps")).then_inc(act.step(), 1)
    act.e.wait_ge(act.steps, act.n)
    act.e.activation(p.diff_ss[:, 16:24], p.diff_ss[:, 8:16], ACT.Exp, scale=-0.5).then_inc(act.event("diff_rstd"), 1)
    act.e.wait_ge(p.sem("diff_gain"), 1)
    act.e.wait_ge(p.act_tiles.full, p.act_tiles.turn(act))
    bank = p.act_tiles.take(act)
    for c in range(2):
        ins = act.e.activation(p.mixT[:, c, :], bank[:, c * S:(c + 1) * S], ACT.Copy, scale=p.small[:, 200:201])
        if c:
            ins.then_inc(p.act_tiles.drained, 1)
        else:
            ins.then_inc(act.step(), 1)
    post_stats_act(p, act, 1)
    act.e.wait_ge(p.sem("x_ready"), 1)
    norm_stats(p, act, p.x, D, p.rstd, "rstd")
    rows_to_columns_evac(p, act, p.hT, p.lp("g_x_pre"), KC, True)
    for j in range(4):
        act.e.wait_ge(p.act_tiles.full, p.act_tiles.turn(act))
        bank = p.act_tiles.take(act)
        act.e.activation(p.xqT[:, 2 * j:2 * j + 2, :], shaped(bank, 2, S), ACT.Copy).then_inc(p.act_tiles.drained, 1)
    attention_x(p, "act", act)
    post_stats_act(p, act, 2)
    act.e.wait_ge(p.sem("x_ready"), 2)
    norm_stats(p, act, p.x, D, p.rstd, "rstd")
    rows_to_columns_evac(p, act, p.hT, p.lp("g_ffn_pre"), KC, True)
    p.both_tiles.taken["act"] = p.mark["hidden"]
    for f in range(FC):
        act.e.wait_ge(p.both_tiles.full, p.both_tiles.turn(act))
        bank = p.both_tiles.take(act)
        if f >= 2:
            act.e.wait_ge(p.both_tiles.drained, p.mark["hidden"] + f - 1)
        act.e.activation(p.silu[:, f % 2, :], bank[:, 0:S], ACT.Silu).then_inc(act.event("silu_ready"), 1)
    post_stats_act(p, act, 3)


def layer_dve(p, dve):
    dve.e.wait_ge(p.sem("layer_params"), 16)
    prod = shaped(p.junk_dve[:, 0:64], 2, 32)
    lam4 = p.lp("lambda", 2, 2, 32)
    dve.e.tensor_tensor(prod, lam4[:, :, 0, :], lam4[:, :, 1, :], ALU.mult).then_inc(dve.step(), 1)
    dve.e.wait_ge(dve.steps, dve.n)
    dve.e.tensor_reduce(p.lam[:, 0:2], prod, AX, ALU.add).then_inc(dve.event("lambda_sums"), 1)
    dve.e.tensor_tensor(p.small[:, 200:201], p.lp("g_diff"), p.lp("lam_rest"), ALU.mult).then_inc(dve.event("diff_gain"), 1)
    norm_rows(p, dve, p.x, p.rstd, p.hrow, D, "rstd", 1)
    dve.e.wait_ge(p.sem("lambda_exps"), 1)
    dve.e.scalar_tensor_tensor(p.lam[:, 0:1], p.lam[:, 0:1], p.lp("lam_init"), p.lam[:, 1:2],
                                      ALU.add, ALU.subtract).then_inc(dve.step(), 1)
    dve.e.wait_ge(dve.steps, dve.n)
    rows_to_columns_evac(p, dve, p.hT, p.lp("g_mix_pre"), KC, False)
    for b in range(NB):
        dve.e.wait_ge(p.dve_tiles.full, p.dve_tiles.turn(dve))
        bank = p.dve_tiles.take(dve)
        dve.e.tensor_copy(p.mla[:, b, :], bank[:, 0:416]).then_inc(p.dve_tiles.drained, 1)
    for b in range(NB):
        dve.e.wait_ge(p.dve_tiles.full, p.dve_tiles.turn(dve))
        bank = p.dve_tiles.take(dve)
        dve.e.tensor_copy(p.v_row[:, b, :], bank[:, 0:384]).then_inc(p.dve_tiles.drained, 1)

    def memory(u):
        if u < 4:
            dve.e.wait_ge(p.dve_tiles.full, p.dve_tiles.turn(dve))
            bank = p.dve_tiles.take(dve)
            dve.e.tensor_copy(p.xkT[:, 2 * u:2 * u + 2, :], shaped(bank, 2, S)).then_inc(p.dve_tiles.drained, 1)
        elif u in (4, 6):
            o = 0 if u == 4 else 512
            for b in range(NB):
                dve.e.wait_ge(p.dve_tiles.full, p.dve_tiles.turn(dve))
                bank = p.dve_tiles.take(dve)
                dve.e.tensor_copy(p.xv[:, b, o:o + 512], bank).then_inc(p.dve_tiles.drained, 1)
    for t in range(len(HEAD_ITEMS) + 1):
        if t == 16:
            mla_dve(p, dve)
        if t < len(HEAD_ITEMS):
            softmax_max_dve(p, dve, t, HEAD_ITEMS[t])
        if t >= 1:
            softmax_scale_dve(p, dve, t - 1, HEAD_ITEMS[t - 1])
        if t >= 2 and has_output(HEAD_ITEMS[t - 2]):
            i = t - 2
            u = beside(HEAD_ITEMS[i], i)
            if u is not None:
                memory(u)
    dve.e.wait_ge(p.act_tiles.drained, p.mark["diff"])
    o4 = p.o_diff.rearrange("p b (h d) -> p (b h) d", d=64)
    sq = shaped(p.junk_dve[:, 0:512], 8, 64)
    dve.e.tensor_tensor(sq, o4, o4, ALU.mult).then_inc(dve.step(), 1)
    dve.e.wait_ge(dve.steps, dve.n)
    dve.e.tensor_reduce(p.diff_ss[:, 0:8], sq, AX, ALU.add).then_inc(dve.event("diff_squares"), 1)
    dve.e.wait_ge(p.sem("diff_rstd"), 1)
    dve.e.tensor_tensor(o4, o4, p.diff_ss[:, 16:24].unsqueeze(2).to_broadcast([P, 8, 64]), ALU.mult).then_inc(dve.event("diff_rows"), 1)
    residual_dve(p, dve, p.lp("g_mix_post"), 1, 2)
    norm_rows(p, dve, p.x, p.rstd, p.hrow, D, "rstd", 3)
    rows_to_columns_evac(p, dve, p.hT, p.lp("g_x_pre"), KC, False)
    attention_x(p, "dve", dve)
    residual_dve(p, dve, p.lp("g_x_post"), 2, 4)
    norm_rows(p, dve, p.x, p.rstd, p.hrow, D, "rstd", 5)
    rows_to_columns_evac(p, dve, p.hT, p.lp("g_ffn_pre"), KC, False)
    for f in range(FC):
        dve.e.wait_ge(p.both_tiles.full, p.both_tiles.turn(dve))
        bank = p.both_tiles.take(dve)
        dve.e.wait_ge(p.sem("silu_ready"), f + 1)
        dve.e.tensor_tensor(p.h1T[:, f, :], p.silu[:, f % 2, :], bank[:, S:2 * S], ALU.mult).then_inc(p.both_tiles.drained, 1)
    residual_dve(p, dve, p.lp("g_ffn_post"), 3, 6)



TWO_PI = 2.0 * math.pi
TURN_HI = 6.28125
TURN_MID = float(np.float32(np.round((TWO_PI - TURN_HI) * 2 ** 21) / 2 ** 21))
TURN_LO = TWO_PI - TURN_HI - TURN_MID
ROUND = 1.5 * 2.0 ** 23
SIN_MAX = 3.1415925


def prologue_dve(p, dve):
    dve.e.wait_ge(p.sem("positions_loaded"), 32)
    posf, posc = p.junk_dve[:, 0:256], p.small[:, 140:142]
    dve.e.tensor_copy(posf, p.pos[:, 0:256]).then_inc(dve.step(), 1)
    dve.e.tensor_copy(posc, p.pos[:, 256:258]).then_inc(dve.step(), 1)
    dve.e.wait_ge(dve.steps, dve.n)
    dve.e.wait_ge(p.sem("const_loaded"), 16)
    for b in range(NB):
        d = p.dist[:, b, :]
        dve.e.tensor_scalar(d, posf, posc[:, b:b + 1], None, ALU.subtract).then_inc(dve.step(), 1)
        dve.e.wait_ge(dve.steps, dve.n)
        dve.e.scalar_tensor_tensor(d, d, -1.0, d, ALU.mult, ALU.max).then_inc(dve.step(), 1)
    ang, turns = shaped(p.junk_dve[:, 256:288], NB, 16), p.junk_dve[:, 320:352]
    flat = p.junk_dve[:, 256:288]
    for b in range(NB):
        dve.e.tensor_scalar(ang[:, b, :], p.c("inv"), posc[:, b:b + 1], None, ALU.mult).then_inc(dve.step(), 1)
    dve.e.wait_ge(dve.steps, dve.n)
    dve.e.tensor_tensor(p.dist_swa, p.dist, p.c("swa_far", NB, S), ALU.add).then_inc(dve.step(), 1)
    for which, quarter in ((0, 0.25), (1, 0.0)):
        red = p.junk_dve[:, 384 + 32 * which:416 + 32 * which]
        dve.e.tensor_scalar(turns, flat, 1.0 / TWO_PI, quarter, ALU.mult, ALU.add).then_inc(dve.step(), 1)
        dve.e.wait_ge(dve.steps, dve.n)
        dve.e.tensor_scalar(turns, turns, ROUND, None, ALU.add).then_inc(dve.step(), 1)
        dve.e.wait_ge(dve.steps, dve.n)
        dve.e.tensor_scalar(turns, turns, ROUND, None, ALU.subtract).then_inc(dve.step(), 1)
        dve.e.wait_ge(dve.steps, dve.n)
        dve.e.scalar_tensor_tensor(red, turns, -TURN_HI, flat, ALU.mult, ALU.add).then_inc(dve.step(), 1)
        dve.e.wait_ge(dve.steps, dve.n)
        dve.e.scalar_tensor_tensor(red, turns, -TURN_MID, red, ALU.mult, ALU.add).then_inc(dve.step(), 1)
        dve.e.wait_ge(dve.steps, dve.n)
        dve.e.scalar_tensor_tensor(red, turns, -TURN_LO, red, ALU.mult, ALU.add).then_inc(dve.step(), 1)
        dve.e.wait_ge(dve.steps, dve.n)
        dve.e.tensor_scalar(red, red, quarter * TWO_PI, SIN_MAX, ALU.add, ALU.min).then_inc(dve.step(), 1)
        dve.e.wait_ge(dve.steps, dve.n)
        dve.e.tensor_scalar(red, red, -SIN_MAX, None, ALU.max).then_inc(dve.event("angles_ready"), 1)
    norm_rows(p, dve, p.xv, p.rstd, p.hrow, D, "mem_rstd", 1)
    rows_to_columns_evac(p, dve, p.memT, None, KC, False)


def prologue_act(p, act):
    act.e.wait_ge(p.sem("const_loaded"), 16)
    act.e.wait_ge(p.sem("mem_loaded"), 16)
    norm_stats(p, act, p.xv, D, p.rstd, "mem_rstd")
    rows_to_columns_evac(p, act, p.memT, None, KC, True)
    act.e.wait_ge(p.sem("angles_ready"), 2)
    act.e.activation(p.rot.rearrange("p a b c -> p (a b c)"), p.junk_dve[:, 384:448], ACT.Sin).then_inc(act.step(), 1)


def prologue_pe(p, pe, w):
    pe.e.wait_ge(p.sem("const_loaded"), 16)
    rows_to_columns_pe(p, pe, w, p.hrow, KC, "mem_rstd", 1)


def layer_pool(p, pool):
    pool.e.wait_ge(p.sem("layer_params"), 16)
    pool.e.wait_ge(p.act_tiles.drained, 2)
    pool.e.wait_ge(p.dve_tiles.drained, 2)
    for c in range(KC):
        ins = pool.e.tensor_scalar(p.memgT[:, c, :], p.memT[:, c, :], p.lp("g_x_mem")[:, c:c + 1], None, ALU.mult)
        if c == KC - 1:
            ins.then_inc(pool.event("memory_gained"), 1)



def second_buffers(p):
    p.at = 0
    p.hrow = p.take(NB, D)
    p.y_att = p.arena[:, 0:1024].rearrange("p (c t) -> p c t", c=4)
    p.y_pool = p.arena[:, 1024:2048].rearrange("p (c t) -> p c t", c=4)
    p.hT = p.take(KC, S)
    p.shifted = p.take(15, S)
    mark = p.at
    p.raw = p.take(19, S)
    p.att = p.take(NB, 768)
    p.qk2 = p.take(5, S)
    p.att_sq = p.take(NB, 640)
    p.zp = [p.take(4, 272) for _ in range(2)]
    p.zp_wide = p.arena[:, p.at - 2176:p.at - 128].rearrange("p (c t) -> p c t", c=8)
    p.pooled = p.take(4, S)
    p.sc = [p.take(NB, S) for _ in range(4)]
    p.pr = [p.take(NB, S) for _ in range(4)]
    p.junk_act = p.arena[:, p.at - 1024:p.at]
    p.pT = [p.take(NB, S) for _ in range(2)]
    p.gate_out = [p.take(2, S) for _ in range(2)]
    p.at = mark
    p.sig = p.take(2, 4, S)
    p.dec = p.take(2, 4, S)
    p.inv_dec = p.take(2, 4, S)
    p.iclr = p.take(2, 4, S)
    p.kd = p.take(4, S)
    p.kk = p.take(4, S)
    p.ksum = p.take(4, S)
    p.gate = p.sig[:, 0]
    p.alpha_rho = p.arena[:, mark:mark + 4096].rearrange("p (w e q t) -> p w e q t", w=2, e=2, q=4)
    BETA, KAPPA, rest = [], [], []
    for _ in range(2):
        BETA.append(p.take(8, 2, CH))
        KAPPA.append(p.take(8, 2, CH))
    for _ in range(5):
        rest.append(p.take(8, CH))
    hT, low = flat(p.hT), flat(p.shifted)
    far, cnt = CONST["swa_far"][0], CONST["pool_cnt"][0]
    for buffer, at in ((hT, 0), (hT, 512), (hT, 1024), (hT, 1536), (low, 3072), (p.par, SECOND_W),
                       (p.par, SECOND_W + 512), (p.const, far), (p.const, cnt), (p.const, cnt + 512)):
        rest.append(shaped(buffer[:, at:at + 512], 8, CH))
    p.BETA, p.KAPPA = BETA, KAPPA
    p.X, p.XT, p.Pb, p.Br, p.Kr, p.Vr = [rest[2 * j:2 * j + 2] for j in range(6)]
    p.U, p.ST = rest[12:14]
    p.at = mark
    p.gates = p.take(24, S)
    assert p.at <= mark + 4 * 2048
    p.at = mark + 4 * 2048 + 4 * 1024
    p.merged = p.take(KC, S)
    p.prod = p.take(2, S)
    p.at = mark
    p.sel = p.take(NB, E_N * CAP)
    p.selw = p.take(NB, E_N * CAP)
    p.sel_g = p.take(NB, P)
    p.selw_g = p.take(NB, P)
    p.xg = p.take(KC, P)
    p.back = p.take(S)
    p.silu_e = p.take(512)
    p.h1 = [p.take(512) for _ in range(2)]
    p.h1g = p.take(KC, P)
    p.y_e = [p.take(512) for _ in range(2)]
    p.aff = p.take(NB, E_N)
    p.posT = p.take(NB, E_N)
    p.affT, p.mask, p.cum, p.ones = [p.take(S) for _ in range(4)]
    p.top = p.take(8)
    assert p.at <= p.arena_w - (EXPERT_SLOTS - SLOTS) * UNIT
    p.rstd2 = p.small[:, 64 + 96:64 + 98]
    p.gt = p.small[:, 204:236]
    p.cols = p.small[:, 112:112 + 15 + 4]
    p.att_ss = p.small[:, 140:200]


def flat(ap):
    names = "abcd"[:len(ap.shape) - 1]
    return ap.rearrange(f"p {' '.join(names)} -> p ({' '.join(names)})")


def chunk_of(e, c):
    return c if e == 0 else NCH - 1 - c


def columns_of(c):
    return [slice(chunk_of(e, c) * CH, chunk_of(e, c) * CH + CH) for e in range(2)]


def each_head():
    for e in range(2):
        for q in range(PAIRS):
            for par in range(2):
                yield e, q, slice(64 * par, 64 * par + 64), e * PAIRS + q


def head_products(p, pe, tiles, terms):
    if tiles.opened >= tiles.size:
        pe.e.wait_ge(tiles.drained, tiles.opened - tiles.size + 1)
    bank = shaped(tiles.open(pe), 8, CH)
    for e, q, r, o in each_head():
        ts = terms(e, q, r, o)
        for j, (a, b) in enumerate(ts):
            ins = pe.e.matmul(bank[r, o, :], a, b, start=j == 0, stop=j == len(ts) - 1)
    ins.then_inc(tiles.full, 1)


def second_pe(p, pe, w):
    w.start(16 * DEPTH * LAYER_UNITS // SLOTS, p.slots, p.slot_loaded, p.slots_free)
    pe.e.wait_ge(p.sem("second_params"), 16)
    rows_to_columns_pe(p, pe, w, p.hrow, KC, "rstd", 1)
    columns_ready(p, pe)
    for _ in range(3):
        project_rows(p, pe, w, p.hT, p.dve_tiles, 256, 1)
    for j in range(10):
        project_columns(p, pe, w, p.hT, p.act_tiles, 2 if j < 9 else 1)
    p.mark["raw"] = p.act_tiles.opened
    for _ in range(2):
        project_columns(p, pe, w, p.hT, p.act_tiles)
    rows_to_columns_pe(p, pe, w, p.att, 5, "qk", 1)
    columns_ready(p, pe)
    attention_pe(p, pe, w, GQA_ITEMS, lambda _: project_columns(p, pe, w, p.hT, p.act_tiles))
    pe.e.wait_ge(p.sem("pooled"), 1)
    for j in range(2):
        if p.act_tiles.opened >= p.act_tiles.size:
            pe.e.wait_ge(p.act_tiles.drained, p.act_tiles.opened - p.act_tiles.size + 1)
        bank = p.act_tiles.open(pe)
        for c in range(2):
            g = 2 * j + c
            ins = pe.e.matmul(bank[:, c * S:(c + 1) * S], p.sp("pool_w", 4, P)[:, g, :], p.pooled[:, g, :])
        ins.then_inc(p.act_tiles.full, 1)
    p.mark["pool"] = p.act_tiles.opened
    for _ in range(2):
        project_columns(p, pe, w, p.hT, p.act_tiles)
    pe.e.wait_ge(p.sem("lora_in"), 1)
    for name, src in (("w2", 12), ("a2", 13)):
        for e in range(2):
            for j in range(2):
                if p.act_tiles.opened >= p.act_tiles.size:
                    pe.e.wait_ge(p.act_tiles.drained, p.act_tiles.opened - p.act_tiles.size + 1)
                bank = p.act_tiles.open(pe)
                r = slice(64 * e, 64 * e + 64)
                for c in range(2):
                    q = 2 * j + c
                    ins = pe.e.matmul(bank[:, c * S:(c + 1) * S], p.sp(name)[r, q * P:(q + 1) * P],
                                      p.shifted[r, src, :])
                ins.then_inc(p.act_tiles.full, 1)

    def head_sums(src, event, n):
        pe.e.wait_ge(p.sem(event), n)
        for j in range(2):
            if p.dve_tiles.opened >= p.dve_tiles.size:
                pe.e.wait_ge(p.dve_tiles.drained, p.dve_tiles.opened - p.dve_tiles.size + 1)
            bank = p.dve_tiles.open(pe)
            pe.e.matmul(bank, p.c("headsum"), flat(src)[:, j * 512:(j + 1) * 512]).then_inc(p.dve_tiles.full, 1)
    head_sums(p.kd, "squares", 1)
    head_sums(p.kd, "bonus_in", 1)
    pe.e.wait_ge(p.sem("recurrence_in"), 1)
    alpha, rho, beta, kappa = p.sig, p.dec, p.iclr, p.inv_dec
    eye = p.c("eye64")
    for m in range(NCH // 2):
        for i in range(2):
            cols = columns_of(2 * m + i)
            for e in range(2):
                for left in (beta, kappa):
                    if p.dve_tiles.opened >= p.dve_tiles.size:
                        pe.e.wait_ge(p.dve_tiles.drained, p.dve_tiles.opened - p.dve_tiles.size + 1)
                    bank = shaped(p.dve_tiles.open(pe), 4, 2, CH)
                    for q in range(PAIRS):
                        for par in range(2):
                            r = slice(64 * par, 64 * par + 64)
                            ins = pe.e.matmul(bank[r, q], left[r, e, q, cols[e]], p.alpha_rho[r, :, e, q, cols[e]])
                    ins.then_inc(p.dve_tiles.full, 1)
            head_products(p, pe, p.act_tiles, lambda e, q, r, o: [(p.shifted[r, 8 + q, cols[e]], eye[r, :])])
            head_products(p, pe, p.act_tiles, lambda e, q, r, o: [(beta[r, e, q, cols[e]], eye[r, :])])
            head_products(p, pe, p.act_tiles, lambda e, q, r, o: [(kappa[r, e, q, cols[e]], eye[r, :])])
        for n in range(6):
            for i in range(2):
                pe.e.wait_ge(p.sem("level_masked"), 12 * m + 2 * n + i + 1)
                if n == 0:
                    head_products(p, pe, p.dve_tiles, lambda e, q, r, o: [(p.Pb[i][r, o, :], eye[r, :])])
                else:
                    head_products(p, pe, p.act_tiles, lambda e, q, r, o: [(p.Pb[i][r, o, :], p.X[i][r, o, :])])
                    p.mark[f"P{i}"] = p.act_tiles.opened
            for i in range(2 if n else 0):
                pe.e.wait_ge(p.act_tiles.drained, p.mark[f"P{i}"])
                if n < 5:
                    head_products(p, pe, p.dve_tiles, lambda e, q, r, o: [(p.XT[i][r, o, :], p.Pb[i][r, o, :])])
                head_products(p, pe, p.dve_tiles, lambda e, q, r, o: [(p.Pb[i][r, o, :], p.XT[i][r, o, :])])
        for i in range(2):
            c = 2 * m + i
            cols = columns_of(c)
            pe.e.wait_ge(p.dve_tiles.drained, p.dve_tiles.opened)
            pe.e.wait_ge(p.sem("state_ready"), c + 1)
            head_products(p, pe, p.act_tiles, lambda e, q, r, o: [(alpha[r, e, q, cols[e]], p.ST[r, o, :]),
                                                                  (p.KAPPA[i][r, o, 0, :], p.Vr[i][r, o, :])])
            pe.e.wait_ge(p.act_tiles.drained, p.act_tiles.opened)
            head_products(p, pe, p.act_tiles, lambda e, q, r, o: [(p.XT[i][r, o, :], p.Pb[i][r, o, :])])
            pe.e.wait_ge(p.act_tiles.drained, p.act_tiles.opened)
            head_products(p, pe, p.dve_tiles, lambda e, q, r, o: [(p.Br[i][r, o, :], p.U[r, o, :]),
                                                                  (p.Kr[i][r, o, :], p.Vr[i][r, o, :])])
            head_products(p, pe, p.act_tiles, lambda e, q, r, o: [(p.ST[r, o, :], rho[r, e, q, cols[e]]),
                                                                  (p.U[r, o, :], p.BETA[i][r, o, 1, :]),
                                                                  (p.Vr[i][r, o, :], p.KAPPA[i][r, o, 1, :])])
            p.mark[f"y{c}"] = p.act_tiles.opened
    for j in range(2):
        if p.act_tiles.opened >= p.act_tiles.size:
            pe.e.wait_ge(p.act_tiles.drained, p.act_tiles.opened - p.act_tiles.size + 1)
        bank = p.act_tiles.open(pe)
        for c in range(2):
            q = 2 * j + c
            ins = pe.e.matmul(bank[:, c * S:(c + 1) * S], p.sp("g2")[:, q * P:(q + 1) * P], p.shifted[:, 14, :])
        ins.then_inc(p.act_tiles.full, 1)
    head_sums(p.kd, "y_sum", 1)
    head_sums(p.kk, "y_sum", 2)
    pe.e.wait_ge(p.sem("y_rwkv"), 1)
    branches = [p.ksum, p.y_pool, p.y_att]
    for n in range(6):
        u = w.next()
        for t in range(2):
            if p.dve_tiles.opened >= p.dve_tiles.size:
                pe.e.wait_ge(p.dve_tiles.drained, p.dve_tiles.opened - p.dve_tiles.size + 1)
            bank = p.dve_tiles.open(pe)
            for c in range(2):
                i = 4 * n + 2 * t + c
                for k in range(4):
                    o = ((2 * t + c) * 4 + k) * P
                    last = c == 1 and k == 3
                    ins = (pe.e.matmul if last else w.mm)(bank[:, c * S:(c + 1) * S], u[:, o:o + P],
                                                          branches[i // 8][:, k, :], start=k == 0, stop=k == 3)
            ins.then_inc(p.dve_tiles.full, 1)
        w.used()
    pe.e.wait_ge(p.sem("merged"), 1)
    for _ in range(2):
        project_rows(p, pe, w, p.merged, p.dve_tiles, 512)
    p.mark["mixed"] = p.dve_tiles.opened
    rows_to_columns_pe(p, pe, w, p.hrow, KC, "rstd", 2)
    columns_ready(p, pe)
    if p.dve_tiles.opened >= p.dve_tiles.size:
        pe.e.wait_ge(p.dve_tiles.drained, p.dve_tiles.opened - p.dve_tiles.size + 1)
    bank = p.dve_tiles.open(pe)
    for b in range(NB):
        for k in range(KC):
            ins = pe.e.matmul(bank[:, b * E_N:(b + 1) * E_N], p.hT[:, k, b * P:(b + 1) * P],
                              p.sp("router", KC, E_N)[:, k, :], start=k == 0, stop=k == KC - 1)
    ins.then_inc(p.dve_tiles.full, 1)
    pe.e.wait_ge(p.sem("affinities"), 1)
    if p.dve_tiles.opened >= p.dve_tiles.size:
        pe.e.wait_ge(p.dve_tiles.drained, p.dve_tiles.opened - p.dve_tiles.size + 1)
    bank = p.dve_tiles.open(pe)
    for b in range(NB):
        ins = pe.e.transpose(bank[0:E_N, b * P:(b + 1) * P], p.aff[:, b, :], p.c("ident"))
    ins.then_inc(p.dve_tiles.full, 1)
    pe.e.wait_ge(p.sem("slots"), 1)
    if p.dve_tiles.opened >= p.dve_tiles.size:
        pe.e.wait_ge(p.dve_tiles.drained, p.dve_tiles.opened - p.dve_tiles.size + 1)
    bank = p.dve_tiles.open(pe)
    for b in range(NB):
        ins = pe.e.transpose(bank[:, b * E_N:(b + 1) * E_N], p.cum[0:E_N, b * P:(b + 1) * P],
                             p.c("ident")[0:E_N, 0:E_N])
    ins.then_inc(p.dve_tiles.full, 1)
    for _ in range(BLOCK2_UNITS - w.n):
        w.next()
        w.used()
    w.flush()
    pe.finish("second", 0)
    p.reset_rings("pe")
    with pe.e.Fori(0, G_N) as g:
        w.start(g * (16 * GROUP_UNITS // EXPERT_SLOTS), p.expert_slots, p.expert_slot_loaded, p.expert_slots_used)
        experts_pe(p, pe, w)
        pe.finish("experts", g)
        p.reset_rings("pe")


def expert_product(p, pe, w, src, tiles):
    if tiles.opened >= tiles.size:
        pe.e.wait_ge(tiles.drained, tiles.opened - tiles.size + 1)
    bank = tiles.open(pe)
    for h in range(2):
        us = [w.next() for _ in range(GE)]
        for k in range(4):
            for e in range(GE):
                r = slice(CAP * e, CAP * e + CAP)
                last = h == 1 and k == 3 and e == GE - 1
                ins = (pe.e.matmul if last else w.mm)(bank[r, :], src[:, 4 * h + k, r],
                                                      us[e][:, k * 512:(k + 1) * 512],
                                                      start=h == 0 and k == 0, stop=h == 1 and k == 3)
        w.used(GE)
    ins.then_inc(tiles.full, 1)


def experts_pe(p, pe, w):
    pe.e.wait_ge(p.sem("group_selected"), 1)
    for j in range(2):
        if p.act_tiles.opened >= p.act_tiles.size:
            pe.e.wait_ge(p.act_tiles.drained, p.act_tiles.opened - p.act_tiles.size + 1)
        bank = shaped(p.act_tiles.open(pe), 4, P)
        for c in range(4):
            for b in range(NB):
                ins = pe.e.matmul(bank[:, c, :], p.hrow[:, b, (4 * j + c) * P:(4 * j + c + 1) * P],
                                  p.sel_g[:, b, :], start=b == 0, stop=b == NB - 1)
        ins.then_inc(p.act_tiles.full, 1)
    if p.dve_tiles.opened >= p.dve_tiles.size:
        pe.e.wait_ge(p.dve_tiles.drained, p.dve_tiles.opened - p.dve_tiles.size + 1)
    bank = p.dve_tiles.open(pe)
    for b in range(NB):
        ins = pe.e.transpose(bank[:, b * P:(b + 1) * P], p.selw_g[:, b, :], p.c("ident"))
    ins.then_inc(p.dve_tiles.full, 1)
    pe.e.wait_ge(p.act_tiles.drained, p.act_tiles.opened)
    for f in range(2):
        expert_product(p, pe, w, p.xg, p.act_tiles)
        expert_product(p, pe, w, p.xg, p.dve_tiles)
        pe.e.wait_ge(p.dve_tiles.drained, p.dve_tiles.opened)
        if p.act_tiles.opened >= p.act_tiles.size:
            pe.e.wait_ge(p.act_tiles.drained, p.act_tiles.opened - p.act_tiles.size + 1)
        bank = p.act_tiles.open(pe)
        for c in range(4):
            ins = w.transpose(bank[:, c * P:(c + 1) * P], p.h1[f][:, c * P:(c + 1) * P], p.c("ident")) if c < 3 else \
                pe.e.transpose(bank[:, c * P:(c + 1) * P], p.h1[f][:, c * P:(c + 1) * P], p.c("ident"))
        ins.then_inc(p.act_tiles.full, 1)
    pe.e.wait_ge(p.act_tiles.drained, p.act_tiles.opened)
    for f in range(2):
        expert_product(p, pe, w, p.h1g, p.act_tiles)
        pe.e.wait_ge(p.act_tiles.drained, p.act_tiles.opened)
        for b in range(NB):
            if p.dve_tiles.opened >= p.dve_tiles.size:
                pe.e.wait_ge(p.dve_tiles.drained, p.dve_tiles.opened - p.dve_tiles.size + 1)
            bank = p.dve_tiles.open(pe)
            pe.e.matmul(bank, p.back[:, b * P:(b + 1) * P], p.y_e[f]).then_inc(p.dve_tiles.full, 1)
    w.flush()


def experts_act(p, act):
    for j in range(2):
        act.e.wait_ge(p.act_tiles.full, p.act_tiles.turn(act))
        bank = shaped(p.act_tiles.take(act), 4, P)
        for c in range(4):
            g = p.sp("g_ffn")[:, 4 * j + c:4 * j + c + 1]
            ins = act.e.activation(p.xg[:, 4 * j + c, :], bank[:, c, :], ACT.Copy, scale=g)
            if c == 3:
                ins.then_inc(p.act_tiles.drained, 1)
            else:
                ins.then_inc(act.step(), 1)
    for f in range(2):
        act.e.wait_ge(p.act_tiles.full, p.act_tiles.turn(act))
        bank = p.act_tiles.take(act)
        if f:
            act.e.wait_ge(p.dve_tiles.drained, 2)
        act.e.activation(p.silu_e, bank, ACT.Silu).then_inc(p.act_tiles.drained, 1)
        act.e.wait_ge(p.act_tiles.full, p.act_tiles.turn(act))
        bank = shaped(p.act_tiles.take(act), 4, P)
        act.e.activation(p.h1g[:, 4 * f:4 * f + 4, :], bank, ACT.Copy).then_inc(p.act_tiles.drained, 1)
    for f in range(2):
        act.e.wait_ge(p.act_tiles.full, p.act_tiles.turn(act))
        bank = p.act_tiles.take(act)
        act.e.activation(p.y_e[f], bank, ACT.Copy).then_inc(p.act_tiles.drained, 1)


def experts_dve(p, dve, g):
    dve.e.tensor_copy(p.selw_g, p.selw[:, :, bass.ds(g * P, P)]).then_inc(dve.step(), 1)
    dve.e.wait_ge(dve.steps, dve.n)
    dve.e.tensor_copy(p.sel_g, p.sel[:, :, bass.ds(g * P, P)]).then_inc(dve.event("group_selected"), 1)
    dve.e.wait_ge(p.dve_tiles.full, p.dve_tiles.turn(dve))
    bank = p.dve_tiles.take(dve)
    dve.e.tensor_copy(p.back, bank[:, 0:S]).then_inc(p.dve_tiles.drained, 1)
    for f in range(2):
        dve.e.wait_ge(p.dve_tiles.full, p.dve_tiles.turn(dve))
        bank = p.dve_tiles.take(dve)
        dve.e.wait_ge(p.act_tiles.drained, 3 + 2 * f)
        dve.e.tensor_tensor(p.h1[f], p.silu_e, bank, ALU.mult).then_inc(p.dve_tiles.drained, 1)
    for f in range(2):
        for b in range(NB):
            dve.e.wait_ge(p.dve_tiles.full, p.dve_tiles.turn(dve))
            bank = p.dve_tiles.take(dve)
            x = p.x[:, b, f * 512:(f + 1) * 512]
            dve.e.tensor_tensor(x, x, bank, ALU.add).then_inc(p.dve_tiles.drained, 1)
    dve.e.wait_ge(p.dve_tiles.drained, p.dve_tiles.taken["dve"])


def second_act(p, act):
    norm_stats(p, act, p.x, D, p.rstd2, "rstd")
    rows_to_columns_evac(p, act, p.hT, p.sp("g_mix"), KC, True)
    for j in range(10):
        n = 2 if j < 9 else 1
        act.e.wait_ge(p.act_tiles.full, p.act_tiles.turn(act))
        bank = p.act_tiles.take(act)
        ins = act.e.activation(p.raw[:, 2 * j:2 * j + n, :], shaped(bank[:, 0:n * S], n, S), ACT.Copy)
        ins.then_inc(p.act_tiles.drained, 1)

    def gate_unit(_):
        j = p.gates_out
        p.gates_out += 1
        act.e.wait_ge(p.act_tiles.full, p.act_tiles.turn(act))
        bank = shaped(p.act_tiles.take(act), 2, S)
        if j >= 2:
            act.e.wait_ge(p.sem(f"gate_stored_{j % 2}"), 16 * (j // 2))
        act.e.activation(p.gate_out[j % 2], bank, ACT.Copy).then_inc(p.act_tiles.drained, 1)
        act.e.wait_ge(p.act_tiles.drained, p.act_tiles.taken["act"])
        act.e.dma_start(p.gate_dram[j], flat(p.gate_out[j % 2])).then_inc(p.sem(f"gate_stored_{j % 2}"), 16)
    p.gates_out = 0
    gate_unit(0)
    gate_unit(1)
    act.e.wait_ge(p.sem("att_squares"), 1)
    act.e.activation(p.att_ss[:, 20:40], p.att_ss[:, 0:20], ACT.Ln, scale=1.0 / 64, bias=p.c("eps")).then_inc(act.step(), 1)
    act.e.wait_ge(act.steps, act.n)
    act.e.activation(p.att_ss[:, 40:60], p.att_ss[:, 20:40], ACT.Exp, scale=-0.5).then_inc(act.event("att_rstd"), 1)
    rows_to_columns_evac(p, act, p.qk2, None, 5, True)
    attention_act(p, act, GQA_ITEMS, p.y_att, gate_unit)
    for j in range(2):
        act.e.wait_ge(p.act_tiles.full, p.act_tiles.turn(act))
        bank = p.act_tiles.take(act)
        for c in range(2):
            g = 2 * j + c
            ins = act.e.activation(p.y_pool[:, g, :], bank[:, c * S:(c + 1) * S], ACT.Copy,
                                   scale=p.sp("pool_scale")[:, g:g + 1])
            if c:
                ins.then_inc(p.act_tiles.drained, 1)
            else:
                ins.then_inc(act.step(), 1)
    gate_unit(10)
    gate_unit(11)
    act.e.wait_ge(p.sem("shift_done"), 1)
    act.e.activation(p.shifted[:, 12, :], p.shifted[:, 12, :], ACT.Tanh).then_inc(act.step(), 1)
    act.e.activation(p.shifted[:, 14, :], p.shifted[:, 14, :], ACT.Sigmoid).then_inc(act.event("lora_in"), 1)
    for name, dst in (("w0", p.sig), ("a0", p.iclr)):
        for e in range(2):
            for j in range(2):
                act.e.wait_ge(p.act_tiles.full, p.act_tiles.turn(act))
                bank = p.act_tiles.take(act)
                for c in range(2):
                    q = 2 * j + c
                    ins = act.e.activation(dst[:, e, q, :], bank[:, c * S:(c + 1) * S], ACT.Sigmoid,
                                           bias=p.sp(name)[:, e * 4 + q:e * 4 + q + 1])
                    if c:
                        ins.then_inc(p.act_tiles.drained, 1)
                    else:
                        ins.then_inc(act.step(), 1)
        p.mark[name] = p.act_tiles.taken["act"]
    act.e.wait_ge(p.sem("norms_in"), 1)
    act.e.activation(flat(p.kd), flat(p.kd), ACT.Ln).then_inc(act.step(), 1)
    act.e.wait_ge(act.steps, act.n)
    act.e.activation(flat(p.kd), flat(p.kd), ACT.Exp, scale=-0.5).then_inc(act.event("norms_out"), 1)
    act.e.wait_ge(p.sem("sums_ready"), 1)
    act.e.activation(flat(p.inv_dec), flat(p.dec), ACT.Exp, scale=DECAY).then_inc(act.step(), 1)
    act.e.wait_ge(act.steps, act.n)
    act.e.activation(flat(p.dec), flat(p.dec), ACT.Exp, scale=-DECAY).then_inc(act.step(), 1)
    act.e.wait_ge(act.steps, act.n)
    act.e.activation(flat(p.sig), flat(p.sig), ACT.Exp, scale=-DECAY).then_inc(act.event("decays_ready"), 1)

    def copy_out(dst, scale=1.0):
        act.e.wait_ge(p.act_tiles.full, p.act_tiles.turn(act))
        bank = shaped(p.act_tiles.take(act), 8, CH)
        act.e.activation(dst, bank, ACT.Copy, scale=scale).then_inc(p.act_tiles.drained, 1)
    for j in range(2):
        act.e.wait_ge(p.sem(f"gate_stored_{j}"), 16 * 6)
    for m in range(NCH // 2):
        for i in range(2):
            copy_out(p.Vr[i])
            copy_out(p.Br[i])
            copy_out(p.Kr[i])
        for n in range(1, 6):
            for i in range(2):
                copy_out(p.Pb[i])
        for i in range(2):
            cols = columns_of(2 * m + i)
            copy_out(p.Pb[i])
            copy_out(p.U, -1.0)
            act.e.wait_ge(p.act_tiles.full, p.act_tiles.turn(act))
            bank = shaped(p.act_tiles.take(act), 2, 4, CH)
            act.e.activation(p.kd[:, :, cols[0]], bank[:, 0], ACT.Copy).then_inc(act.step(), 1)
            act.e.activation(p.kk[:, :, cols[1]], bank[:, 1], ACT.Copy).then_inc(p.act_tiles.drained, 1)
    for j in range(2):
        act.e.wait_ge(p.act_tiles.full, p.act_tiles.turn(act))
        bank = shaped(p.act_tiles.take(act), 2, S)
        act.e.activation(p.gate[:, 2 * j:2 * j + 2, :], bank, ACT.Copy).then_inc(p.act_tiles.drained, 1)
    act.e.wait_ge(p.sem("variances_in"), 1)
    act.e.activation(flat(p.kk), flat(p.kk), ACT.Ln, scale=1.0 / 64, bias=p.c("ln_eps")).then_inc(act.step(), 1)
    act.e.wait_ge(act.steps, act.n)
    act.e.activation(flat(p.kk), flat(p.kk), ACT.Exp, scale=-0.5).then_inc(act.event("y_rstd"), 1)
    act.e.wait_ge(p.sem("y_rwkv"), 1)
    act.e.dma_start(p.gates.rearrange("p (n c) t -> p n (c t)", n=12), p.gate_dram.rearrange("n p w -> p n w")).then_inc(
        p.sem("gates_loaded"), 16)
    act.e.wait_ge(p.sem("gates_loaded"), 16)
    for b in range(3):
        g = flat(p.gates[:, 8 * b:8 * b + 8, :])
        act.e.activation(g, g, ACT.Sigmoid).then_inc(act.event("gates_ready"), 1)
    act.e.wait_ge(p.sem("mixed"), 1)
    norm_stats(p, act, p.x, D, p.rstd2, "rstd")
    rows_to_columns_evac(p, act, p.hT, p.sp("g_ffn"), KC, True)
    act.e.wait_ge(p.sem("logits"), 1)
    for b in range(NB):
        ins = act.e.activation(p.aff[:, b, :], p.aff[:, b, :], ACT.Exp, bias=p.cols[:, 2 + b:3 + b],
                               accum_out=p.cols[:, 4 + b:5 + b])
        if b:
            ins.then_inc(act.event("affinity_exps"), 1)
        else:
            ins.then_inc(act.step(), 1)
    act.finish("second", 0)
    p.reset_rings("act")
    with act.e.Fori(0, G_N) as g:
        experts_act(p, act)
        act.finish("experts", g)
        p.reset_rings("act")
    norm_stats(p, act, p.x, D, p.rstd2, "final_rstd")


def second_dve(p, dve):
    e_ = dve.e
    dve.e.wait_ge(p.sem("second_params"), 16)
    norm_rows(p, dve, p.x, p.rstd2, p.hrow, D, "rstd", 1)
    rows_to_columns_evac(p, dve, p.hT, p.sp("g_mix"), KC, False)
    for j in range(3):
        for b in range(NB):
            dve.e.wait_ge(p.dve_tiles.full, p.dve_tiles.turn(dve))
            bank = p.dve_tiles.take(dve)
            e_.tensor_copy(p.att[:, b, j * 256:(j + 1) * 256], bank[:, 0:256]).then_inc(p.dve_tiles.drained, 1)
    dve.e.wait_ge(p.dve_tiles.drained, p.dve_tiles.taken["dve"])
    qk = p.att[:, :, 0:640]
    e_.tensor_tensor(p.att_sq, qk, qk, ALU.mult).then_inc(dve.step(), 1)
    dve.e.wait_ge(dve.steps, dve.n)
    e_.tensor_reduce(p.att_ss[:, 0:20], p.att_sq.rearrange("p b (h d) -> p (b h) d", d=64), AX, ALU.add).then_inc(dve.event("att_squares"), 1)
    dve.e.wait_ge(p.sem("att_rstd"), 1)
    for b in range(NB):
        h = qk[:, b, :].rearrange("p (h d) -> p h d", d=64)
        rs = p.att_ss[:, 40 + 10 * b:50 + 10 * b].unsqueeze(2).to_broadcast([P, 10, 64])
        e_.tensor_tensor(h, h, rs, ALU.mult).then_inc(dve.step(), 1)
        dve.e.wait_ge(dve.steps, dve.n)
        e_.tensor_tensor(h[:, 0:8], h[:, 0:8], spread(p.sp("q_norm"), 1, 8), ALU.mult).then_inc(dve.step(), 1)
        e_.tensor_tensor(h[:, 8:10], h[:, 8:10], spread(p.sp("k_norm"), 1, 2), ALU.mult).then_inc(dve.step(), 1)
        dve.e.wait_ge(dve.steps, dve.n)
        pairs = qk[:, b, :].rearrange("p (h d two) -> p two h d", d=32, two=2)
        cos = spread(p.c("cos", NB, 32)[:, b, :], 1, 10)
        sin = spread(p.c("sin", NB, 32)[:, b, :], 1, 10)
        sq = flat(p.att_sq)
        tmp = [shaped(sq[:, j * 320:(j + 1) * 320], 10, 32) for j in range(4)]
        rotate(p, dve, (pairs[:, 0], pairs[:, 1]), pairs[:, 0], pairs[:, 1], cos, sin, tmp)
        dve.e.wait_ge(dve.steps, dve.n)
    e_.tensor_copy(p.small[:, 255:256], p.c("eps")).then_inc(dve.event("qk_rows"), 1)
    rows_to_columns_evac(p, dve, p.qk2, None, 5, False)
    attention_dve(p, dve, GQA_ITEMS)
    dve.e.wait_ge(p.sem("shift_done"), 1)
    dve.e.wait_ge(p.act_tiles.drained, p.mark["pool"])
    r, k, v = p.shifted[:, 0:4, :], p.shifted[:, 4:8, :], p.shifted[:, 8:12, :]
    for q in range(PAIRS):
        e_.tensor_scalar(p.kk[:, q, :], k[:, q, :], p.sp("k_k")[:, q:q + 1], None, ALU.mult).then_inc(dve.step(), 1)
    dve.e.wait_ge(dve.steps, dve.n)
    e_.tensor_tensor(p.kd, p.kk, p.kk, ALU.mult).then_inc(dve.event("squares"), 1)
    for j in range(2):
        dve.e.wait_ge(p.dve_tiles.full, p.dve_tiles.turn(dve))
        bank = shaped(p.dve_tiles.take(dve), 2, S)
        e_.tensor_scalar(p.kd[:, 2 * j:2 * j + 2, :], bank, 1e-24, None, ALU.max).then_inc(p.dve_tiles.drained, 1)
    dve.e.wait_ge(p.dve_tiles.drained, p.dve_tiles.taken["dve"])
    e_.tensor_scalar(p.small[:, 255:256], p.c("eps"), 1.0, None, ALU.mult).then_inc(dve.event("norms_in"), 1)
    dve.e.wait_ge(p.act_tiles.drained, p.mark["w0"])
    for e in range(2):
        for q in range(PAIRS):
            o, s = p.dec[:, e, q, :], p.sig[:, e, q, :]
            if e:
                o, s = o[:, ::-1], s[:, ::-1]
            e_.tensor_tensor_scan(o, p.c("scan_keep"), s, 0.0, ALU.mult, ALU.add).then_inc(dve.step(), 1)
    dve.e.wait_ge(dve.steps, dve.n)
    e_.tensor_tensor(flat(p.sig), flat(p.dec), flat(p.sig), ALU.subtract).then_inc(dve.event("sums_ready"), 1)
    dve.e.wait_ge(p.sem("norms_out"), 1)
    e_.tensor_tensor(p.kk, p.kk, p.kd, ALU.mult).then_inc(dve.step(), 1)
    dve.e.wait_ge(p.act_tiles.drained, p.mark["a0"])
    one_less = p.cols[:, 15:19]
    e_.tensor_scalar(one_less, p.sp("k_a"), -1.0, 1.0, ALU.mult, ALU.add).then_inc(dve.step(), 1)
    dve.e.wait_ge(dve.steps, dve.n)
    dve.e.wait_ge(p.sem("decays_ready"), 1)
    gt = shaped(p.gt, 2, 4, NCH)
    for e in range(2):
        g = p.dec[:, e].rearrange("p q (c t) -> p q c t", t=CH)
        e_.tensor_copy(gt[:, e], g[:, :, :, CH - 1] if e == 0 else g[:, :, ::-1, 0]).then_inc(dve.step(), 1)
    dve.e.wait_ge(dve.steps, dve.n)
    for e in range(2):
        for q in range(PAIRS):
            e_.tensor_scalar(p.kd[:, q, :], p.iclr[:, e, q, :], p.sp("k_a")[:, q:q + 1],
                                     one_less[:, q:q + 1], ALU.mult, ALU.add).then_inc(dve.step(), 1)
        dve.e.wait_ge(dve.steps, dve.n)
        e_.tensor_tensor(p.kd, p.kd, k, ALU.mult).then_inc(dve.step(), 1)
        e_.tensor_tensor(p.iclr[:, e], p.iclr[:, e], p.kk, ALU.mult).then_inc(dve.step(), 1)
        e_.tensor_tensor(p.sig[:, e], p.sig[:, e], p.kk, ALU.mult).then_inc(dve.step(), 1)
        e_.tensor_tensor(p.dec[:, e], p.dec[:, e], r, ALU.mult).then_inc(dve.step(), 1)
        dve.e.wait_ge(dve.steps, dve.n)
        e_.tensor_tensor(p.iclr[:, e], p.iclr[:, e], p.inv_dec[:, e], ALU.mult).then_inc(dve.step(), 1)
        dve.e.wait_ge(dve.steps, dve.n)
        e_.tensor_tensor(p.inv_dec[:, e], p.inv_dec[:, e], p.kd, ALU.mult).then_inc(dve.step(), 1)
        if e == 0:
            e_.tensor_copy(p.ksum, p.kd).then_inc(dve.step(), 1)
        else:
            e_.tensor_tensor(p.ksum, p.ksum, p.kd, ALU.add).then_inc(dve.step(), 1)
        dve.e.wait_ge(dve.steps, dve.n)
    for q in range(PAIRS):
        ins = e_.scalar_tensor_tensor(p.kd[:, q, :], p.ksum[:, q, :], p.sp("r_k")[:, q:q + 1], r[:, q, :],
                                      ALU.mult, ALU.mult)
        if q == 3:
            ins.then_inc(dve.event("bonus_in"), 1)
        else:
            ins.then_inc(dve.step(), 1)
    for j in range(2):
        dve.e.wait_ge(p.dve_tiles.full, p.dve_tiles.turn(dve))
        bank = shaped(p.dve_tiles.take(dve), 2, S)
        sl = slice(2 * j, 2 * j + 2)
        e_.tensor_tensor(p.ksum[:, sl, :], bank, v[:, sl, :], ALU.mult).then_inc(p.dve_tiles.drained, 1)
    e_.memset(p.ST, 0.0).then_inc(dve.event("state_ready"), 1)
    dve.e.wait_ge(p.sem("state_ready"), 1)
    e_.tensor_copy(p.small[:, 255:256], p.c("eps")).then_inc(dve.event("recurrence_in"), 1)
    by_dir = lambda ap: ap.rearrange("p (e q) t -> p e q t", e=2)
    eye8 = spread(p.c("eye64"), 1, 8)
    for j in range(2):
        dve.e.wait_ge(p.sem(f"gate_stored_{j}"), 16 * 6)
    causal = p.c("causal", 2, 2, CH)
    levels = p.c("level", 6, 2, CH)
    for m in range(NCH // 2):
        for i in range(2):
            for e in range(2):
                for dst in (p.BETA[i], p.KAPPA[i]):
                    dve.e.wait_ge(p.dve_tiles.full, p.dve_tiles.turn(dve))
                    bank = shaped(p.dve_tiles.take(dve), 4, 2, CH)
                    e_.tensor_tensor(dst[:, 4 * e:4 * e + 4], bank, spread(causal[:, e], 1, 4), ALU.mult).then_inc(
                        p.dve_tiles.drained, 1)
            dve.e.wait_ge(p.dve_tiles.drained, p.dve_tiles.taken["dve"])
            e_.tensor_tensor(by_dir(p.Pb[i]), by_dir(p.BETA[i][:, :, 0, :]), spread(levels[:, 0], 2, 4), ALU.mult).then_inc(
                dve.event("level_masked"), 1)
        for n in range(6):
            for i in range(2):
                if n < 5:
                    dve.e.wait_ge(p.dve_tiles.full, p.dve_tiles.turn(dve))
                    bank = shaped(p.dve_tiles.take(dve), 8, CH)
                    e_.tensor_tensor(p.X[i], p.X[i] if n else eye8, bank, ALU.subtract).then_inc(p.dve_tiles.drained, 1)
                if n == 0:
                    dve.e.wait_ge(p.sem("level_masked"), 12 * m + i + 1)
                    e_.tensor_tensor(p.XT[i], eye8, p.Pb[i], ALU.subtract).then_inc(dve.step(), 1)
                    dve.e.wait_ge(dve.steps, dve.n)
                else:
                    dve.e.wait_ge(p.dve_tiles.full, p.dve_tiles.turn(dve))
                    bank = shaped(p.dve_tiles.take(dve), 8, CH)
                    e_.tensor_tensor(p.XT[i], p.XT[i], bank, ALU.subtract).then_inc(p.dve_tiles.drained, 1)
                if n < 5:
                    e_.tensor_tensor(by_dir(p.Pb[i]), by_dir(p.BETA[i][:, :, 0, :]), spread(levels[:, n + 1], 2, 4),
                                     ALU.mult).then_inc(dve.event("level_masked"), 1)
        for i in range(2):
            c = 2 * m + i
            dve.e.wait_ge(p.dve_tiles.full, p.dve_tiles.turn(dve))
            bank = shaped(p.dve_tiles.take(dve), 8, CH)
            dve.e.wait_ge(p.act_tiles.drained, p.mark[f"y{c}"])
            e_.tensor_tensor(p.ST, p.ST, bank, ALU.add).then_inc(p.dve_tiles.drained, 1)
            dve.e.wait_ge(p.dve_tiles.drained, p.dve_tiles.taken["dve"])
            whole = shaped(p.gt, 8, NCH)[:, :, c:c + 1].to_broadcast([P, 8, CH])
            e_.tensor_tensor(p.ST, p.ST, whole, ALU.mult).then_inc(dve.event("state_ready"), 1)
            dve.e.wait_ge(p.sem("state_ready"), c + 2)
    e_.tensor_tensor(p.kd, p.kd, p.kk, ALU.add).then_inc(dve.event("y_sum"), 1)
    dve.e.wait_ge(p.sem("y_sum"), 1)
    for j in range(2):
        dve.e.wait_ge(p.dve_tiles.full, p.dve_tiles.turn(dve))
        bank = shaped(p.dve_tiles.take(dve), 2, S)
        sl = slice(2 * j, 2 * j + 2)
        e_.scalar_tensor_tensor(p.kd[:, sl, :], bank, -1.0 / 64, p.kd[:, sl, :],
                                                       ALU.mult, ALU.add).then_inc(p.dve_tiles.drained, 1)
    dve.e.wait_ge(p.dve_tiles.drained, p.dve_tiles.taken["dve"])
    e_.tensor_tensor(p.kk, p.kd, p.kd, ALU.mult).then_inc(dve.event("y_sum"), 1)
    for j in range(2):
        dve.e.wait_ge(p.dve_tiles.full, p.dve_tiles.turn(dve))
        bank = shaped(p.dve_tiles.take(dve), 2, S)
        e_.tensor_copy(p.kk[:, 2 * j:2 * j + 2, :], bank).then_inc(p.dve_tiles.drained, 1)
    dve.e.wait_ge(p.dve_tiles.drained, p.dve_tiles.taken["dve"])
    e_.tensor_copy(p.small[:, 255:256], p.c("eps")).then_inc(dve.event("variances_in"), 1)
    dve.e.wait_ge(p.sem("y_rstd"), 1)
    e_.tensor_tensor(p.kd, p.kd, p.kk, ALU.mult).then_inc(dve.step(), 1)
    dve.e.wait_ge(dve.steps, dve.n)
    for q in range(PAIRS):
        e_.tensor_scalar(p.kd[:, q, :], p.kd[:, q, :], p.sp("ln_w")[:, q:q + 1], p.sp("ln_b")[:, q:q + 1],
                                 ALU.mult, ALU.add).then_inc(dve.step(), 1)
    dve.e.wait_ge(dve.steps, dve.n)
    e_.tensor_tensor(p.kd, p.kd, p.ksum, ALU.add).then_inc(dve.step(), 1)
    dve.e.wait_ge(dve.steps, dve.n)
    e_.tensor_tensor(p.ksum, p.kd, p.gate, ALU.mult).then_inc(dve.event("y_rwkv"), 1)
    for i in range(12):
        if i % 4 == 0:
            dve.e.wait_ge(p.sem("gates_ready"), i // 4 + 1)
        dve.e.wait_ge(p.dve_tiles.full, p.dve_tiles.turn(dve))
        bank = shaped(p.dve_tiles.take(dve), 2, S)
        d = slice(2 * (i % 4), 2 * (i % 4) + 2)
        gates = p.gates[:, 2 * i:2 * i + 2, :]
        if i < 4:
            e_.tensor_tensor(p.merged[:, d, :], bank, gates, ALU.mult).then_inc(p.dve_tiles.drained, 1)
        else:
            e_.tensor_tensor(p.prod, bank, gates, ALU.mult).then_inc(p.dve_tiles.drained, 1)
            dve.e.wait_ge(p.dve_tiles.drained, p.dve_tiles.taken["dve"])
            ins = e_.tensor_tensor(p.merged[:, d, :], p.merged[:, d, :], p.prod, ALU.add)
            if i == 11:
                ins.then_inc(dve.event("merged"), 1)
            else:
                ins.then_inc(dve.step(), 1)
                dve.e.wait_ge(dve.steps, dve.n)
    for half in range(2):
        for b in range(NB):
            dve.e.wait_ge(p.dve_tiles.full, p.dve_tiles.turn(dve))
            bank = p.dve_tiles.take(dve)
            x = p.x[:, b, half * 512:(half + 1) * 512]
            e_.tensor_tensor(x, x, bank, ALU.add).then_inc(p.dve_tiles.drained, 1)
    dve.e.wait_ge(p.dve_tiles.drained, p.dve_tiles.taken["dve"])
    e_.tensor_copy(p.small[:, 255:256], p.c("eps")).then_inc(dve.event("mixed"), 1)
    norm_rows(p, dve, p.x, p.rstd2, p.hrow, D, "rstd", 2)
    rows_to_columns_evac(p, dve, p.hT, p.sp("g_ffn"), KC, False)
    dve.e.wait_ge(p.dve_tiles.full, p.dve_tiles.turn(dve))
    bank = shaped(p.dve_tiles.take(dve)[:, 0:NB * E_N], NB, E_N)
    e_.tensor_copy(p.aff, bank).then_inc(p.dve_tiles.drained, 1)
    dve.e.wait_ge(p.dve_tiles.drained, p.dve_tiles.taken["dve"])
    e_.tensor_reduce(p.cols[:, 0:2], p.aff, AX, ALU.max).then_inc(dve.step(), 1)
    dve.e.wait_ge(dve.steps, dve.n)
    e_.tensor_scalar(p.cols[:, 2:4], p.cols[:, 0:2], -1.0, None, ALU.mult).then_inc(dve.event("logits"), 1)
    dve.e.wait_ge(p.sem("affinity_exps"), 1)
    e_.reciprocal(p.cols[:, 6:8], p.cols[:, 4:6]).then_inc(dve.step(), 1)
    dve.e.wait_ge(dve.steps, dve.n)
    e_.tensor_tensor(p.aff, p.aff, p.cols[:, 6:8].unsqueeze(2).to_broadcast([P, NB, E_N]), ALU.mult).then_inc(dve.event("affinities"), 1)
    e_.memset(p.ones[0:E_N, :], 1.0).then_inc(dve.step(), 1)
    dve.e.wait_ge(p.dve_tiles.full, p.dve_tiles.turn(dve))
    bank = p.dve_tiles.take(dve)
    e_.tensor_copy(p.affT[0:E_N, :], bank[0:E_N, 0:S]).then_inc(p.dve_tiles.drained, 1)
    dve.e.wait_ge(p.dve_tiles.drained, p.dve_tiles.taken["dve"])
    for _ in range(CAP // 8):
        e_.max(p.top[0:E_N, :], p.affT[0:E_N, :]).then_inc(dve.step(), 1)
        dve.e.wait_ge(dve.steps, dve.n)
        e_.match_replace(p.affT[0:E_N, :], p.top[0:E_N, :], p.affT[0:E_N, :], -1.0).then_inc(dve.step(), 1)
        dve.e.wait_ge(dve.steps, dve.n)
    e_.tensor_scalar(p.mask[0:E_N, :], p.affT[0:E_N, :], 0.0, None, ALU.is_lt).then_inc(dve.step(), 1)
    dve.e.wait_ge(dve.steps, dve.n)
    e_.tensor_tensor_scan(p.cum[0:E_N, :], p.ones[0:E_N, :], p.mask[0:E_N, :], 0.0, ALU.mult, ALU.add).then_inc(dve.step(), 1)
    dve.e.wait_ge(dve.steps, dve.n)
    e_.tensor_tensor(p.cum[0:E_N, :], p.cum[0:E_N, :], p.mask[0:E_N, :], ALU.mult).then_inc(dve.step(), 1)
    dve.e.wait_ge(dve.steps, dve.n)
    e_.tensor_scalar(p.cum[0:E_N, :], p.cum[0:E_N, :], 1.0, None, ALU.subtract).then_inc(dve.event("slots"), 1)
    dve.e.wait_ge(p.dve_tiles.full, p.dve_tiles.turn(dve))
    bank = shaped(p.dve_tiles.take(dve)[:, 0:NB * E_N], NB, E_N)
    e_.tensor_copy(p.posT, bank).then_inc(p.dve_tiles.drained, 1)
    dve.e.wait_ge(p.dve_tiles.drained, p.dve_tiles.taken["dve"])
    for b in range(NB):
        s3 = p.sel[:, b, :].rearrange("p (e c) -> p e c", c=CAP)
        e_.tensor_tensor(s3, spread(p.c("iota"), 1, E_N), p.posT[:, b, :].unsqueeze(2).to_broadcast([P, E_N, CAP]),
                                ALU.is_equal).then_inc(dve.step(), 1)
        dve.e.wait_ge(dve.steps, dve.n)
        e_.tensor_tensor(p.selw[:, b, :].rearrange("p (e c) -> p e c", c=CAP), s3,
                                p.aff[:, b, :].unsqueeze(2).to_broadcast([P, E_N, CAP]), ALU.mult).then_inc(dve.step(), 1)
        dve.e.wait_ge(dve.steps, dve.n)
    dve.finish("second", 0)
    p.reset_rings("dve")
    with dve.e.Fori(0, G_N) as g:
        experts_dve(p, dve, g)
        dve.finish("experts", g)
        p.reset_rings("dve")
    dve.e.wait_ge(p.sem("final_rstd"), 1)
    for b in range(NB):
        ins = e_.scalar_tensor_tensor(p.x[:, b, :], p.x[:, b, :], p.rstd2[:, b:b + 1], p.sp("g_final"),
                                      ALU.mult, ALU.mult)
        ins.then_inc(dve.event("y_final"), 1)


def second_pool(p, pool):
    pool.e.wait_ge(p.act_tiles.drained, p.mark["raw"])
    e_ = pool.e
    m0 = p.cols[:, 0:15]
    e_.tensor_tensor(m0, p.sp("mu_prev"), p.sp("mu_next"), ALU.add).then_inc(pool.step(), 1)
    pool.e.wait_ge(pool.steps, pool.n)
    e_.tensor_scalar(m0, m0, -1.0, 1.0, ALU.mult, ALU.add).then_inc(pool.step(), 1)
    pool.e.wait_ge(pool.steps, pool.n)
    raw, out = p.raw[:, 0:15, :], p.shifted
    near = p.zp_wide
    for shift, gain in ((0, m0), (1, p.sp("mu_prev")), (-1, p.sp("mu_next"))):
        dst, src = slice(max(shift, 0), S + min(shift, 0)), slice(max(-shift, 0), S + min(-shift, 0))
        g = gain.unsqueeze(2).to_broadcast([P, 15, S - abs(shift)])
        if shift == 0:
            e_.tensor_tensor(out, raw, g, ALU.mult).then_inc(pool.step(), 1)
            pool.e.wait_ge(pool.steps, pool.n)
            continue
        for c0, c1 in ((0, 8), (8, 15)):
            part = near[:, 0:c1 - c0, 0:S - 1]
            e_.tensor_tensor(part, raw[:, c0:c1, src], g[:, c0:c1], ALU.mult).then_inc(pool.step(), 1)
            pool.e.wait_ge(pool.steps, pool.n)
            ins = e_.tensor_tensor(out[:, c0:c1, dst], out[:, c0:c1, dst], part, ALU.add)
            if shift < 0 and c1 == 15:
                ins.then_inc(pool.event("shift_done"), 1)
            else:
                ins.then_inc(pool.step(), 1)
                pool.e.wait_ge(pool.steps, pool.n)
    z, a, b = p.raw[:, 15:19, :], p.zp[0], p.zp[1]
    pool.e.wait_ge(p.sem("shift_done"), 1)
    e_.memset(flat(a), 0.0).then_inc(pool.step(), 1)
    pool.e.wait_ge(pool.steps, pool.n)
    e_.memset(flat(b), 0.0).then_inc(pool.step(), 1)
    pool.e.wait_ge(pool.steps, pool.n)
    e_.tensor_copy(a[:, :, 8:8 + S], z).then_inc(pool.step(), 1)
    pool.e.wait_ge(pool.steps, pool.n)
    src, dst = a, b
    for n in range(4):
        w = 1 << n
        e_.tensor_tensor(dst[:, n:4, 0:272 - w], src[:, n:4, 0:272 - w], src[:, n:4, w:272], ALU.add).then_inc(pool.step(), 1)
        pool.e.wait_ge(pool.steps, pool.n)
        lo = 8 - w
        e_.tensor_tensor(p.pooled[:, n, :], dst[:, n, lo:lo + S], p.c("pool_cnt", 4, S)[:, n, :], ALU.mult).then_inc(pool.step(), 1)
        pool.e.wait_ge(pool.steps, pool.n)
        src, dst = dst, src
    e_.tensor_tensor(p.pooled, p.pooled, z, ALU.subtract).then_inc(pool.event("pooled"), 1)
    pool.finish("second", 0)
    with pool.e.Fori(0, G_N) as g:
        pool.finish("experts", g)


def build(nc, stream, x, mem, pos_row, pos_col, const, layer_par, second_par, out):
    from contextlib import ExitStack
    with ExitStack() as ctx:
        p = Program(nc, ctx, None)
        first_buffers(p)
        p.pos = p.sb("positions", 258, I32)
        p.gate_dram = nc.dram_tensor("gate_dram", (12, P, 512), F32, kind="Internal").ap()
        loads = ["const_loaded", "mem_loaded", "x_loaded", "positions_loaded", "layer_params", "second_params"]
        for name in loads + ["pe_steps", "act_steps", "dve_steps", "pool_steps", "layer_met", "start_met",
                             "second_met", "experts_met", "y_final", "stored", "passed"]:
            p.sem(name)
        block = ctx.enter_context(nc.Block())

        def reset(eng):
            p.reset_rings(eng.name)

        @block.tensor
        def _(e):
            pe = Engine(p, e, "pe")
            w = Weights(p, pe)
            prologue_pe(p, pe, w)
            pe.finish("start", 0)
            reset(pe)
            with e.Fori(0, DEPTH) as l:
                w.start(l * (16 * LAYER_UNITS // SLOTS), p.slots, p.slot_loaded, p.slots_free)
                layer_pe(p, pe, w)
                pe.finish("layer", l)
                reset(pe)
            second_buffers(p)
            second_pe(p, pe, w)

        @block.scalar
        def _(e):
            first_buffers(p)
            act = Engine(p, e, "act")
            act.e.dma_start(p.const[:, :], const).then_inc(p.sem("const_loaded"), 16)
            act.e.dma_start(p.x, x.rearrange("(b p) d -> p b d", p=P)).then_inc(p.sem("x_loaded"), 16)
            prologue_act(p, act)
            act.e.wait_ge(p.sem("x_loaded"), 16)
            act.finish("start", 0)
            reset(act)
            with e.Fori(0, DEPTH) as l:
                act.mine.add("layer_params")
                e.dma_start(p.par[:, 0:LAYER_W], layer_par[bass.ds(l * P, P), :]).then_inc(
                    p.sem("layer_params"), 16)
                layer_act(p, act)
                act.finish("layer", l)
                reset(act)
            second_buffers(p)
            e.dma_start(p.par[:, 0:SECOND_W], second_par).then_inc(p.sem("second_params"), 16)
            e.wait_ge(p.sem("second_params"), 16)
            second_act(p, act)

        @block.vector
        def _(e):
            first_buffers(p)
            dve = Engine(p, e, "dve")
            prologue_dve(p, dve)
            dve.finish("start", 0)
            reset(dve)
            with e.Fori(0, DEPTH) as l:
                layer_dve(p, dve)
                dve.finish("layer", l)
                reset(dve)
            second_buffers(p)
            second_dve(p, dve)

        @block.gpsimd
        def _(e):
            first_buffers(p)
            pool = Engine(p, e, "pool")
            e.dma_start(p.xv, mem.rearrange("(b p) d -> p b d", p=P)).then_inc(p.sem("mem_loaded"), 16)
            e.dma_start(p.pos[:, 0:256], pos_row).then_inc(p.sem("positions_loaded"), 16)
            e.dma_start(p.pos[:, 256:258], pos_col).then_inc(p.sem("positions_loaded"), 16)
            pool.finish("start", 0)
            with e.Fori(0, DEPTH) as l:
                layer_pool(p, pool)
                pool.finish("layer", l)
            second_buffers(p)
            second_pool(p, pool)

        @block.sync
        def _(e):
            e.sem_inc(p.slots_free, SLOTS)
            with e.Fori(0, DENSE_UNITS // SLOTS) as r:
                for s in range(SLOTS):
                    e.wait_ge(p.slots_free, r * SLOTS + (s + 1))
                    e.dma_start(p.slots[s], stream[bass.ds((r * SLOTS + s) * P, P), :]).then_inc(
                        p.slot_loaded[s], 16)
            for s in range(EXPERT_SLOTS):
                if s < SLOTS:
                    e.wait_ge(p.slots_free, DENSE_UNITS + s + 1)
                elif s == SLOTS:
                    e.wait_ge(p.sem("second_met"), 8)
                e.dma_start(p.expert_slots[s], stream[(DENSE_UNITS + s) * P:(DENSE_UNITS + s + 1) * P, :]).then_inc(
                    p.expert_slot_loaded[s], 16)
            with e.Fori(0, EXPERT_UNITS // EXPERT_SLOTS - 1) as r:
                for s in range(EXPERT_SLOTS):
                    e.wait_ge(p.expert_slots_used, r * EXPERT_SLOTS + (s + 1))
                    e.dma_start(p.expert_slots[s], stream[bass.ds(
                        (r * EXPERT_SLOTS + (DENSE_UNITS + EXPERT_SLOTS + s)) * P, P), :]).then_inc(
                            p.expert_slot_loaded[s], 16)
            e.wait_ge(p.sem("y_final"), NB)
            e.dma_start(out.rearrange("(b p) d -> p b d", p=P), p.x).then_inc(p.sem("stored"), 16)
            e.wait_ge(p.sem("stored"), 16)



def packed(spec, width, values):
    out = np.zeros((P, width), np.float32)
    for name, (a, b) in spec.items():
        v = np.asarray(values[name], np.float32)
        out[:, a:b] = v.reshape(v.shape[0], b - a) if v.shape[0] == P else np.broadcast_to(v.reshape(1, b - a), (P, b - a))
    return out


def by_chunk(v):
    return np.ascontiguousarray(np.asarray(v).reshape(-1, P).T)


def unit(a):
    out = np.zeros((P, UNIT), np.float32)
    a = a.reshape(P, -1)
    out[:, 0:a.shape[1]] = a
    return out


def column_units(w):
    K, n = w.shape
    u = w.reshape(K // P, P, n).transpose(1, 0, 2)
    return [unit(np.concatenate([u[:, :, c:c + P].reshape(P, -1) for c in range(a, min(a + 256, n), P)], axis=1))
            for a in range(0, n, 256)]


def row_units(w, width, split=2):
    K, n = w.shape
    u = w.reshape(K // P, P, n).transpose(1, 0, 2)
    kn = K // P // split
    return [unit(u[:, h * kn:(h + 1) * kn, a:a + width]) for a in range(0, n, width) for h in range(split)]


def constants():
    t = np.arange(P)
    s64 = t % 64
    f = np.arange(64)
    c = {"ident": np.eye(P), "inv": 10000.0 ** (-np.arange(16) / np.float32(16))}
    q = (np.arange(NB)[None, :] * P + t[:, None])[:, :, None]
    c["swa_far"] = np.where(np.abs(q - np.arange(S)) <= 128, 0.0, FAR)
    c["headsum"] = (t[:, None] // 64 == t[None, :] // 64)
    c["eye64"] = s64[:, None] == f
    before = [s64[:, None] < f, s64[:, None] > f]
    upto = [s64[:, None] <= f, s64[:, None] >= f]
    c["causal"] = np.stack([np.stack([before[e], upto[e]], 1) for e in range(2)], 1)
    level = []
    for n in range(6):
        b = 1 << n
        cross = (s64[:, None] // (2 * b) == f // (2 * b)) & (s64[:, None] // b != f // b)
        level.append(np.stack([cross & m for m in before], 1))
    c["level"] = np.stack(level, 1)
    c["scan_keep"] = (np.arange(S) % CH != 0)
    tok = np.arange(S)
    freqs = (np.float32(10000.0) ** (-np.arange(0, 32, 2, dtype=np.float32) / np.float32(32))).astype(np.float32)
    ang = np.concatenate([(tok // 64).astype(np.float32)[:, None] * freqs,
                          (tok % 64).astype(np.float32)[:, None] * freqs], axis=1)
    c["cos"] = np.cos(ang).reshape(NB, P, 32).transpose(1, 0, 2)
    c["sin"] = np.sin(ang).reshape(NB, P, 32).transpose(1, 0, 2)
    cnt = []
    for w in (2, 4, 8, 16):
        lo = w // 2
        hi = w - lo - 1
        cnt.append(1.0 / (np.clip(tok + hi + 1, 0, S) - np.clip(tok - lo, 0, S)))
    c["pool_cnt"] = np.stack(cnt).reshape(1, -1)
    c["iota"] = np.arange(32)
    c["eps"], c["ln_eps"], c["half_pi"] = [EPS], [LN_EPS], [math.pi / 2]
    out = {}
    for k, v in c.items():
        v = np.asarray(v, np.float32)
        out[k] = v if v.shape[0] == P else v.reshape(1, -1)
    return packed(CONST, CONST_W, out)


SWA_ORDER = [h for j in range(4) for h in (j, j + 4)]


def heads(order, size=64, start=0):
    return np.concatenate([start + np.arange(h * size, (h + 1) * size) for h in order])


def layer_arrays(i, l):
    w = i["w_in"][l]
    off = np.cumsum([0, 256, 256, 256, 256, 128, 32, 512, 128, 128])
    aq, ak, av, bq, bkv, bkr, cq, ck, cv = [w[:, off[j]:off[j + 1]] for j in range(9)]
    units = row_units(np.concatenate([bq, bkv, bkr], 1), 416)
    units += row_units(np.concatenate([av, cv], 1), 384)
    units += column_units(np.concatenate([aq, ak, cq[:, heads(SWA_ORDER)], ck], 1))
    units += column_units(i["w_xkv"][l][:, 0:D]) + row_units(i["w_xkv"][l][:, D:], 512)
    wo = i["w_out"][l]
    units += row_units(np.concatenate([wo[0:512], wo[512:][heads(SWA_ORDER)]], 0), 512)
    units += column_units(i["w_xq"][l]) + row_units(i["w_xo"][l], 512)
    wf, wd = i["w_ffn_in"][l], i["w_ffn_out"][l]
    gu = [column_units(np.concatenate([wf[:, f * P:(f + 1) * P], wf[:, FF + f * P:FF + (f + 1) * P]], 1))[0]
          for f in range(FC)]
    down = [unit(wd[j * 256:(j + 1) * 256].reshape(2, P, D).transpose(1, 0, 2)) for j in range(FC // 2)]
    for j in range(FC // 2):
        units += gu[2 * j:2 * j + 2]
        if j:
            units.append(down[j - 1])
    units.append(down[-1])
    units += [np.zeros((P, UNIT), np.float32)] * (LAYER_UNITS - len(units))
    init = 0.8 - 0.6 * math.exp(-0.3 * l)
    par = packed(LAYER, LAYER_W, {
        "g_mix_pre": by_chunk(i["g_mix_pre"][l]), "g_x_pre": by_chunk(i["g_x_pre"][l]),
        "g_x_mem": by_chunk(i["g_x_mem"][l]), "g_ffn_pre": by_chunk(i["g_ffn_pre"][l]),
        "g_q": by_chunk(i["mla_q_norm_g"][l]), "g_kv": by_chunk(i["mla_kv_norm_g"][l]),
        "g_diff": np.concatenate([i["diff_head_g"][l]] * 2).reshape(P, 1), "sinks": i["swa_sinks"][l].reshape(1, -1),
        "lambda": i["diff_lambda"][l].reshape(1, -1), "lam_init": np.array([init]), "lam_rest": np.array([1 - init]),
        "kv_up": i["mla_w_kv_up"][l], "q_up": i["mla_w_q_up"][l].reshape(2, P, 384).transpose(1, 0, 2),
        "g_mix_post": i["g_mix_post"][l].reshape(1, -1), "g_x_post": i["g_x_post"][l].reshape(1, -1),
        "g_ffn_post": i["g_ffn_post"][l].reshape(1, -1),
    })
    return units, par


def second_arrays(i):
    w = i["w_in_2"][0]
    rw, pool, att, gate = np.split(w, [1920, 2432, 3200], axis=1)
    att = np.concatenate([att[:, heads(SWA_ORDER)], att[:, 512:]], 1)
    units = row_units(att, 256, 1) + column_units(np.concatenate([rw, pool], 1)) + column_units(gate)
    for b in ("rwkv", "pool", "attn"):
        wb = i[f"w_branch_{b}_2"][0]
        if b == "attn":
            wb = wb[heads(SWA_ORDER)]
        u = wb.reshape(4, P, D).transpose(1, 0, 2)
        units += [unit(np.concatenate([u[:, :, c:c + P].reshape(P, -1) for c in range(a, a + 512, P)], 1))
                  for a in range(0, D, 512)]
    units += row_units(i["w_out_2"][0], 512)
    units += [np.zeros((P, UNIT), np.float32)] * (BLOCK2_UNITS - len(units))
    for g in range(G_N):
        def experts(w, f):
            return [unit(w[g * GE + e].reshape(KC, P, D)[4 * h:4 * h + 4, :, f * 512:(f + 1) * 512].transpose(1, 0, 2))
                    for h in range(2) for e in range(GE)]
        for f in range(2):
            units += experts(i["exp_gate_2"][0], f) + experts(i["exp_up_2"][0], f)
        for f in range(2):
            units += experts(i["exp_down_2"][0], f)
    col = lambda n: by_chunk(i[n + "_2"][0])
    both = lambda n: np.concatenate([by_chunk(i[n + "_2"][0, e]) for e in range(2)], 1)
    row = lambda n: i[n + "_2"][0].reshape(1, -1)
    par = packed(SECOND, SECOND_W, {
        "g_mix": col("norm_mix"), "mu_prev": col("shift_prev"), "mu_next": col("shift_next"),
        "w0": both("rwkv_w0"), "a0": both("rwkv_a0"), "k_k": col("rwkv_k_k"), "k_a": col("rwkv_k_a"),
        "r_k": col("rwkv_r_k"), "ln_w": col("rwkv_ln_w"), "ln_b": col("rwkv_ln_b"), "pool_scale": col("pool_scale"),
        "g_ffn": col("norm_ffn"), "q_norm": row("q_norm"), "k_norm": row("k_norm"),
        "router": i["router_2"][0].reshape(KC, P, E_N).transpose(1, 0, 2),
        "w2": i["rwkv_w2_2"][0].reshape(P, 512), "a2": i["rwkv_a2_2"][0].reshape(P, 512),
        "g2": i["rwkv_g2_2"][0], "pool_w": i["pool_w_2"][0].transpose(1, 0, 2),
        "g_final": i["norm_final_2"].reshape(1, -1),
    })
    return units, par


def kernel(**inputs):
    import concourse.bacc as bacc
    from concourse.bass_utils import run_bass_kernel_spmd

    i = {k: np.asarray(v) for k, v in inputs.items()}
    units, pars = [], []
    for l in range(DEPTH):
        u, par = layer_arrays(i, l)
        units += u
        pars.append(par)
    u2, second = second_arrays(i)
    units += u2
    pos = i["positions"].reshape(-1)
    arrays = {
        "stream": np.concatenate(units, 0), "x": i["x"].reshape(S, D), "mem": i["mem"].reshape(S, D),
        "pos_row": np.ascontiguousarray(np.broadcast_to(pos[None, :], (P, S))),
        "pos_col": np.ascontiguousarray(pos.reshape(NB, P).T),
        "const": constants(), "layer_par": np.concatenate(pars, 0), "second_par": second,
    }
    nc = bacc.Bacc("TRN2", target_bir_lowering=False, num_devices=1)
    aps = [nc.dram_tensor("in_" + k, a.shape, mybir.dt.from_np(a.dtype), kind="ExternalInput").ap() for k, a in arrays.items()]
    out = nc.dram_tensor("out", (S, D), F32, kind="ExternalOutput").ap()
    build(nc, *aps, out)
    r = run_bass_kernel_spmd(nc, [{"in_" + k: a for k, a in arrays.items()}], core_ids=[0])
    return r.results[0]["out"].reshape(1, S, D)
```

```python
import math

import numpy as np
import concourse.bass as bass
from concourse import mybir

F32 = mybir.dt.float32
I32 = mybir.dt.int32
ALU = mybir.AluOpType
ACT = mybir.ActivationFunctionType
AX = mybir.AxisListType.X

P = 128
S = 256
NB = S // P
D = 1024
KC = D // P
DEPTH = 2
FF = 2816
FC = FF // P
UNIT = 2048
SLOTS = 8
EXPERT_SLOTS = 12
E_N = 16
CAP = 32
G_N = 4
GE = E_N // G_N
EF = 1024
HEADS2 = 8
PAIRS = 4
CH = 64
NCH = S // CH
EPS = 1e-6
LN_EPS = 64e-5
FAR = 1e30
LAYER_UNITS = 64
BLOCK2_UNITS = 35
GROUP_UNITS = 48
DENSE_UNITS = DEPTH * LAYER_UNITS + BLOCK2_UNITS
EXPERT_UNITS = G_N * GROUP_UNITS
DECAY = math.exp(-0.5)
SLOPES = [2.0 ** (-8.0 * (i + 1) / 12) for i in range(12)]


def columns(*parts):
    at, out = 0, {}
    for name, width in parts:
        out[name] = (at, at + width)
        at += width
    return out, at


CONST, CONST_W = columns(
    ("ident", 128), ("inv", 16), ("swa_far", 512), ("headsum", 128), ("eye64", 64),
    ("causal", 256), ("level", 6 * 128), ("scan_keep", 256),
    ("cos", 64), ("sin", 64), ("pool_cnt", 1024), ("iota", 32), ("eps", 1), ("ln_eps", 1), ("half_pi", 1),
)
LAYER, LAYER_W = columns(
    ("g_mix_pre", 8), ("g_x_pre", 8), ("g_x_mem", 8), ("g_q", 2), ("g_kv", 1),
    ("g_diff", 1), ("sinks", 8), ("lambda", 128), ("lam_init", 1), ("lam_rest", 1), ("kv_up", 512),
    ("q_up", 768), ("g_mix_post", 1024), ("g_x_post", 1024),
    ("g_ffn_pre", 8), ("g_ffn_post", 1024),
)
EARLY_W = LAYER["g_ffn_pre"][0]
SECOND, SECOND_W = columns(
    ("g_mix", 8), ("mu_prev", 15), ("mu_next", 15), ("w0", 8), ("a0", 8), ("k_k", 4), ("k_a", 4),
    ("r_k", 4), ("ln_w", 4), ("ln_b", 4), ("pool_scale", 4), ("g_ffn", 8), ("q_norm", 64),
    ("k_norm", 64), ("router", 128), ("w2", 512), ("a2", 512), ("g2", 512), ("pool_w", 512),
    ("g_final", 1024),
)
assert SECOND_W <= EARLY_W
BRANCH_ORDER = (1, 2, 0)
BY_HALF = [(0, 0), (0, 1), (1, 0), (1, 1)]
BY_BLOCK = [(0, 0), (1, 0), (0, 1), (1, 1)]


class Engine:

    def __init__(self, prog, eng, name):
        self.prog, self.e, self.name = prog, eng, name
        self.steps = prog.sem(f"{name}_steps")
        self.n = 0
        self.mine = {f"{name}_steps"}

    def step(self):
        self.n += 1
        return self.steps

    def event(self, event):
        self.mine.add(event)
        return self.prog.sem(event)

    def finish(self, scope, turn):
        if self.n:
            self.e.wait_ge(self.steps, self.n)
        met = self.prog.sem(f"{scope}_met")
        self.e.drain().then_inc(met, 1)
        self.e.wait_ge(met, turn * 8 + 4)
        self.e.sem_inc(self.prog.sem("passed"), 1)
        for name in sorted(self.mine):
            self.e.sem_clear(self.prog.sem(name))
        self.e.drain().then_inc(met, 1)
        self.e.wait_ge(met, turn * 8 + 8)
        self.n = 0
        self.mine = {f"{self.name}_steps"}


class TileRing:

    def __init__(self, prog, name, banks):
        self.full, self.drained = prog.sem(f"{name}_tile_full"), prog.sem(f"{name}_tile_drained")
        self.names = (f"{name}_tile_full", f"{name}_tile_drained")
        self.banks, self.size = banks, len(banks)
        self.opened = 0
        self.taken = {}

    def open(self, pe):
        pe.mine.add(self.names[0])
        self.opened += 1
        return self.banks[(self.opened - 1) % self.size]

    def turn(self, eng):
        return self.taken.get(eng.name, 0) + 1

    def take(self, eng):
        if eng.name != "act" or self.names[1] != "both_tile_drained":
            eng.mine.add(self.names[1])
        self.taken[eng.name] = self.turn(eng)
        return self.banks[(self.taken[eng.name] - 1) % self.size]

    def reset(self, name):
        if name == "pe":
            self.opened = 0
        self.taken[name] = 0


class Weights:

    def __init__(self, prog, pe):
        self.prog, self.pe = prog, pe
        self.owed = 0

    def start(self, base, slots, loaded, free):
        self.n, self.base = 0, base
        self.slots, self.loaded, self.free = slots, loaded, free

    def next(self):
        s, r = self.n % len(self.slots), self.n // len(self.slots)
        self.n += 1
        self.pe.e.wait_ge(self.loaded[s], self.base + 16 * (r + 1))
        return self.slots[s]

    def used(self, n=1):
        self.owed += n

    def mm(self, out, lhsT, rhs, start=True, stop=True):
        ins = self.pe.e.matmul(out, lhsT, rhs, start=start, stop=stop)
        return self._tell(ins)

    def transpose(self, out, in_, identity):
        return self._tell(self.pe.e.transpose(out, in_, identity))

    def _tell(self, ins):
        if self.owed:
            ins.then_inc(self.free, self.owed)
            self.owed = 0
        return ins

    def flush(self):
        if self.owed:
            self.pe.e.drain().then_inc(self.free, self.owed)
            self.owed = 0


class Program:
    def __init__(self, nc, ctx, io):
        self.nc, self.ctx, self.io = nc, ctx, io
        self.sems = {}
        self.count = {}
        self.mark = {}
        self.slots_free = self.sem("slots_free")
        self.slot_loaded = [self.sem(f"slot_loaded_{s}") for s in range(SLOTS)]
        ring = self.sb("ring", SLOTS * UNIT)
        self.slots = [ring[:, s * UNIT:(s + 1) * UNIT] for s in range(SLOTS)]
        self.expert_slot_loaded = [self.sem(f"expert_slot_loaded_{s}") for s in range(EXPERT_SLOTS)]
        self.expert_slots_used = self.sem("expert_slots_used")
        self.const = self.sb("const", CONST_W)
        self.par = self.sb("par", max(LAYER_W, SECOND_W))
        self.x = self.sb("x", NB * D)[:, :].rearrange("p (b d) -> p b d", b=NB)
        self.small = self.sb("small", 256)
        self.arena_w = 26240
        self.arena = self.sb("arena", self.arena_w)
        self.at = 0
        tail = [self.arena[:, self.arena_w - (j + 1) * UNIT:self.arena_w - j * UNIT]
                for j in range(EXPERT_SLOTS - SLOTS)]
        first = DENSE_UNITS % SLOTS
        self.expert_slots = self.slots[first:] + self.slots[:first] + tail
        self.ps = [ctx.enter_context(nc.psum_tensor(f"ps{i}", [P, 512], F32)) for i in range(8)]
        b = [t[:, :] for t in self.ps]
        self.act_tiles = TileRing(self, "act", b[0:2])
        self.dve_tiles = TileRing(self, "dve", b[2:6])
        self.both_tiles = TileRing(self, "both", b[6:8])

    def sem(self, name):
        if name not in self.sems:
            self.sems[name] = self.ctx.enter_context(self.nc.semaphore(name))
        return self.sems[name]

    def sb(self, name, width, dt=F32):
        return self.ctx.enter_context(self.nc.sbuf_tensor(name, [P, width], dt))

    def take(self, *shape):
        width = int(np.prod(shape))
        ap = self.arena[:, self.at:self.at + width]
        self.at += width
        assert self.at <= self.arena_w, self.at
        return shaped(ap, *shape)

    def c(self, name, *shape):
        a, b = CONST[name]
        return shaped(self.const[:, a:b], *shape)

    def lp(self, name, *shape):
        a, b = LAYER[name]
        return shaped(self.par[:, a:b], *shape)

    def sp(self, name, *shape):
        a, b = SECOND[name]
        return shaped(self.par[:, a:b], *shape)

    def reset_rings(self, name):
        for r in (self.act_tiles, self.dve_tiles, self.both_tiles):
            r.reset(name)


def shaped(ap, *shape):
    if len(shape) < 2:
        return ap
    names = "abcd"[:len(shape)]
    spec = f"p ({' '.join(names)}) -> p {' '.join(names)}"
    return ap.rearrange(spec, **{n: s for n, s in zip(names[:-1], shape[:-1])})


def spread(ap, axis, n):
    u = ap.unsqueeze(axis)
    shape = list(u.shape)
    shape[axis] = n
    return u.to_broadcast(shape)



def norm_stats(p, act, src, width, out, tag):
    for b in range(NB):
        act.e.activation(p.junk_act[:, 0:width], src[:, b, 0:width], ACT.Square,
                                accum_out=p.small_act[:, b:b + 1]).then_inc(act.step(), 1)
        act.e.wait_ge(act.steps, act.n)
    act.e.activation(out, p.small_act[:, 0:2], ACT.Sqrt, scale=1.0 / width, bias=p.c("eps")).then_inc(act.event(tag), 1)


def norm_rows(p, dve, src, rstd, dst, tag):
    for b in range(NB):
        ins = dve.e.tensor_scalar(dst[:, b, :], src[:, b, :], rstd[:, b:b + 1], None, ALU.mult)
        if b == NB - 1:
            ins.then_inc(dve.event(tag), 1)
        else:
            ins.then_inc(dve.step(), 1)


def half_squares_act(p, act, src, b, seen):
    return act.e.activation(p.junk_act[:, 512 * seen:512 * seen + 512], src, ACT.Square, scale=D ** -0.5,
                            accum_out=p.small_act[:, 2 * b + seen:2 * b + seen + 1])


def root_act(p, act, b, seen, out):
    base = p.norm_base[:, b:b + 1]
    if not seen:
        return act.e.activation(base, p.small_act[:, 2 * b:2 * b + 1], ACT.Identity, bias=p.c("eps"))
    return act.e.activation(out, p.small_act[:, 2 * b + 1:2 * b + 2], ACT.Sqrt, bias=base)


def pre_norm_act(p, act, order, ready=None, counts=(0,) * 4):
    seen = [0] * NB
    for (half, b), count in zip(order, counts):
        if count:
            act.e.wait_ge(ready, count)
        half_squares_act(p, act, p.x[:, b, half * 512:half * 512 + 512], b, seen[b]).then_inc(act.step(), 1)
        act.e.wait_ge(act.steps, act.n)
        ins = root_act(p, act, b, seen[b], p.pre_root[:, b:b + 1])
        if seen[b]:
            ins.then_inc(act.event("pre_root"), 1)
        else:
            ins.then_inc(act.step(), 1)
            act.e.wait_ge(act.steps, act.n)
        seen[b] += 1


def diagonal_dve(p, dve, b, n):
    dve.e.wait_ge(p.sem("pre_root"), n)
    dve.e.reciprocal(p.pre_rstd[:, b:b + 1], p.pre_root[:, b:b + 1]).then_inc(dve.step(), 1)
    dve.e.wait_ge(dve.steps, dve.n)
    dve.e.tensor_scalar(p.diag[:, b, :], p.c("ident"), p.pre_rstd[:, b:b + 1], None, ALU.mult).then_inc(
        dve.event("diagonal"), 1)


def normed_columns_pe(p, pe, w, n):
    banks = []
    for j in range(KC // 2):
        tiles = p.act_tiles if j % 2 == 0 else p.dve_tiles
        if tiles.opened >= tiles.size:
            pe.e.wait_ge(tiles.drained, tiles.opened - tiles.size + 1)
        bank = tiles.open(pe)
        banks.append((tiles, bank))
    for b in range(NB):
        if n is not None:
            pe.e.wait_ge(p.sem("diagonal"), n + b + 1)
        for j, (tiles, bank) in enumerate(banks):
            for c in range(2):
                last = b == NB - 1 and c == 1
                o = c * S + b * P
                ins = (pe.e.matmul if last else w.mm)(bank[:, o:o + P], p.x[:, b, (2 * j + c) * P:(2 * j + c + 1) * P],
                                                      p.diag[:, b, :])
                if last:
                    ins.then_inc(tiles.full, 1)


def rows_to_columns_pe(p, pe, w, src, chunks, tag, n):
    pe.e.wait_ge(p.sem(tag + "_rows"), n)
    ident = p.c("ident")
    for j in range((chunks + 1) // 2):
        tiles = p.act_tiles if j % 2 == 0 else p.dve_tiles
        if tiles.opened >= tiles.size:
            pe.e.wait_ge(tiles.drained, tiles.opened - tiles.size + 1)
        bank = tiles.open(pe)
        for c in range(2 * j, min(2 * j + 2, chunks)):
            for b in range(NB):
                o = (c - 2 * j) * S + b * P
                ins = w.transpose(bank[:, o:o + P], src[:, b, c * P:(c + 1) * P], ident) if not (
                    c == min(2 * j + 2, chunks) - 1 and b == NB - 1) else pe.e.transpose(
                        bank[:, o:o + P], src[:, b, c * P:(c + 1) * P], ident)
        ins.then_inc(tiles.full, 1)


def rows_to_columns_evac(p, eng, dst, gain, chunks, mine):
    for j in range((chunks + 1) // 2):
        if (j % 2 == 0) != mine:
            continue
        tiles = p.act_tiles if mine else p.dve_tiles
        eng.e.wait_ge(tiles.full, tiles.turn(eng))
        bank = tiles.take(eng)
        cs = range(2 * j, min(2 * j + 2, chunks))
        for c in cs:
            o = (c - 2 * j) * S
            g = 1.0 if gain is None else gain[:, c:c + 1]
            if mine:
                ins = eng.e.activation(dst[:, c, :], bank[:, o:o + S], ACT.Copy, scale=g)
            else:
                ins = eng.e.tensor_scalar(dst[:, c, :], bank[:, o:o + S], g, None, ALU.mult)
            if c == cs[-1]:
                ins.then_inc(tiles.drained, 1)
            else:
                ins.then_inc(eng.step(), 1)


def columns_ready(p, pe):
    pe.e.wait_ge(p.act_tiles.drained, p.act_tiles.opened)
    pe.e.wait_ge(p.dve_tiles.drained, p.dve_tiles.opened)



def project_columns(p, pe, w, src, tiles, n=2):
    u = w.next()
    if tiles.opened >= tiles.size:
        pe.e.wait_ge(tiles.drained, tiles.opened - tiles.size + 1)
    bank = tiles.open(pe)
    for c in range(n):
        for k in range(KC):
            o = (c * KC + k) * P
            last = c == n - 1 and k == KC - 1
            ins = (pe.e.matmul if last else w.mm)(bank[:, c * S:(c + 1) * S], u[:, o:o + P], src[:, k, :],
                                                  start=k == 0, stop=k == KC - 1)
    ins.then_inc(tiles.full, 1)
    w.used()


def project_rows(p, pe, w, src, tiles, width, split=2):
    kn = KC // split
    banks = []
    for _ in range(NB):
        if tiles.opened >= tiles.size:
            pe.e.wait_ge(tiles.drained, tiles.opened - tiles.size + 1)
        bank = tiles.open(pe)
        banks.append(bank)
    for h in range(split):
        u = w.next()
        for b in range(NB):
            for k in range(kn):
                kk = h * kn + k
                last = h == split - 1 and k == kn - 1
                ins = (pe.e.matmul if last else w.mm)(banks[b][:, 0:width], src[:, kk, b * P:(b + 1) * P],
                                                      u[:, k * width:(k + 1) * width],
                                                      start=kk == 0, stop=kk == KC - 1)
                if last:
                    ins.then_inc(tiles.full, 1)
        w.used()



def first_buffers(p):
    p.at = 0
    p.hrow = p.take(NB, D)
    p.hT = p.take(KC, S)
    p.memT = p.take(KC, S)
    p.memgT = shaped(p.hrow.rearrange("p b d -> p (b d)"), KC, S)
    p.mla = p.take(NB, 416)
    p.v_row = p.take(NB, 384)
    p.qk = p.take(10, S)
    p.xqT = p.qk[:, 0:8, :]
    p.xkT = p.take(KC, S)
    p.xv = p.take(NB, D)
    p.mixT = p.hT
    p.dist = p.take(NB, S)
    p.dist_swa = p.take(NB, S)
    p.rot = p.take(2, NB, 16)
    mark = p.at
    p.cq = p.take(NB, 384)
    p.cqT = p.take(3, S)
    p.q_mla = p.take(NB, 4, 96)
    p.k_mla = shaped(p.cq.rearrange("p b d -> p (b d)"), NB, 4, 96)
    p.kv = p.take(NB, 512)
    p.qT_mla = p.qk[:, 0:4, :]
    p.kT_mla = p.take(4, S)
    p.o_diff = p.take(NB, 256)
    p.sc = [p.take(NB, S) for _ in range(4)]
    p.pr = [p.take(NB, S) for _ in range(4)]
    p.junk_act = p.arena[:, p.at - 1024:p.at]
    p.pT = [p.take(NB, S) for _ in range(2)]
    p.junk_dve = p.take(512)
    end = p.at
    p.at = mark
    p.h1T = p.take(FC, S)
    p.silu = p.take(2, S)
    p.at = max(p.at, end)
    p.small_act = p.small[:, 0:8]
    p.rstd = p.small[:, 8:10]
    p.pre_rstd = p.small[:, 136:138]
    p.norm_base = p.small[:, 138:140]
    p.pre_root, p.post_root = p.small[:, 4:6], p.small[:, 6:8]
    p.diag = p.c("swa_far")[:, 0:NB * P].rearrange("p (b t) -> p b t", b=NB)
    p.lam = p.small[:, 10:16]
    p.mx = p.small[:, 16:48]
    p.sums = p.small[:, 48:112]
    p.diff_ss = p.small[:, 112:136]


HEAD_ITEMS = ([("diff", h, m) for h in range(4) for m in range(2)]
              + [("swa", h, 0) for j in range(4) for h in (j, j + 4)]
              + [("mla", h, 0) for h in range(4)])
X_ITEMS = [("x", h, 0) for h in range(4)]
GQA_ITEMS = [("gqa", h, 0) for j in range(4) for h in (j, j + 4)]
SCALE = {"gqa": 64 ** -0.5, "diff": 32 ** -0.5, "swa": 64 ** -0.5, "mla": 96 ** -0.5, "x": 256 ** -0.5}


def beside(item, i):
    kind, h, m = item
    if kind == "gqa":
        return i
    i = i - 1 if kind == "diff" else i
    return i // 2 if i % 2 == 0 and i < 16 else None


def scores_pe(p, pe, w, i, item):
    kind, h, m = item
    if p.both_tiles.opened >= p.both_tiles.size:
        pe.e.wait_ge(p.both_tiles.drained, p.both_tiles.opened - p.both_tiles.size + 1)
    bank = p.both_tiles.open(pe)
    for b in range(NB):
        q = slice(b * P, (b + 1) * P)
        if kind == "diff":
            r = slice(64 * (h % 2) + 32 * m, 64 * (h % 2) + 32 * m + 32)
            parts = [(p.qk[r, h // 2, q], p.qk[r, 2 + h // 2, :])]
        elif kind == "swa":
            r = slice(64 * (h // 4), 64 * (h // 4) + 64)
            parts = [(p.qk[r, 4 + h % 4, q], p.qk[r, 8, :])]
        elif kind == "gqa":
            r = slice(64 * (h // 4), 64 * (h // 4) + 64)
            parts = [(p.qk2[r, h % 4, q], p.qk2[r, 4, :])]
        elif kind == "mla":
            parts = [(p.qT_mla[0:96, h, q], p.kT_mla[0:96, h, :])]
        else:
            parts = [(p.xqT[:, 2 * h + c, q], p.xkT[:, 2 * h + c, :]) for c in range(2)]
        for j, (a, k) in enumerate(parts):
            ins = pe.e.matmul(bank[:, b * S:(b + 1) * S], a, k, start=j == 0, stop=j == len(parts) - 1)
    ins.then_inc(p.both_tiles.full, 1)


def softmax_max_dve(p, dve, i, item):
    kind, h, m = item
    scale = SCALE[kind]
    dve.e.wait_ge(p.both_tiles.full, p.both_tiles.turn(dve))
    bank = shaped(p.both_tiles.take(dve), NB, S)
    sc, mx = p.sc[i % 4], p.mx[:, 2 * (i % 8):2 * (i % 8) + 2]
    nm = p.mx[:, 16 + 2 * (i % 8):18 + 2 * (i % 8)]
    if i >= 4:
        dve.e.wait_ge(p.sem("probs_made"), i - 3)
    if kind in ("diff", "swa"):
        slope = SLOPES[h + 8] if kind == "diff" else SLOPES[h]
        dist = p.dist if kind == "diff" else p.dist_swa
        dve.e.scalar_tensor_tensor(sc, dist, -slope / scale, bank, ALU.mult, ALU.add).then_inc(p.both_tiles.drained, 1)
    else:
        dve.e.tensor_copy(sc, bank).then_inc(p.both_tiles.drained, 1)
    dve.e.wait_ge(p.both_tiles.drained, p.both_tiles.taken["dve"])
    dve.e.tensor_reduce(mx, sc, AX, ALU.max).then_inc(dve.step(), 1)
    dve.e.wait_ge(dve.steps, dve.n)
    if kind == "swa":
        dve.e.tensor_scalar(mx, mx, scale, p.lp("sinks")[:, h:h + 1], ALU.mult, ALU.max).then_inc(dve.step(), 1)
        dve.e.wait_ge(dve.steps, dve.n)
        dve.e.tensor_scalar(nm, mx, -1.0, None, ALU.mult).then_inc(dve.event("max_found"), 1)
    else:
        dve.e.tensor_scalar(nm, mx, -scale, None, ALU.mult).then_inc(dve.event("max_found"), 1)


def softmax_exp_act(p, act, i, item):
    kind, h, m = item
    act.e.wait_ge(p.sem("max_found"), i + 1)
    if i >= 4:
        act.e.wait_ge(p.sem("probs_scaled"), i - 3)
    nm = p.mx[:, 16 + 2 * (i % 8):18 + 2 * (i % 8)]
    sums = p.sums[:, 4 * (i % 8):4 * (i % 8) + 4]
    if kind == "swa":
        act.e.activation(sums[:, 2:4], nm, ACT.Exp, bias=p.lp("sinks")[:, h:h + 1]).then_inc(act.step(), 1)
    for b in range(NB):
        ins = act.e.activation(p.pr[i % 4][:, b, :], p.sc[i % 4][:, b, :], ACT.Exp,
                               bias=nm[:, b:b + 1], scale=SCALE[kind], accum_out=sums[:, b:b + 1])
        if b == NB - 1:
            ins.then_inc(act.event("probs_made"), 1)
        else:
            ins.then_inc(act.step(), 1)


def softmax_scale_dve(p, dve, i, item):
    kind, h, m = item
    dve.e.wait_ge(p.sem("probs_made"), i + 1)
    sums = p.sums[:, 4 * (i % 8):4 * (i % 8) + 4]
    pr = p.pr[i % 4]
    if kind == "swa":
        dve.e.tensor_tensor(sums[:, 0:2], sums[:, 0:2], sums[:, 2:4], ALU.add).then_inc(dve.step(), 1)
        dve.e.wait_ge(dve.steps, dve.n)
    dve.e.reciprocal(sums[:, 0:2], sums[:, 0:2]).then_inc(dve.step(), 1)
    dve.e.wait_ge(dve.steps, dve.n)
    if kind == "diff" and m == 1:
        dve.e.tensor_scalar(sums[:, 0:2], sums[:, 0:2], p.lam[:, 0:1], None, ALU.mult).then_inc(dve.step(), 1)
        dve.e.wait_ge(dve.steps, dve.n)
    for b in range(NB):
        ins = dve.e.tensor_scalar(pr[:, b, :], pr[:, b, :], sums[:, b:b + 1], None, ALU.mult)
        if kind == "diff" and m == 1 or b < NB - 1:
            ins.then_inc(dve.step(), 1)
        else:
            ins.then_inc(dve.event("probs_scaled"), 1)
    if kind == "diff" and m == 1:
        dve.e.wait_ge(p.sem("probs_scaled"), i)
        dve.e.wait_ge(dve.steps, dve.n)
        dve.e.tensor_tensor(p.pr[(i - 1) % 4], p.pr[(i - 1) % 4], pr, ALU.subtract).then_inc(dve.event("probs_scaled"), 1)


def probs_source(p, i, item):
    return p.pr[(i - 1) % 4] if item[0] == "diff" else p.pr[i % 4]


def has_output(item):
    return not (item[0] == "diff" and item[2] == 0)


def probs_transpose_pe(p, pe, w, i, item):
    pe.e.wait_ge(p.sem("probs_scaled"), i + 1)
    src = probs_source(p, i, item)
    if p.act_tiles.opened >= p.act_tiles.size:
        pe.e.wait_ge(p.act_tiles.drained, p.act_tiles.opened - p.act_tiles.size + 1)
    bank = p.act_tiles.open(pe)
    for kb in range(NB):
        for b in range(NB):
            o = kb * S + b * P
            ins = pe.e.transpose(bank[:, o:o + P], src[:, b, kb * P:(kb + 1) * P], p.c("ident"))
    ins.then_inc(p.act_tiles.full, 1)


def values_pe(p, pe, w, i, item, nth):
    kind, h, m = item
    pe.e.wait_ge(p.act_tiles.drained, p.act_tiles.opened)
    pT = p.pT[nth % 2]
    if kind == "diff":
        if p.act_tiles.opened >= p.act_tiles.size:
            pe.e.wait_ge(p.act_tiles.drained, p.act_tiles.opened - p.act_tiles.size + 1)
        bank = p.act_tiles.open(pe)
        for b in range(NB):
            for kb in range(NB):
                ins = pe.e.matmul(bank[:, b * 64:b * 64 + 64], pT[:, kb, b * P:(b + 1) * P],
                                  p.v_row[:, kb, h * 64:h * 64 + 64], start=kb == 0, stop=kb == NB - 1)
        ins.then_inc(p.act_tiles.full, 1)
    elif kind == "x":
        if p.act_tiles.opened >= p.act_tiles.size:
            pe.e.wait_ge(p.act_tiles.drained, p.act_tiles.opened - p.act_tiles.size + 1)
        bank = p.act_tiles.open(pe)
        for c in range(2):
            for kb in range(NB):
                o = h * 256 + c * P
                ins = pe.e.matmul(bank[:, c * S:(c + 1) * S], p.xv[:, kb, o:o + P], pT[:, kb, :],
                                  start=kb == 0, stop=kb == NB - 1)
        ins.then_inc(p.act_tiles.full, 1)
    else:
        half = h % 2 if kind == "mla" else h // 4
        if p.act_tiles.opened >= p.act_tiles.size:
            pe.e.wait_ge(p.act_tiles.drained, p.act_tiles.opened - p.act_tiles.size + 1)
        bank = p.act_tiles.open(pe)
        for kb in range(NB):
            v = (p.att[:, kb, 640 + 64 * half:704 + 64 * half] if kind == "gqa" else
                 p.kv[:, kb, h * P + 64:h * P + 128] if kind == "mla"
                 else p.v_row[:, kb, 256 + 64 * (h // 4):320 + 64 * (h // 4)])
            ins = pe.e.matmul(bank[64 * half:64 * half + 64, 0:S], v, pT[:, kb, :],
                              start=kb == 0, stop=kb == NB - 1)
        ins.then_inc(p.act_tiles.full, 1)


def attention_pe(p, pe, w, items, memory=None):
    nth = 0
    for t in range(len(items) + 2):
        if t < len(items):
            if items[t][0] == "mla" and (t == 0 or items[t - 1][0] != "mla"):
                mla_columns_pe(p, pe, w)
            scores_pe(p, pe, w, t, items[t])
        if t >= 2 and has_output(items[t - 2]):
            probs_transpose_pe(p, pe, w, t - 2, items[t - 2])
            u = beside(items[t - 2], t - 2)
            if memory is not None and u is not None:
                memory(u)
            values_pe(p, pe, w, t - 2, items[t - 2], nth)
            nth += 1
            if items[t - 2] == ("diff", 3, 1):
                p.mark["diff"] = p.act_tiles.opened


def attention_dve(p, dve, items, before=None):
    for t in range(len(items) + 1):
        if t < len(items):
            if before and t in before:
                before[t]()
            softmax_max_dve(p, dve, t, items[t])
        if t >= 1:
            softmax_scale_dve(p, dve, t - 1, items[t - 1])


def attention_act(p, act, items, dst, memory=None, before=None):
    nth = 0
    for t in range(len(items) + 2):
        if t < len(items):
            if before and t in before:
                before[t]()
        output = t >= 2 and has_output(items[t - 2])
        if output:
            act.e.wait_ge(p.act_tiles.full, p.act_tiles.turn(act))
            bank = shaped(p.act_tiles.take(act), NB, S)
            act.e.activation(p.pT[nth % 2], bank, ACT.Copy).then_inc(p.act_tiles.drained, 1)
        if t < len(items):
            softmax_exp_act(p, act, t, items[t])
        if output:
            i, item = t - 2, items[t - 2]
            kind, h, m = item
            u = beside(item, i)
            if memory is not None and u is not None:
                memory(u)
            act.e.wait_ge(p.act_tiles.full, p.act_tiles.turn(act))
            bank = p.act_tiles.take(act)
            if kind == "diff":
                out = p.o_diff[:, :, h * 64:h * 64 + 64]
                act.e.activation(out, shaped(bank[:, 0:128], NB, 64), ACT.Copy).then_inc(p.act_tiles.drained, 1)
            elif kind == "x":
                act.e.activation(dst[:, 2 * h:2 * h + 2, :], shaped(bank, 2, S), ACT.Copy).then_inc(p.act_tiles.drained, 1)
            else:
                half = h % 2 if kind == "mla" else h // 4
                c = h % 4 if kind == "gqa" else 2 + h // 2 if kind == "mla" else 4 + h % 4
                r = slice(64 * half, 64 * half + 64)
                act.e.activation(dst[r, c, :], bank[r, 0:S], ACT.Copy).then_inc(p.act_tiles.drained, 1)
            nth += 1


def mla_columns_pe(p, pe, w):
    rows_to_columns_pe(p, pe, w, p.cq, 3, "latent", 1)
    columns_ready(p, pe)
    for b in range(NB):
        if p.dve_tiles.opened >= p.dve_tiles.size:
            pe.e.wait_ge(p.dve_tiles.drained, p.dve_tiles.opened - p.dve_tiles.size + 1)
        bank = p.dve_tiles.open(pe)
        for c in range(2):
            ins = pe.e.matmul(bank[:, 0:384], p.cqT[:, c, b * P:(b + 1) * P],
                              p.lp("q_up")[:, c * 384:(c + 1) * 384], start=c == 0, stop=c == 1)
        ins.then_inc(p.dve_tiles.full, 1)
    for b in range(NB):
        if p.dve_tiles.opened >= p.dve_tiles.size:
            pe.e.wait_ge(p.dve_tiles.drained, p.dve_tiles.opened - p.dve_tiles.size + 1)
        bank = p.dve_tiles.open(pe)
        ins = pe.e.matmul(bank[:, 0:512], p.cqT[:, 2, b * P:(b + 1) * P], p.lp("kv_up"))
        ins.then_inc(p.dve_tiles.full, 1)
    pe.e.wait_ge(p.sem("mla_rows"), 1)
    for src in (p.q_mla, p.k_mla):
        for j in range(2):
            if p.dve_tiles.opened >= p.dve_tiles.size:
                pe.e.wait_ge(p.dve_tiles.drained, p.dve_tiles.opened - p.dve_tiles.size + 1)
            bank = p.dve_tiles.open(pe)
            for c in range(2):
                for b in range(NB):
                    o = c * S + b * P
                    ins = pe.e.transpose(bank[0:96, o:o + P], src[:, b, 2 * j + c, :], p.c("ident"))
            ins.then_inc(p.dve_tiles.full, 1)
    pe.e.wait_ge(p.dve_tiles.drained, p.dve_tiles.opened)


def latent_stats_act(p, act):
    junk = p.q_mla.rearrange("p b h d -> p (b h d)")[:, 0:256]
    act.e.wait_ge(p.dve_tiles.drained, p.mark["mla"])
    for b in range(NB):
        act.e.activation(junk, p.mla[:, b, 0:256], ACT.Square,
                                accum_out=p.small_act[:, b:b + 1]).then_inc(act.step(), 1)
        act.e.wait_ge(act.steps, act.n)
        act.e.activation(junk[:, 0:128], p.mla[:, b, 256:384], ACT.Square,
                                accum_out=p.small_act[:, 2 + b:3 + b]).then_inc(act.step(), 1)
        act.e.wait_ge(act.steps, act.n)
    act.e.activation(p.small_act[:, 4:6], p.small_act[:, 0:2], ACT.Ln, scale=1.0 / 256, bias=p.c("eps")).then_inc(act.step(), 1)
    act.e.wait_ge(act.steps, act.n)
    act.e.activation(p.small_act[:, 6:8], p.small_act[:, 2:4], ACT.Ln, scale=1.0 / 128, bias=p.c("eps")).then_inc(act.step(), 1)
    act.e.wait_ge(act.steps, act.n)
    act.e.activation(p.lam[:, 2:6], p.small_act[:, 4:8], ACT.Exp, scale=-0.5).then_inc(act.event("latent_rstd"), 1)


def rotate(p, dve, dst, x1, x2, cos, sin, tmp):
    d1, d2 = dst
    t1, t2, t3, t4 = tmp
    dve.e.tensor_tensor(t1, x1, cos, ALU.mult).then_inc(dve.step(), 1)
    dve.e.tensor_tensor(t2, x2, sin, ALU.mult).then_inc(dve.step(), 1)
    dve.e.tensor_tensor(t3, x1, sin, ALU.mult).then_inc(dve.step(), 1)
    dve.e.tensor_tensor(t4, x2, cos, ALU.mult).then_inc(dve.step(), 1)
    dve.e.wait_ge(dve.steps, dve.n)
    dve.e.tensor_tensor(d1, t1, t2, ALU.subtract).then_inc(dve.step(), 1)
    dve.e.tensor_tensor(d2, t3, t4, ALU.add).then_inc(dve.step(), 1)


def mla_dve(p, dve):
    dve.e.wait_ge(p.sem("latent_rstd"), 1)
    for b in range(NB):
        dve.e.tensor_scalar(p.cq[:, b, 0:256], p.mla[:, b, 0:256], p.lam[:, 2 + b:3 + b], None, ALU.mult).then_inc(dve.step(), 1)
        ins = dve.e.tensor_scalar(p.cq[:, b, 256:384], p.mla[:, b, 256:384], p.lam[:, 4 + b:5 + b], None, ALU.mult)
        if b == NB - 1:
            ins.then_inc(dve.event("latent_rows"), 1)
        else:
            ins.then_inc(dve.step(), 1)
    dve.e.wait_ge(p.dve_tiles.full, p.dve_tiles.turn(dve))
    bank = p.dve_tiles.take(dve)
    dve.e.tensor_scalar(p.cqT[:, 2, :], bank[:, 0:S], p.lp("g_kv"), None, ALU.mult).then_inc(p.dve_tiles.drained, 1)
    tmp = [shaped(p.junk_dve[:, j * 64:(j + 1) * 64], 4, 16) for j in range(4)]
    for b in range(NB):
        dve.e.wait_ge(p.dve_tiles.full, p.dve_tiles.turn(dve))
        bank = shaped(p.dve_tiles.take(dve)[:, 0:384], 4, 96)
        dve.e.tensor_copy(p.q_mla[:, b], bank).then_inc(p.dve_tiles.drained, 1)
    dve.e.wait_ge(p.dve_tiles.drained, p.dve_tiles.taken["dve"])
    for b in range(NB):
        dve.e.wait_ge(p.dve_tiles.full, p.dve_tiles.turn(dve))
        bank = p.dve_tiles.take(dve)
        dve.e.tensor_copy(p.kv[:, b, :], bank).then_inc(p.dve_tiles.drained, 1)
    dve.e.wait_ge(p.dve_tiles.drained, p.dve_tiles.taken["dve"])
    for b in range(NB):
        cos, sin = spread(p.rot[:, 0, b, :], 1, 4), spread(p.rot[:, 1, b, :], 1, 4)
        rotate(p, dve, (p.q_mla[:, b, :, 64:80], p.q_mla[:, b, :, 80:96]),
               p.q_mla[:, b, :, 64:80], p.q_mla[:, b, :, 80:96], cos, sin, tmp)
        dve.e.wait_ge(dve.steps, dve.n)
        t = [x[:, 0, :] for x in tmp]
        kr = p.mla[:, b, 384:416]
        rotate(p, dve, (kr[:, 0:16], kr[:, 16:32]), kr[:, 0:16], kr[:, 16:32],
               p.rot[:, 0, b, :], p.rot[:, 1, b, :], t)
        dve.e.wait_ge(dve.steps, dve.n)
        dve.e.tensor_copy(p.k_mla[:, b, :, 0:64], shaped(p.kv[:, b, :], 4, 128)[:, :, 0:64]).then_inc(dve.step(), 1)
        ins = dve.e.tensor_copy(p.k_mla[:, b, :, 64:96], spread(kr, 1, 4))
        if b == NB - 1:
            ins.then_inc(dve.event("mla_rows"), 1)
        else:
            ins.then_inc(dve.step(), 1)
    for dst in (p.qT_mla, p.kT_mla):
        for j in range(2):
            dve.e.wait_ge(p.dve_tiles.full, p.dve_tiles.turn(dve))
            bank = shaped(p.dve_tiles.take(dve), 2, S)
            dve.e.tensor_copy(dst[0:96, 2 * j:2 * j + 2, :], bank[0:96]).then_inc(p.dve_tiles.drained, 1)


def mla_act(p, act):
    act.e.wait_ge(p.act_tiles.full, p.act_tiles.turn(act))
    bank = p.act_tiles.take(act)
    act.e.activation(p.cqT[:, 0, :], bank[:, 0:S], ACT.Copy, scale=p.lp("g_q")[:, 0:1]).then_inc(act.step(), 1)
    act.e.activation(p.cqT[:, 1, :], bank[:, S:2 * S], ACT.Copy, scale=p.lp("g_q")[:, 1:2]).then_inc(p.act_tiles.drained, 1)


def residual_act(p, act, r, order):
    first = p.mark[f"mix{r + 1}"] - 4
    seen = [0] * NB
    for t, (half, b) in enumerate(order):
        act.e.wait_ge(p.dve_tiles.full, first + t + 1)
        bank = p.dve_tiles.banks[(first + t) % p.dve_tiles.size]
        half_squares_act(p, act, bank, b, seen[b]).then_inc(act.event("squared"), 1)
        act.e.wait_ge(p.sem("squared"), 4 * r + t + 1)
        ins = root_act(p, act, b, seen[b], p.post_root[:, b:b + 1])
        if not seen[b]:
            ins.then_inc(act.step(), 1)
            act.e.wait_ge(act.steps, act.n)
        else:
            ins.then_inc(act.event("post_root"), 1)
            pre_norm_act(p, act, [(0, b), (1, b)], p.sem("x_ready"), [4 * r + 2 * b + 1, 4 * r + 2 * b + 2])
        seen[b] += 1


def residual_dve(p, dve, gain, r, order):
    seen = [0] * NB
    for t, (half, b) in enumerate(order):
        dve.e.wait_ge(p.sem("squared"), 4 * r + t + 1)
        bank = p.dve_tiles.take(dve)
        hs = slice(half * 512, half * 512 + 512)
        dve.e.tensor_tensor(p.hrow[:, b, hs], bank, gain[:, hs], ALU.mult).then_inc(p.dve_tiles.drained, 1)
        seen[b] += 1
        if seen[b] == 2:
            dve.e.wait_ge(p.dve_tiles.drained, p.dve_tiles.taken["dve"])
            dve.e.wait_ge(p.sem("post_root"), 2 * r + b + 1)
            dve.e.reciprocal(p.rstd[:, b:b + 1], p.post_root[:, b:b + 1]).then_inc(dve.step(), 1)
            dve.e.wait_ge(dve.steps, dve.n)
            for h in range(2):
                hs = slice(h * 512, h * 512 + 512)
                dve.e.scalar_tensor_tensor(p.x[:, b, hs], p.hrow[:, b, hs], p.rstd[:, b:b + 1], p.x[:, b, hs],
                                           ALU.mult, ALU.add).then_inc(dve.event("x_ready"), 1)
            diagonal_dve(p, dve, b, 2 * r + b + 1)



def layer_pe(p, pe, w, l):
    normed_columns_pe(p, pe, w, None)
    pe.e.wait_ge(p.sem("layer_params"), l * 16 + 16)
    columns_ready(p, pe)
    project_rows(p, pe, w, p.hT, p.dve_tiles, 416)
    p.mark["mla"] = p.dve_tiles.opened
    project_rows(p, pe, w, p.hT, p.dve_tiles, 384)
    for j in range(5):
        project_columns(p, pe, w, p.hT, p.act_tiles, 2 if j < 4 else 1)
    columns_ready(p, pe)
    pe.e.wait_ge(p.sem("memory_gained"), 1)

    def memory(u):
        if u < 4:
            project_columns(p, pe, w, p.memgT, p.dve_tiles)
        elif u in (4, 6):
            project_rows(p, pe, w, p.memgT, p.dve_tiles, 512)
    attention_pe(p, pe, w, HEAD_ITEMS, memory)
    rows_to_columns_pe(p, pe, w, p.o_diff, 2, "diff", 1)
    columns_ready(p, pe)
    for _ in range(2):
        project_rows(p, pe, w, p.mixT, p.dve_tiles, 512)
    p.mark["mix1"] = p.dve_tiles.opened
    normed_columns_pe(p, pe, w, 0)
    columns_ready(p, pe)
    for _ in range(4):
        project_columns(p, pe, w, p.hT, p.act_tiles)
    columns_ready(p, pe)
    attention_x(p, "pe", pe, w)
    columns_ready(p, pe)
    for _ in range(2):
        project_rows(p, pe, w, p.mixT, p.dve_tiles, 512)
    p.mark["mix2"] = p.dve_tiles.opened
    normed_columns_pe(p, pe, w, 2)
    columns_ready(p, pe)
    acc = []
    for _ in range(4):
        if p.dve_tiles.opened >= p.dve_tiles.size:
            pe.e.wait_ge(p.dve_tiles.drained, p.dve_tiles.opened - p.dve_tiles.size + 1)
        bank = p.dve_tiles.open(pe)
        acc.append(bank)
    p.mark["hidden"] = p.both_tiles.opened

    def down(j):
        u = w.next()
        pe.e.wait_ge(p.both_tiles.drained, p.mark["hidden"] + 2 * j + 2)
        for t, (half, b) in enumerate(BY_BLOCK):
            for c in range(2):
                f = 2 * j + c
                last = f == FC - 1
                o = c * D + half * 512
                ins = (pe.e.matmul if last else w.mm)(acc[t], p.h1T[:, f, b * P:(b + 1) * P],
                                                      u[:, o:o + 512], start=f == 0, stop=last)
                if last:
                    ins.then_inc(p.dve_tiles.full, 1)
        w.used()
    for j in range(FC // 2):
        for _ in range(2):
            project_columns(p, pe, w, p.hT, p.both_tiles)
        if j:
            down(j - 1)
    down(FC // 2 - 1)
    p.mark["mix3"] = p.dve_tiles.opened
    for _ in range(LAYER_UNITS - w.n):
        w.next()
        w.used()
    w.flush()


def attention_x(p, name, eng, w=None):
    items = X_ITEMS
    n0 = len(HEAD_ITEMS)
    if name == "pe":
        for t in range(len(items) + 2):
            if t < len(items):
                scores_pe(p, eng, w, n0 + t, items[t])
            if t >= 2:
                probs_transpose_pe(p, eng, w, n0 + t - 2, items[t - 2])
                values_pe(p, eng, w, n0 + t - 2, items[t - 2], t)
    elif name == "dve":
        for t in range(len(items) + 1):
            if t < len(items):
                softmax_max_dve(p, eng, n0 + t, items[t])
            if t >= 1:
                softmax_scale_dve(p, eng, n0 + t - 1, items[t - 1])
    else:
        for t in range(len(items) + 2):
            if t >= 2:
                eng.e.wait_ge(p.act_tiles.full, p.act_tiles.turn(eng))
                bank = shaped(p.act_tiles.take(eng), NB, S)
                eng.e.activation(p.pT[t % 2], bank, ACT.Copy).then_inc(p.act_tiles.drained, 1)
            if t < len(items):
                softmax_exp_act(p, eng, n0 + t, items[t])
            if t >= 2:
                h = items[t - 2][1]
                eng.e.wait_ge(p.act_tiles.full, p.act_tiles.turn(eng))
                bank = shaped(p.act_tiles.take(eng), 2, S)
                eng.e.activation(p.mixT[:, 2 * h:2 * h + 2, :], bank, ACT.Copy).then_inc(p.act_tiles.drained, 1)


def layer_act(p, act, l, layer_par):
    act.e.wait_ge(p.sem("layer_params"), l * 16 + 16)
    act.e.dma_start(p.par[:, EARLY_W:LAYER_W], layer_par[bass.ds(l * P, P), EARLY_W:LAYER_W]).then_inc(
        act.event("ffn_params"), 16)
    act.e.wait_ge(p.sem("lambda_sums"), 1)
    act.e.activation(p.lam[:, 0:2], p.lam[:, 0:2], ACT.Exp).then_inc(act.event("lambda_exps"), 1)
    rows_to_columns_evac(p, act, p.hT, p.lp("g_mix_pre"), KC, True)
    for j in range(5):
        act.e.wait_ge(p.act_tiles.full, p.act_tiles.turn(act))
        bank = p.act_tiles.take(act)
        n = 2 if j < 4 else 1
        act.e.activation(p.qk[:, 2 * j:2 * j + n, :], shaped(bank[:, 0:n * S], n, S), ACT.Copy).then_inc(p.act_tiles.drained, 1)
    attention_act(p, act, HEAD_ITEMS, p.mixT, None, {9: lambda: latent_stats_act(p, act), 16: lambda: mla_act(p, act)})
    act.e.wait_ge(p.sem("diff_squares"), 1)
    act.e.activation(p.diff_ss[:, 8:16], p.diff_ss[:, 0:8], ACT.Sqrt, scale=1.0 / 64, bias=p.c("eps")).then_inc(
        act.event("diff_roots"), 1)
    act.e.wait_ge(p.sem("diff_gain"), 1)
    act.e.wait_ge(p.act_tiles.full, p.act_tiles.turn(act))
    bank = p.act_tiles.take(act)
    for c in range(2):
        ins = act.e.activation(p.mixT[:, c, :], bank[:, c * S:(c + 1) * S], ACT.Copy, scale=p.small[:, 200:201])
        if c:
            ins.then_inc(p.act_tiles.drained, 1)
        else:
            ins.then_inc(act.step(), 1)
    residual_act(p, act, 0, BY_HALF)
    rows_to_columns_evac(p, act, p.hT, p.lp("g_x_pre"), KC, True)
    for j in range(4):
        act.e.wait_ge(p.act_tiles.full, p.act_tiles.turn(act))
        bank = p.act_tiles.take(act)
        act.e.activation(p.xqT[:, 2 * j:2 * j + 2, :], shaped(bank, 2, S), ACT.Copy).then_inc(p.act_tiles.drained, 1)
    attention_x(p, "act", act)
    residual_act(p, act, 1, BY_HALF)
    act.e.dma_start(p.par[:, 0:EARLY_W], layer_par[bass.ds(l * P + P, P), 0:EARLY_W]).then_inc(
        p.sem("layer_params"), 16)
    act.e.wait_ge(p.sem("ffn_params"), 16)
    rows_to_columns_evac(p, act, p.hT, p.lp("g_ffn_pre"), KC, True)
    p.both_tiles.taken["act"] = p.mark["hidden"]
    for f in range(FC):
        act.e.wait_ge(p.both_tiles.full, p.both_tiles.turn(act))
        bank = p.both_tiles.take(act)
        if f >= 2:
            act.e.wait_ge(p.both_tiles.drained, p.mark["hidden"] + f - 1)
        act.e.activation(p.silu[:, f % 2, :], bank[:, 0:S], ACT.Silu).then_inc(act.event("silu_ready"), 1)
    residual_act(p, act, 2, BY_BLOCK)


def layer_dve(p, dve, l):
    dve.e.wait_ge(p.sem("layer_params"), l * 16 + 16)
    prod = shaped(p.junk_dve[:, 0:64], 2, 32)
    lam4 = p.lp("lambda", 2, 2, 32)
    dve.e.tensor_tensor(prod, lam4[:, :, 0, :], lam4[:, :, 1, :], ALU.mult).then_inc(dve.step(), 1)
    dve.e.wait_ge(dve.steps, dve.n)
    dve.e.tensor_reduce(p.lam[:, 0:2], prod, AX, ALU.add).then_inc(dve.event("lambda_sums"), 1)
    dve.e.tensor_tensor(p.small[:, 200:201], p.lp("g_diff"), p.lp("lam_rest"), ALU.mult).then_inc(dve.event("diff_gain"), 1)
    dve.e.wait_ge(p.sem("lambda_exps"), 1)
    dve.e.scalar_tensor_tensor(p.lam[:, 0:1], p.lam[:, 0:1], p.lp("lam_init"), p.lam[:, 1:2],
                                      ALU.add, ALU.subtract).then_inc(dve.step(), 1)
    dve.e.wait_ge(dve.steps, dve.n)
    rows_to_columns_evac(p, dve, p.hT, p.lp("g_mix_pre"), KC, False)
    for b in range(NB):
        dve.e.wait_ge(p.dve_tiles.full, p.dve_tiles.turn(dve))
        bank = p.dve_tiles.take(dve)
        dve.e.tensor_copy(p.mla[:, b, :], bank[:, 0:416]).then_inc(p.dve_tiles.drained, 1)
    for b in range(NB):
        dve.e.wait_ge(p.dve_tiles.full, p.dve_tiles.turn(dve))
        bank = p.dve_tiles.take(dve)
        dve.e.tensor_copy(p.v_row[:, b, :], bank[:, 0:384]).then_inc(p.dve_tiles.drained, 1)

    def memory(u):
        if u < 4:
            dve.e.wait_ge(p.dve_tiles.full, p.dve_tiles.turn(dve))
            bank = p.dve_tiles.take(dve)
            dve.e.tensor_copy(p.xkT[:, 2 * u:2 * u + 2, :], shaped(bank, 2, S)).then_inc(p.dve_tiles.drained, 1)
        elif u in (4, 6):
            o = 0 if u == 4 else 512
            for b in range(NB):
                dve.e.wait_ge(p.dve_tiles.full, p.dve_tiles.turn(dve))
                bank = p.dve_tiles.take(dve)
                dve.e.tensor_copy(p.xv[:, b, o:o + 512], bank).then_inc(p.dve_tiles.drained, 1)
    for t in range(len(HEAD_ITEMS) + 1):
        if t == 16:
            mla_dve(p, dve)
        if t < len(HEAD_ITEMS):
            softmax_max_dve(p, dve, t, HEAD_ITEMS[t])
        if t >= 1:
            softmax_scale_dve(p, dve, t - 1, HEAD_ITEMS[t - 1])
        if t >= 2 and has_output(HEAD_ITEMS[t - 2]):
            i = t - 2
            u = beside(HEAD_ITEMS[i], i)
            if u is not None:
                memory(u)
    dve.e.wait_ge(p.act_tiles.drained, p.mark["diff"])
    o4 = p.o_diff.rearrange("p b (h d) -> p (b h) d", d=64)
    sq = shaped(p.junk_dve[:, 0:512], 8, 64)
    dve.e.tensor_tensor(sq, o4, o4, ALU.mult).then_inc(dve.step(), 1)
    dve.e.wait_ge(dve.steps, dve.n)
    dve.e.tensor_reduce(p.diff_ss[:, 0:8], sq, AX, ALU.add).then_inc(dve.event("diff_squares"), 1)
    dve.e.wait_ge(p.sem("diff_roots"), 1)
    dve.e.reciprocal(p.diff_ss[:, 16:24], p.diff_ss[:, 8:16]).then_inc(dve.step(), 1)
    dve.e.wait_ge(dve.steps, dve.n)
    dve.e.tensor_tensor(o4, o4, p.diff_ss[:, 16:24].unsqueeze(2).to_broadcast([P, 8, 64]), ALU.mult).then_inc(dve.event("diff_rows"), 1)
    residual_dve(p, dve, p.lp("g_mix_post"), 0, BY_HALF)
    rows_to_columns_evac(p, dve, p.hT, p.lp("g_x_pre"), KC, False)
    attention_x(p, "dve", dve)
    residual_dve(p, dve, p.lp("g_x_post"), 1, BY_HALF)
    dve.e.wait_ge(p.sem("ffn_params"), 16)
    rows_to_columns_evac(p, dve, p.hT, p.lp("g_ffn_pre"), KC, False)
    for f in range(FC):
        dve.e.wait_ge(p.both_tiles.full, p.both_tiles.turn(dve))
        bank = p.both_tiles.take(dve)
        dve.e.wait_ge(p.sem("silu_ready"), f + 1)
        dve.e.tensor_tensor(p.h1T[:, f, :], p.silu[:, f % 2, :], bank[:, S:2 * S], ALU.mult).then_inc(p.both_tiles.drained, 1)
    residual_dve(p, dve, p.lp("g_ffn_post"), 2, BY_BLOCK)



TWO_PI = 2.0 * math.pi
TURN_HI = 6.28125
TURN_MID = float(np.float32(np.round((TWO_PI - TURN_HI) * 2 ** 21) / 2 ** 21))
TURN_LO = TWO_PI - TURN_HI - TURN_MID
ROUND = 1.5 * 2.0 ** 23
SIN_MAX = 3.1415925


def prologue_dve(p, dve):
    dve.e.wait_ge(p.sem("positions_loaded"), 32)
    posf, posc = p.junk_dve[:, 0:256], p.small[:, 140:142]
    dve.e.tensor_copy(posf, p.pos[:, 0:256]).then_inc(dve.step(), 1)
    dve.e.tensor_copy(posc, p.pos[:, 256:258]).then_inc(dve.step(), 1)
    dve.e.wait_ge(dve.steps, dve.n)
    dve.e.wait_ge(p.sem("const_loaded"), 16)
    for b in range(NB):
        d = p.dist[:, b, :]
        dve.e.tensor_scalar(d, posf, posc[:, b:b + 1], None, ALU.subtract).then_inc(dve.step(), 1)
        dve.e.wait_ge(dve.steps, dve.n)
        dve.e.scalar_tensor_tensor(d, d, -1.0, d, ALU.mult, ALU.max).then_inc(dve.step(), 1)
    ang, turns = shaped(p.junk_dve[:, 256:288], NB, 16), p.junk_dve[:, 320:352]
    flat = p.junk_dve[:, 256:288]
    for b in range(NB):
        dve.e.tensor_scalar(ang[:, b, :], p.c("inv"), posc[:, b:b + 1], None, ALU.mult).then_inc(dve.step(), 1)
    dve.e.wait_ge(dve.steps, dve.n)
    dve.e.tensor_tensor(p.dist_swa, p.dist, p.c("swa_far", NB, S), ALU.add).then_inc(dve.step(), 1)
    for which, quarter in ((0, 0.25), (1, 0.0)):
        red = p.junk_dve[:, 384 + 32 * which:416 + 32 * which]
        dve.e.tensor_scalar(turns, flat, 1.0 / TWO_PI, quarter, ALU.mult, ALU.add).then_inc(dve.step(), 1)
        dve.e.wait_ge(dve.steps, dve.n)
        dve.e.tensor_scalar(turns, turns, ROUND, None, ALU.add).then_inc(dve.step(), 1)
        dve.e.wait_ge(dve.steps, dve.n)
        dve.e.tensor_scalar(turns, turns, ROUND, None, ALU.subtract).then_inc(dve.step(), 1)
        dve.e.wait_ge(dve.steps, dve.n)
        dve.e.scalar_tensor_tensor(red, turns, -TURN_HI, flat, ALU.mult, ALU.add).then_inc(dve.step(), 1)
        dve.e.wait_ge(dve.steps, dve.n)
        dve.e.scalar_tensor_tensor(red, turns, -TURN_MID, red, ALU.mult, ALU.add).then_inc(dve.step(), 1)
        dve.e.wait_ge(dve.steps, dve.n)
        dve.e.scalar_tensor_tensor(red, turns, -TURN_LO, red, ALU.mult, ALU.add).then_inc(dve.step(), 1)
        dve.e.wait_ge(dve.steps, dve.n)
        dve.e.tensor_scalar(red, red, quarter * TWO_PI, SIN_MAX, ALU.add, ALU.min).then_inc(dve.step(), 1)
        dve.e.wait_ge(dve.steps, dve.n)
        dve.e.tensor_scalar(red, red, -SIN_MAX, None, ALU.max).then_inc(dve.event("angles_ready"), 1)
    dve.e.wait_ge(p.sem("mem_root"), 1)
    dve.e.reciprocal(p.rstd, p.rstd).then_inc(dve.step(), 1)
    dve.e.wait_ge(dve.steps, dve.n)
    norm_rows(p, dve, p.xv, p.rstd, p.hrow, "mem_rows")
    dve.e.wait_ge(dve.steps, dve.n)
    for b in range(NB):
        diagonal_dve(p, dve, b, b + 1)
    rows_to_columns_evac(p, dve, p.memT, None, KC, False)


def prologue_act(p, act):
    act.e.wait_ge(p.sem("const_loaded"), 16)
    act.e.wait_ge(p.sem("mem_loaded"), 16)
    norm_stats(p, act, p.xv, D, p.rstd, "mem_root")
    act.e.wait_ge(p.sem("mem_root"), 1)
    act.e.wait_ge(p.sem("x_loaded"), 16)
    pre_norm_act(p, act, BY_BLOCK)
    rows_to_columns_evac(p, act, p.memT, None, KC, True)
    act.e.wait_ge(p.sem("angles_ready"), 2)
    act.e.activation(p.rot.rearrange("p a b c -> p (a b c)"), p.junk_dve[:, 384:448], ACT.Sin).then_inc(act.step(), 1)


def prologue_pe(p, pe, w):
    pe.e.wait_ge(p.sem("const_loaded"), 16)
    rows_to_columns_pe(p, pe, w, p.hrow, KC, "mem", 1)


def layer_pool(p, pool, l):
    pool.e.wait_ge(p.sem("layer_params"), l * 16 + 16)
    pool.e.sem_inc(p.sem("passed"), 1)
    for c in range(KC):
        ins = pool.e.tensor_scalar(p.memgT[:, c, :], p.memT[:, c, :], p.lp("g_x_mem")[:, c:c + 1], None, ALU.mult)
        if c == KC - 1:
            ins.then_inc(pool.event("memory_gained"), 1)



def second_buffers(p):
    p.at = 0
    p.hrow = p.take(NB, D)
    p.y_att = p.arena[:, 0:1024].rearrange("p (c t) -> p c t", c=4)
    p.y_pool = p.arena[:, 1024:2048].rearrange("p (c t) -> p c t", c=4)
    p.hT = p.take(KC, S)
    p.shifted = p.take(15, S)
    mark = p.at
    p.raw = p.take(19, S)
    p.att = p.take(NB, 768)
    p.qk2 = p.take(5, S)
    p.att_sq = p.take(NB, 640)
    p.zp = [p.take(4, 272) for _ in range(2)]
    p.zp_wide = p.arena[:, p.at - 2176:p.at - 128].rearrange("p (c t) -> p c t", c=8)
    p.pooled = p.take(4, S)
    p.sc = [p.take(NB, S) for _ in range(4)]
    p.pr = [p.take(NB, S) for _ in range(4)]
    p.pT = [p.take(NB, S) for _ in range(2)]
    p.gate_out = [p.take(2, S) for _ in range(2)]
    p.at = mark
    p.sig = p.take(2, 4, S)
    p.dec = p.take(2, 4, S)
    p.inv_dec = p.take(2, 4, S)
    p.iclr = p.take(2, 4, S)
    p.kd = p.take(4, S)
    p.kk = p.take(4, S)
    p.ksum = p.take(4, S)
    p.gate = p.sig[:, 0]
    p.alpha_rho = p.arena[:, mark:mark + 4096].rearrange("p (w e q t) -> p w e q t", w=2, e=2, q=4)
    BETA, KAPPA, rest = [], [], []
    for _ in range(2):
        BETA.append(p.take(8, 2, CH))
        KAPPA.append(p.take(8, 2, CH))
    for _ in range(5):
        rest.append(p.take(8, CH))
    hT, low = flat(p.hT), flat(p.shifted)
    far, cnt = CONST["swa_far"][0], CONST["pool_cnt"][0]
    for buffer, at in ((hT, 0), (hT, 512), (hT, 1024), (hT, 1536), (low, 3072), (p.par, SECOND_W),
                       (p.par, SECOND_W + 512), (p.const, far), (p.const, cnt), (p.const, cnt + 512)):
        rest.append(shaped(buffer[:, at:at + 512], 8, CH))
    p.BETA, p.KAPPA = BETA, KAPPA
    p.X, p.XT, p.Pb, p.Br, p.Kr, p.Vr = [rest[2 * j:2 * j + 2] for j in range(6)]
    p.U, p.ST = rest[12:14]
    p.keys_0 = shaped(flat(BETA[0]), 4, S)
    p.at = mark
    p.gates = p.take(24, S)
    pass
    p.merged = p.take(KC, S)
    assert p.at <= mark + 4 * 2048
    p.prod = shaped(flat(p.kd)[:, 0:2 * S], 2, S)
    p.junk_act = p.arena[:, mark:mark + D]
    p.at = mark
    p.sel = p.take(NB, E_N * CAP)
    p.selw = p.take(NB, E_N * CAP)
    p.sel_g = p.take(NB, P)
    p.selw_g = p.take(NB, P)
    p.xg = p.take(KC, P)
    p.back = p.take(S)
    p.silu_e = p.take(512)
    p.h1 = [p.take(512) for _ in range(2)]
    p.h1g = p.take(KC, P)
    p.y_e = [p.take(512) for _ in range(2)]
    p.aff = p.take(NB, E_N)
    p.posT = p.take(NB, E_N)
    p.affT, p.mask, p.cum, p.ones = [p.take(S) for _ in range(4)]
    p.top = p.take(8)
    assert p.at <= p.arena_w - (EXPERT_SLOTS - SLOTS) * UNIT
    p.gt = p.small[:, 204:236]
    p.cols = p.small[:, 112:112 + 15 + 4]
    p.att_ss = p.small[:, 140:200]


def flat(ap):
    names = "abcd"[:len(ap.shape) - 1]
    return ap.rearrange(f"p {' '.join(names)} -> p ({' '.join(names)})")


def chunk_of(e, c):
    return c if e == 0 else NCH - 1 - c


def columns_of(c):
    return [slice(chunk_of(e, c) * CH, chunk_of(e, c) * CH + CH) for e in range(2)]


def each_head():
    for e in range(2):
        for q in range(PAIRS):
            for par in range(2):
                yield e, q, slice(64 * par, 64 * par + 64), e * PAIRS + q


def head_products(p, pe, tiles, terms):
    if tiles.opened >= tiles.size:
        pe.e.wait_ge(tiles.drained, tiles.opened - tiles.size + 1)
    bank = shaped(tiles.open(pe), 8, CH)
    for e, q, r, o in each_head():
        ts = terms(e, q, r, o)
        for j, (a, b) in enumerate(ts):
            ins = pe.e.matmul(bank[r, o, :], a, b, start=j == 0, stop=j == len(ts) - 1)
    ins.then_inc(tiles.full, 1)


def level_columns(ap, n, bit):
    return ap.rearrange("p h (g two s) -> p h g two s", two=2, s=1 << n)[:, :, :, bit, :]


def level_product(p, pe, tiles, n, other, left, right):
    if tiles.opened >= tiles.size:
        pe.e.wait_ge(tiles.drained, tiles.opened - tiles.size + 1)
    bank = shaped(tiles.open(pe)[:, 0:8 * CH // 2], 8, CH // 2)
    for e, q, r, o in each_head():
        rhs = level_columns(right[:, o:o + 1, :], n, e ^ other)[r, 0]
        ins = pe.e.matmul(bank[r, o, :].rearrange("p (g s) -> p g s", s=1 << n), left[r, o, :], rhs)
    ins.then_inc(tiles.full, 1)


def level_tile(bank, n, e):
    return bank[:, e * 4 * CH // 2:(e + 1) * 4 * CH // 2].rearrange("p (h g s) -> p h g s", h=4, s=1 << n)


def second_pe(p, pe, w):
    w.start(16 * DEPTH * LAYER_UNITS // SLOTS, p.slots, p.slot_loaded, p.slots_free)
    normed_columns_pe(p, pe, w, None)
    pe.e.wait_ge(p.sem("layer_params"), 16 * (DEPTH + 1))
    columns_ready(p, pe)
    for _ in range(3):
        project_rows(p, pe, w, p.hT, p.dve_tiles, 256, 1)
    for j in range(10):
        project_columns(p, pe, w, p.hT, p.act_tiles, 2 if j < 9 else 1)
    p.mark["raw"] = p.act_tiles.opened
    rows_to_columns_pe(p, pe, w, p.att, 5, "qk", 1)
    columns_ready(p, pe)
    attention_pe(p, pe, w, GQA_ITEMS, lambda _: project_columns(p, pe, w, p.hT, p.act_tiles))
    pe.e.wait_ge(p.sem("pooled"), 1)
    for j in range(2):
        if p.act_tiles.opened >= p.act_tiles.size:
            pe.e.wait_ge(p.act_tiles.drained, p.act_tiles.opened - p.act_tiles.size + 1)
        bank = p.act_tiles.open(pe)
        for c in range(2):
            g = 2 * j + c
            ins = pe.e.matmul(bank[:, c * S:(c + 1) * S], p.sp("pool_w", 4, P)[:, g, :], p.pooled[:, g, :])
        ins.then_inc(p.act_tiles.full, 1)
    p.mark["pool"] = p.act_tiles.opened
    for _ in range(2):
        project_columns(p, pe, w, p.hT, p.act_tiles)
    pe.e.wait_ge(p.sem("lora_in"), 1)
    for name, src in (("w2", 12), ("a2", 13)):
        for e in range(2):
            for j in range(2):
                if p.act_tiles.opened >= p.act_tiles.size:
                    pe.e.wait_ge(p.act_tiles.drained, p.act_tiles.opened - p.act_tiles.size + 1)
                bank = p.act_tiles.open(pe)
                r = slice(64 * e, 64 * e + 64)
                for c in range(2):
                    q = 2 * j + c
                    ins = pe.e.matmul(bank[:, c * S:(c + 1) * S], p.sp(name)[r, q * P:(q + 1) * P],
                                      p.shifted[r, src, :])
                ins.then_inc(p.act_tiles.full, 1)

    def head_sums(src, event, n):
        pe.e.wait_ge(p.sem(event), n)
        for j in range(2):
            if p.dve_tiles.opened >= p.dve_tiles.size:
                pe.e.wait_ge(p.dve_tiles.drained, p.dve_tiles.opened - p.dve_tiles.size + 1)
            bank = p.dve_tiles.open(pe)
            pe.e.matmul(bank, p.c("headsum"), flat(src)[:, j * 512:(j + 1) * 512]).then_inc(p.dve_tiles.full, 1)
    head_sums(p.kd, "squares", 1)
    for _ in range(2):
        project_columns(p, pe, w, p.hT, p.act_tiles)
    pe.e.wait_ge(p.sem("recurrence_in"), 1)
    pe.e.wait_ge(p.sem("alpha_ready"), 1)
    alpha, rho, beta, kappa = p.sig, p.dec, p.iclr, p.inv_dec
    eye = p.c("eye64")
    for m in range(NCH // 2):
        for i in range(2):
            cols = columns_of(2 * m + i)
            for e in range(2):
                for left in (beta, kappa):
                    if p.dve_tiles.opened >= p.dve_tiles.size:
                        pe.e.wait_ge(p.dve_tiles.drained, p.dve_tiles.opened - p.dve_tiles.size + 1)
                    bank = shaped(p.dve_tiles.open(pe), 4, 2, CH)
                    for q in range(PAIRS):
                        for par in range(2):
                            r = slice(64 * par, 64 * par + 64)
                            ins = pe.e.matmul(bank[r, q], left[r, e, q, cols[e]], p.alpha_rho[r, :, e, q, cols[e]])
                    ins.then_inc(p.dve_tiles.full, 1)
            head_products(p, pe, p.act_tiles, lambda e, q, r, o: [(p.shifted[r, 8 + q, cols[e]], eye[r, :])])
            head_products(p, pe, p.act_tiles, lambda e, q, r, o: [(beta[r, e, q, cols[e]], eye[r, :])])
            head_products(p, pe, p.act_tiles, lambda e, q, r, o: [(kappa[r, e, q, cols[e]], eye[r, :])])
        if m == 0:
            head_sums(p.kd, "bonus_in", 1)
        for n in range(6):
            for i in range(2):
                pe.e.wait_ge(p.sem("level_masked"), 12 * m + 2 * n + i + 1)
                if n == 0:
                    head_products(p, pe, p.dve_tiles, lambda e, q, r, o: [(p.Pb[i][r, o, :], eye[r, :])])
                else:
                    level_product(p, pe, p.act_tiles, n, 0, p.Pb[i], p.X[i])
                    p.mark[f"P{i}"] = p.act_tiles.opened
            for i in range(2 if n else 0):
                pe.e.wait_ge(p.act_tiles.drained, p.mark[f"P{i}"])
                if n < 5:
                    level_product(p, pe, p.dve_tiles, n, 0, p.XT[i], p.Pb[i])
                level_product(p, pe, p.dve_tiles, n, 1, p.Pb[i], p.XT[i])
        for i in range(2):
            c = 2 * m + i
            cols = columns_of(c)
            pe.e.wait_ge(p.dve_tiles.drained, p.dve_tiles.opened)
            pe.e.wait_ge(p.sem("state_ready"), c + 1)
            head_products(p, pe, p.act_tiles, lambda e, q, r, o: [(alpha[r, e, q, cols[e]], p.ST[r, o, :]),
                                                                  (p.KAPPA[i][r, o, 0, :], p.Vr[i][r, o, :])])
            pe.e.wait_ge(p.act_tiles.drained, p.act_tiles.opened)
            head_products(p, pe, p.act_tiles, lambda e, q, r, o: [(p.XT[i][r, o, :], p.Pb[i][r, o, :])])
            pe.e.wait_ge(p.act_tiles.drained, p.act_tiles.opened)
            head_products(p, pe, p.dve_tiles, lambda e, q, r, o: [(p.Br[i][r, o, :], p.U[r, o, :]),
                                                                  (p.Kr[i][r, o, :], p.Vr[i][r, o, :])])
            head_products(p, pe, p.act_tiles, lambda e, q, r, o: [(p.ST[r, o, :], rho[r, e, q, cols[e]]),
                                                                  (p.U[r, o, :], p.BETA[i][r, o, 1, :]),
                                                                  (p.Vr[i][r, o, :], p.KAPPA[i][r, o, 1, :])])
            p.mark[f"y{c}"] = p.act_tiles.opened
    for j in range(2):
        if p.act_tiles.opened >= p.act_tiles.size:
            pe.e.wait_ge(p.act_tiles.drained, p.act_tiles.opened - p.act_tiles.size + 1)
        bank = p.act_tiles.open(pe)
        for c in range(2):
            q = 2 * j + c
            ins = pe.e.matmul(bank[:, c * S:(c + 1) * S], p.sp("g2")[:, q * P:(q + 1) * P], p.shifted[:, 14, :])
        ins.then_inc(p.act_tiles.full, 1)
    head_sums(p.kd, "y_sum", 1)
    head_sums(p.kk, "y_sum", 2)
    branches = [p.y_pool, p.y_att, p.ksum]
    for n in range(6):
        if n == 4:
            pe.e.wait_ge(p.sem("y_rwkv"), 1)
        u = w.next()
        for t in range(2):
            if p.dve_tiles.opened >= p.dve_tiles.size:
                pe.e.wait_ge(p.dve_tiles.drained, p.dve_tiles.opened - p.dve_tiles.size + 1)
            bank = p.dve_tiles.open(pe)
            for c in range(2):
                i = 4 * n + 2 * t + c
                for k in range(4):
                    o = ((2 * t + c) * 4 + k) * P
                    last = c == 1 and k == 3
                    ins = (pe.e.matmul if last else w.mm)(bank[:, c * S:(c + 1) * S], u[:, o:o + P],
                                                          branches[i // 8][:, k, :], start=k == 0, stop=k == 3)
            ins.then_inc(p.dve_tiles.full, 1)
        w.used()
    pe.e.wait_ge(p.sem("merged"), 1)
    for _ in range(2):
        project_rows(p, pe, w, p.merged, p.dve_tiles, 512)
    p.mark["mixed"] = p.dve_tiles.opened
    normed_columns_pe(p, pe, w, 0)
    columns_ready(p, pe)
    if p.dve_tiles.opened >= p.dve_tiles.size:
        pe.e.wait_ge(p.dve_tiles.drained, p.dve_tiles.opened - p.dve_tiles.size + 1)
    bank = p.dve_tiles.open(pe)
    for b in range(NB):
        for k in range(KC):
            ins = pe.e.matmul(bank[:, b * E_N:(b + 1) * E_N], p.hT[:, k, b * P:(b + 1) * P],
                              p.sp("router", KC, E_N)[:, k, :], start=k == 0, stop=k == KC - 1)
    ins.then_inc(p.dve_tiles.full, 1)
    pe.e.wait_ge(p.sem("affinities"), 1)
    if p.dve_tiles.opened >= p.dve_tiles.size:
        pe.e.wait_ge(p.dve_tiles.drained, p.dve_tiles.opened - p.dve_tiles.size + 1)
    bank = p.dve_tiles.open(pe)
    for b in range(NB):
        ins = pe.e.transpose(bank[0:E_N, b * P:(b + 1) * P], p.aff[:, b, :], p.c("ident"))
    ins.then_inc(p.dve_tiles.full, 1)
    pe.e.wait_ge(p.sem("slots"), 1)
    if p.dve_tiles.opened >= p.dve_tiles.size:
        pe.e.wait_ge(p.dve_tiles.drained, p.dve_tiles.opened - p.dve_tiles.size + 1)
    bank = p.dve_tiles.open(pe)
    for b in range(NB):
        ins = pe.e.transpose(bank[:, b * E_N:(b + 1) * E_N], p.cum[0:E_N, b * P:(b + 1) * P],
                             p.c("ident")[0:E_N, 0:E_N])
    ins.then_inc(p.dve_tiles.full, 1)
    w.flush()
    pe.finish("second", 0)
    p.reset_rings("pe")
    with pe.e.Fori(0, G_N) as g:
        w.start(g * (16 * GROUP_UNITS // EXPERT_SLOTS), p.expert_slots, p.expert_slot_loaded, p.expert_slots_used)
        experts_pe(p, pe, w)
        pe.finish("experts", g)
        p.reset_rings("pe")


def expert_product(p, pe, w, src, tiles):
    if tiles.opened >= tiles.size:
        pe.e.wait_ge(tiles.drained, tiles.opened - tiles.size + 1)
    bank = tiles.open(pe)
    for h in range(2):
        us = [w.next() for _ in range(GE)]
        for k in range(4):
            for e in range(GE):
                r = slice(CAP * e, CAP * e + CAP)
                last = h == 1 and k == 3 and e == GE - 1
                ins = (pe.e.matmul if last else w.mm)(bank[r, :], src[:, 4 * h + k, r],
                                                      us[e][:, k * 512:(k + 1) * 512],
                                                      start=h == 0 and k == 0, stop=h == 1 and k == 3)
        w.used(GE)
    ins.then_inc(tiles.full, 1)


def experts_pe(p, pe, w):
    pe.e.wait_ge(p.sem("group_selected"), 1)
    for j in range(2):
        if p.act_tiles.opened >= p.act_tiles.size:
            pe.e.wait_ge(p.act_tiles.drained, p.act_tiles.opened - p.act_tiles.size + 1)
        bank = shaped(p.act_tiles.open(pe), 4, P)
        for c in range(4):
            for b in range(NB):
                ins = pe.e.matmul(bank[:, c, :], p.hrow[:, b, (4 * j + c) * P:(4 * j + c + 1) * P],
                                  p.sel_g[:, b, :], start=b == 0, stop=b == NB - 1)
        ins.then_inc(p.act_tiles.full, 1)
    if p.dve_tiles.opened >= p.dve_tiles.size:
        pe.e.wait_ge(p.dve_tiles.drained, p.dve_tiles.opened - p.dve_tiles.size + 1)
    bank = p.dve_tiles.open(pe)
    for b in range(NB):
        ins = pe.e.transpose(bank[:, b * P:(b + 1) * P], p.selw_g[:, b, :], p.c("ident"))
    ins.then_inc(p.dve_tiles.full, 1)
    pe.e.wait_ge(p.act_tiles.drained, p.act_tiles.opened)
    for f in range(2):
        expert_product(p, pe, w, p.xg, p.act_tiles)
        expert_product(p, pe, w, p.xg, p.dve_tiles)
        pe.e.wait_ge(p.dve_tiles.drained, p.dve_tiles.opened)
        if p.act_tiles.opened >= p.act_tiles.size:
            pe.e.wait_ge(p.act_tiles.drained, p.act_tiles.opened - p.act_tiles.size + 1)
        bank = p.act_tiles.open(pe)
        for c in range(4):
            ins = w.transpose(bank[:, c * P:(c + 1) * P], p.h1[f][:, c * P:(c + 1) * P], p.c("ident")) if c < 3 else \
                pe.e.transpose(bank[:, c * P:(c + 1) * P], p.h1[f][:, c * P:(c + 1) * P], p.c("ident"))
        ins.then_inc(p.act_tiles.full, 1)
    pe.e.wait_ge(p.act_tiles.drained, p.act_tiles.opened)
    for f in range(2):
        expert_product(p, pe, w, p.h1g, p.act_tiles)
        pe.e.wait_ge(p.act_tiles.drained, p.act_tiles.opened)
        for b in range(NB):
            if p.dve_tiles.opened >= p.dve_tiles.size:
                pe.e.wait_ge(p.dve_tiles.drained, p.dve_tiles.opened - p.dve_tiles.size + 1)
            bank = p.dve_tiles.open(pe)
            pe.e.matmul(bank, p.back[:, b * P:(b + 1) * P], p.y_e[f]).then_inc(p.dve_tiles.full, 1)
    w.flush()


def experts_act(p, act):
    for j in range(2):
        act.e.wait_ge(p.act_tiles.full, p.act_tiles.turn(act))
        bank = shaped(p.act_tiles.take(act), 4, P)
        for c in range(4):
            g = p.sp("g_ffn")[:, 4 * j + c:4 * j + c + 1]
            ins = act.e.activation(p.xg[:, 4 * j + c, :], bank[:, c, :], ACT.Copy, scale=g)
            if c == 3:
                ins.then_inc(p.act_tiles.drained, 1)
            else:
                ins.then_inc(act.step(), 1)
    for f in range(2):
        act.e.wait_ge(p.act_tiles.full, p.act_tiles.turn(act))
        bank = p.act_tiles.take(act)
        if f:
            act.e.wait_ge(p.dve_tiles.drained, 2)
        act.e.activation(p.silu_e, bank, ACT.Silu).then_inc(p.act_tiles.drained, 1)
        act.e.wait_ge(p.act_tiles.full, p.act_tiles.turn(act))
        bank = shaped(p.act_tiles.take(act), 4, P)
        act.e.activation(p.h1g[:, 4 * f:4 * f + 4, :], bank, ACT.Copy).then_inc(p.act_tiles.drained, 1)
    for f in range(2):
        act.e.wait_ge(p.act_tiles.full, p.act_tiles.turn(act))
        bank = p.act_tiles.take(act)
        act.e.activation(p.y_e[f], bank, ACT.Copy).then_inc(p.act_tiles.drained, 1)


def experts_dve(p, dve, g):
    dve.e.tensor_copy(p.selw_g, p.selw[:, :, bass.ds(g * P, P)]).then_inc(dve.step(), 1)
    dve.e.wait_ge(dve.steps, dve.n)
    dve.e.tensor_copy(p.sel_g, p.sel[:, :, bass.ds(g * P, P)]).then_inc(dve.event("group_selected"), 1)
    dve.e.wait_ge(p.dve_tiles.full, p.dve_tiles.turn(dve))
    bank = p.dve_tiles.take(dve)
    dve.e.tensor_copy(p.back, bank[:, 0:S]).then_inc(p.dve_tiles.drained, 1)
    for f in range(2):
        dve.e.wait_ge(p.dve_tiles.full, p.dve_tiles.turn(dve))
        bank = p.dve_tiles.take(dve)
        dve.e.wait_ge(p.act_tiles.drained, 3 + 2 * f)
        dve.e.tensor_tensor(p.h1[f], p.silu_e, bank, ALU.mult).then_inc(p.dve_tiles.drained, 1)
    for f in range(2):
        for b in range(NB):
            dve.e.wait_ge(p.dve_tiles.full, p.dve_tiles.turn(dve))
            bank = p.dve_tiles.take(dve)
            x = p.x[:, b, f * 512:(f + 1) * 512]
            dve.e.tensor_tensor(x, x, bank, ALU.add).then_inc(p.dve_tiles.drained, 1)
    dve.e.wait_ge(p.dve_tiles.drained, p.dve_tiles.taken["dve"])


def second_act(p, act):
    act.e.wait_ge(p.sem("layer_params"), 16 * (DEPTH + 1))
    rows_to_columns_evac(p, act, p.hT, p.sp("g_mix"), KC, True)
    for j in range(10):
        n = 2 if j < 9 else 1
        act.e.wait_ge(p.act_tiles.full, p.act_tiles.turn(act))
        bank = p.act_tiles.take(act)
        ins = act.e.activation(p.raw[:, 2 * j:2 * j + n, :], shaped(bank[:, 0:n * S], n, S), ACT.Copy)
        ins.then_inc(p.act_tiles.drained, 1)
        if j == 1:
            act.e.wait_ge(p.sem("att_squares"), 1)
            act.e.activation(p.att_ss[:, 20:40], p.att_ss[:, 0:20], ACT.Sqrt, scale=1.0 / 64, bias=p.c("eps")).then_inc(
                act.event("att_roots"), 1)

    def gate_unit(_):
        j = p.gates_out
        p.gates_out += 1
        act.e.wait_ge(p.act_tiles.full, p.act_tiles.turn(act))
        bank = shaped(p.act_tiles.take(act), 2, S)
        if j >= 2:
            act.e.wait_ge(p.sem(f"gate_stored_{j % 2}"), 16 * (j // 2))
        act.e.activation(p.gate_out[j % 2], bank, ACT.Copy).then_inc(p.act_tiles.drained, 1)
        act.e.wait_ge(p.act_tiles.drained, p.act_tiles.taken["act"])
        act.e.dma_start(p.gate_dram[j], flat(p.gate_out[j % 2])).then_inc(p.sem(f"gate_stored_{j % 2}"), 16)
    p.gates_out = 0
    rows_to_columns_evac(p, act, p.qk2, None, 5, True)
    attention_act(p, act, GQA_ITEMS, p.y_att, gate_unit)
    for j in range(2):
        act.e.wait_ge(p.act_tiles.full, p.act_tiles.turn(act))
        bank = p.act_tiles.take(act)
        for c in range(2):
            g = 2 * j + c
            ins = act.e.activation(p.y_pool[:, g, :], bank[:, c * S:(c + 1) * S], ACT.Copy,
                                   scale=p.sp("pool_scale")[:, g:g + 1])
            if c:
                ins.then_inc(p.act_tiles.drained, 1)
            else:
                ins.then_inc(act.step(), 1)
    gate_unit(8)
    act.e.wait_ge(p.sem("shift_done"), 1)
    act.e.activation(p.shifted[:, 12, :], p.shifted[:, 12, :], ACT.Tanh).then_inc(act.step(), 1)
    act.e.activation(p.shifted[:, 14, :], p.shifted[:, 14, :], ACT.Sigmoid).then_inc(act.event("lora_in"), 1)
    gate_unit(9)
    for name, dst in (("w0", p.sig), ("a0", p.iclr)):
        for e in range(2):
            for j in range(2):
                act.e.wait_ge(p.act_tiles.full, p.act_tiles.turn(act))
                bank = p.act_tiles.take(act)
                for c in range(2):
                    q = 2 * j + c
                    ins = act.e.activation(dst[:, e, q, :], bank[:, c * S:(c + 1) * S], ACT.Sigmoid,
                                           bias=p.sp(name)[:, e * 4 + q:e * 4 + q + 1])
                    if c:
                        ins.then_inc(p.act_tiles.drained, 1)
                    else:
                        ins.then_inc(act.step(), 1)
        p.mark[name] = p.act_tiles.taken["act"]
    act.e.wait_ge(p.sem("norms_in"), 1)
    act.e.activation(flat(p.kd), flat(p.kd), ACT.Ln).then_inc(act.step(), 1)
    act.e.wait_ge(act.steps, act.n)
    act.e.activation(flat(p.kd), flat(p.kd), ACT.Exp, scale=-0.5).then_inc(act.event("norms_out"), 1)
    act.e.wait_ge(p.sem("sums_ready"), 1)
    act.e.activation(flat(p.inv_dec), flat(p.dec), ACT.Exp, scale=DECAY).then_inc(act.event("decays_ready"), 1)
    act.e.wait_ge(p.sem("decays_ready"), 1)
    act.e.activation(flat(p.dec), flat(p.dec), ACT.Exp, scale=-DECAY).then_inc(act.event("decays_ready"), 1)
    act.e.activation(flat(p.sig), flat(p.sig), ACT.Exp, scale=-DECAY).then_inc(act.event("decays_ready"), 1)
    gate_unit(10)
    gate_unit(11)

    def copy_out(dst, scale=1.0):
        act.e.wait_ge(p.act_tiles.full, p.act_tiles.turn(act))
        bank = shaped(p.act_tiles.take(act), 8, CH)
        act.e.activation(dst, bank, ACT.Copy, scale=scale).then_inc(p.act_tiles.drained, 1)
    for j in range(2):
        act.e.wait_ge(p.sem(f"gate_stored_{j}"), 16 * 6)
    for m in range(NCH // 2):
        for i in range(2):
            copy_out(p.Vr[i])
            copy_out(p.Br[i])
            copy_out(p.Kr[i])
        for n in range(1, 6):
            for i in range(2):
                act.e.wait_ge(p.act_tiles.full, p.act_tiles.turn(act))
                bank = p.act_tiles.take(act)
                for e in range(2):
                    ins = act.e.activation(level_columns(p.Pb[i][:, 4 * e:4 * e + 4], n, e), level_tile(bank, n, e), ACT.Copy)
                    if e:
                        ins.then_inc(p.act_tiles.drained, 1)
                    else:
                        ins.then_inc(act.step(), 1)
        for i in range(2):
            cols = columns_of(2 * m + i)
            copy_out(p.Pb[i])
            copy_out(p.U, -1.0)
            act.e.wait_ge(p.act_tiles.full, p.act_tiles.turn(act))
            bank = shaped(p.act_tiles.take(act), 2, 4, CH)
            act.e.activation(p.kd[:, :, cols[0]], bank[:, 0], ACT.Copy).then_inc(act.step(), 1)
            act.e.activation(p.kk[:, :, cols[1]], bank[:, 1], ACT.Copy).then_inc(p.act_tiles.drained, 1)
    gates_sb = p.gates.rearrange("p (n c) t -> p n (c t)", n=12)
    gates_dram = p.gate_dram.rearrange("n p w -> p n w")
    for b in BRANCH_ORDER[:2]:
        act.e.dma_start(gates_sb[:, 4 * b:4 * b + 4], gates_dram[:, 4 * b:4 * b + 4]).then_inc(
            act.event(f"gates_loaded_{b}"), 16)
    for j in range(2):
        act.e.wait_ge(p.act_tiles.full, p.act_tiles.turn(act))
        bank = shaped(p.act_tiles.take(act), 2, S)
        act.e.activation(p.gate[:, 2 * j:2 * j + 2, :], bank, ACT.Copy).then_inc(p.act_tiles.drained, 1)
    act.e.wait_ge(p.sem("variances_in"), 1)
    act.e.activation(flat(p.kk), flat(p.kk), ACT.Ln, scale=1.0 / 64, bias=p.c("ln_eps")).then_inc(act.step(), 1)
    act.e.wait_ge(act.steps, act.n)
    act.e.activation(flat(p.kk), flat(p.kk), ACT.Exp, scale=-0.5).then_inc(act.event("y_rstd"), 1)
    for b in BRANCH_ORDER:
        if b == BRANCH_ORDER[-1]:
            act.e.wait_ge(p.sem("y_rwkv"), 1)
            act.e.sem_inc(p.sem("recurrence_left"), 1)
            act.e.dma_start(gates_sb[:, 4 * b:4 * b + 4], gates_dram[:, 4 * b:4 * b + 4]).then_inc(
                act.event(f"gates_loaded_{b}"), 16)
        act.e.wait_ge(p.sem(f"gates_loaded_{b}"), 16)
        g = flat(p.gates[:, 8 * b:8 * b + 8, :])
        act.e.activation(g, g, ACT.Sigmoid).then_inc(act.event("gates_ready"), 1)
    pre_norm_act(p, act, BY_HALF, p.dve_tiles.drained, [p.mark["mixed"] - 3 + t for t in range(4)])
    rows_to_columns_evac(p, act, p.hT, p.sp("g_ffn"), KC, True)
    act.e.wait_ge(p.sem("logits"), 1)
    for b in range(NB):
        ins = act.e.activation(p.aff[:, b, :], p.aff[:, b, :], ACT.Exp, bias=p.cols[:, 2 + b:3 + b],
                               accum_out=p.cols[:, 4 + b:5 + b])
        if b:
            ins.then_inc(act.event("affinity_exps"), 1)
        else:
            ins.then_inc(act.step(), 1)
    act.finish("second", 0)
    p.reset_rings("act")
    with act.e.Fori(0, G_N) as g:
        experts_act(p, act)
        act.finish("experts", g)
        p.reset_rings("act")
    norm_stats(p, act, p.x, D, p.pre_rstd, "final_root")


def second_dve(p, dve):
    e_ = dve.e
    dve.e.wait_ge(p.sem("layer_params"), 16 * (DEPTH + 1))
    rows_to_columns_evac(p, dve, p.hT, p.sp("g_mix"), KC, False)
    for j in range(3):
        for b in range(NB):
            dve.e.wait_ge(p.dve_tiles.full, p.dve_tiles.turn(dve))
            bank = p.dve_tiles.take(dve)
            e_.tensor_copy(p.att[:, b, j * 256:(j + 1) * 256], bank[:, 0:256]).then_inc(p.dve_tiles.drained, 1)
    dve.e.wait_ge(p.dve_tiles.drained, p.dve_tiles.taken["dve"])
    qk = p.att[:, :, 0:640]
    e_.tensor_tensor(p.att_sq, qk, qk, ALU.mult).then_inc(dve.step(), 1)
    dve.e.wait_ge(dve.steps, dve.n)
    e_.tensor_reduce(p.att_ss[:, 0:20], p.att_sq.rearrange("p b (h d) -> p (b h) d", d=64), AX, ALU.add).then_inc(dve.event("att_squares"), 1)
    dve.e.wait_ge(p.sem("att_roots"), 1)
    e_.reciprocal(p.att_ss[:, 40:60], p.att_ss[:, 20:40]).then_inc(dve.step(), 1)
    dve.e.wait_ge(dve.steps, dve.n)
    for b in range(NB):
        h = qk[:, b, :].rearrange("p (h d) -> p h d", d=64)
        rs = p.att_ss[:, 40 + 10 * b:50 + 10 * b].unsqueeze(2).to_broadcast([P, 10, 64])
        e_.tensor_tensor(h, h, rs, ALU.mult).then_inc(dve.step(), 1)
        dve.e.wait_ge(dve.steps, dve.n)
        e_.tensor_tensor(h[:, 0:8], h[:, 0:8], spread(p.sp("q_norm"), 1, 8), ALU.mult).then_inc(dve.step(), 1)
        e_.tensor_tensor(h[:, 8:10], h[:, 8:10], spread(p.sp("k_norm"), 1, 2), ALU.mult).then_inc(dve.step(), 1)
        dve.e.wait_ge(dve.steps, dve.n)
        pairs = qk[:, b, :].rearrange("p (h d two) -> p two h d", d=32, two=2)
        cos = spread(p.c("cos", NB, 32)[:, b, :], 1, 10)
        sin = spread(p.c("sin", NB, 32)[:, b, :], 1, 10)
        sq = flat(p.att_sq)
        tmp = [shaped(sq[:, j * 320:(j + 1) * 320], 10, 32) for j in range(4)]
        rotate(p, dve, (pairs[:, 0], pairs[:, 1]), pairs[:, 0], pairs[:, 1], cos, sin, tmp)
        dve.e.wait_ge(dve.steps, dve.n)
    e_.tensor_copy(p.small[:, 255:256], p.c("eps")).then_inc(dve.event("qk_rows"), 1)
    rows_to_columns_evac(p, dve, p.qk2, None, 5, False)
    attention_dve(p, dve, GQA_ITEMS)
    dve.e.wait_ge(p.sem("shift_done"), 1)
    dve.e.wait_ge(p.act_tiles.drained, p.mark["pool"])
    r, k, v = p.shifted[:, 0:4, :], p.shifted[:, 4:8, :], p.shifted[:, 8:12, :]
    for q in range(PAIRS):
        e_.tensor_scalar(p.kk[:, q, :], k[:, q, :], p.sp("k_k")[:, q:q + 1], None, ALU.mult).then_inc(dve.step(), 1)
    dve.e.wait_ge(dve.steps, dve.n)
    e_.tensor_tensor(p.kd, p.kk, p.kk, ALU.mult).then_inc(dve.event("squares"), 1)
    dve.e.wait_ge(p.act_tiles.drained, p.mark["w0"])
    for e in range(2):
        for q in range(PAIRS):
            o, s = p.dec[:, e, q, :], p.sig[:, e, q, :]
            if e:
                o, s = o[:, ::-1], s[:, ::-1]
            e_.tensor_tensor_scan(o, p.c("scan_keep"), s, 0.0, ALU.mult, ALU.add).then_inc(dve.step(), 1)
    dve.e.wait_ge(dve.steps, dve.n)
    e_.tensor_tensor(flat(p.sig), flat(p.dec), flat(p.sig), ALU.subtract).then_inc(dve.event("sums_ready"), 1)
    for j in range(2):
        dve.e.wait_ge(p.dve_tiles.full, p.dve_tiles.turn(dve))
        bank = shaped(p.dve_tiles.take(dve), 2, S)
        e_.tensor_scalar(p.kd[:, 2 * j:2 * j + 2, :], bank, 1e-24, None, ALU.max).then_inc(p.dve_tiles.drained, 1)
    dve.e.wait_ge(p.dve_tiles.drained, p.dve_tiles.taken["dve"])
    e_.tensor_scalar(p.small[:, 255:256], p.c("eps"), 1.0, None, ALU.mult).then_inc(dve.event("norms_in"), 1)
    dve.e.wait_ge(p.act_tiles.drained, p.mark["a0"])
    one_less = p.cols[:, 15:19]
    e_.tensor_scalar(one_less, p.sp("k_a"), -1.0, 1.0, ALU.mult, ALU.add).then_inc(dve.step(), 1)
    dve.e.wait_ge(dve.steps, dve.n)
    k_of = [p.keys_0, p.ksum]
    for e in range(2):
        for q in range(PAIRS):
            e_.tensor_scalar(k_of[e][:, q, :], p.iclr[:, e, q, :], p.sp("k_a")[:, q:q + 1],
                             one_less[:, q:q + 1], ALU.mult, ALU.add).then_inc(dve.step(), 1)
    dve.e.wait_ge(dve.steps, dve.n)
    for e in range(2):
        e_.tensor_tensor(k_of[e], k_of[e], k, ALU.mult).then_inc(dve.step(), 1)
    dve.e.wait_ge(p.sem("norms_out"), 1)
    e_.tensor_tensor(p.kk, p.kk, p.kd, ALU.mult).then_inc(dve.event("keys_normed"), 1)
    dve.e.wait_ge(p.sem("keys_normed"), 1)
    for e in range(2):
        e_.tensor_tensor(p.iclr[:, e], p.iclr[:, e], p.kk, ALU.mult).then_inc(dve.step(), 1)
    dve.e.wait_ge(dve.steps, dve.n)
    dve.e.wait_ge(p.sem("decays_ready"), 1)
    for e in range(2):
        e_.tensor_tensor(p.iclr[:, e], p.iclr[:, e], p.inv_dec[:, e], ALU.mult).then_inc(dve.step(), 1)
    dve.e.wait_ge(dve.steps, dve.n)
    for e in range(2):
        e_.tensor_tensor(p.inv_dec[:, e], p.inv_dec[:, e], k_of[e], ALU.mult).then_inc(dve.step(), 1)
    dve.e.wait_ge(p.sem("decays_ready"), 2)
    gt = shaped(p.gt, 2, 4, NCH)
    for e in range(2):
        g = p.dec[:, e].rearrange("p q (c t) -> p q c t", t=CH)
        e_.tensor_copy(gt[:, e], g[:, :, :, CH - 1] if e == 0 else g[:, :, ::-1, 0]).then_inc(dve.step(), 1)
    dve.e.wait_ge(dve.steps, dve.n)
    for e in range(2):
        e_.tensor_tensor(p.dec[:, e], p.dec[:, e], r, ALU.mult).then_inc(dve.step(), 1)
    e_.memset(p.ST, 0.0).then_inc(dve.event("state_ready"), 1)
    dve.e.wait_ge(dve.steps, dve.n)
    dve.e.wait_ge(p.sem("state_ready"), 1)
    e_.tensor_tensor(p.ksum, p.ksum, p.keys_0, ALU.add).then_inc(dve.event("recurrence_in"), 1)
    dve.e.wait_ge(p.sem("recurrence_in"), 1)
    for q in range(PAIRS):
        ins = e_.scalar_tensor_tensor(p.kd[:, q, :], p.ksum[:, q, :], p.sp("r_k")[:, q:q + 1], r[:, q, :],
                                      ALU.mult, ALU.mult)
        if q == 3:
            ins.then_inc(dve.event("bonus_in"), 1)
        else:
            ins.then_inc(dve.step(), 1)
    by_dir = lambda ap: ap.rearrange("p (e q) t -> p e q t", e=2)
    eye8 = spread(p.c("eye64"), 1, 8)
    for j in range(2):
        dve.e.wait_ge(p.sem(f"gate_stored_{j}"), 16 * 6)
    causal = p.c("causal", 2, 2, CH)
    levels = p.c("level", 6, 2, CH)
    for m in range(NCH // 2):
        for i in range(2):
            for e in range(2):
                for dst in (p.BETA[i], p.KAPPA[i]):
                    dve.e.wait_ge(p.dve_tiles.full, p.dve_tiles.turn(dve))
                    bank = shaped(p.dve_tiles.take(dve), 4, 2, CH)
                    e_.tensor_tensor(dst[:, 4 * e:4 * e + 4], bank, spread(causal[:, e], 1, 4), ALU.mult).then_inc(
                        p.dve_tiles.drained, 1)
            dve.e.wait_ge(p.dve_tiles.drained, p.dve_tiles.taken["dve"])
            e_.tensor_tensor(by_dir(p.Pb[i]), by_dir(p.BETA[i][:, :, 0, :]), spread(levels[:, 0], 2, 4), ALU.mult).then_inc(
                dve.event("level_masked"), 1)
        if m == 0:
            for j in range(2):
                dve.e.wait_ge(p.dve_tiles.full, p.dve_tiles.turn(dve))
                bank = shaped(p.dve_tiles.take(dve), 2, S)
                sl = slice(2 * j, 2 * j + 2)
                e_.tensor_tensor(p.ksum[:, sl, :], bank, v[:, sl, :], ALU.mult).then_inc(p.dve_tiles.drained, 1)
        for n in range(6):
            for i in range(2):
                if n == 0:
                    dve.e.wait_ge(p.dve_tiles.full, p.dve_tiles.turn(dve))
                    bank = shaped(p.dve_tiles.take(dve), 8, CH)
                    e_.tensor_tensor(p.X[i], eye8, bank, ALU.subtract).then_inc(p.dve_tiles.drained, 1)
                if n == 0:
                    dve.e.wait_ge(p.sem("level_masked"), 12 * m + i + 1)
                    e_.tensor_tensor(p.XT[i], eye8, p.Pb[i], ALU.subtract).then_inc(dve.step(), 1)
                    dve.e.wait_ge(dve.steps, dve.n)
                for dst, other in () if n == 0 else ((p.XT[i], 1),) if n == 5 else ((p.X[i], 0), (p.XT[i], 1)):
                    dve.e.wait_ge(p.dve_tiles.full, p.dve_tiles.turn(dve))
                    bank = p.dve_tiles.take(dve)
                    for e in range(2):
                        part = level_columns(dst[:, 4 * e:4 * e + 4], n, e ^ other)
                        ins = e_.tensor_tensor(part, part, level_tile(bank, n, e), ALU.subtract)
                        if e:
                            ins.then_inc(p.dve_tiles.drained, 1)
                        else:
                            ins.then_inc(dve.step(), 1)
                if n < 5:
                    e_.tensor_tensor(by_dir(p.Pb[i]), by_dir(p.BETA[i][:, :, 0, :]), spread(levels[:, n + 1], 2, 4),
                                     ALU.mult).then_inc(dve.event("level_masked"), 1)
        for i in range(2):
            c = 2 * m + i
            dve.e.wait_ge(p.dve_tiles.full, p.dve_tiles.turn(dve))
            bank = shaped(p.dve_tiles.take(dve), 8, CH)
            dve.e.wait_ge(p.act_tiles.drained, p.mark[f"y{c}"])
            e_.tensor_tensor(p.ST, p.ST, bank, ALU.add).then_inc(p.dve_tiles.drained, 1)
            dve.e.wait_ge(p.dve_tiles.drained, p.dve_tiles.taken["dve"])
            whole = shaped(p.gt, 8, NCH)[:, :, c:c + 1].to_broadcast([P, 8, CH])
            e_.tensor_tensor(p.ST, p.ST, whole, ALU.mult).then_inc(dve.event("state_ready"), 1)
            dve.e.wait_ge(p.sem("state_ready"), c + 2)
    e_.tensor_tensor(p.kd, p.kd, p.kk, ALU.add).then_inc(dve.event("y_sum"), 1)
    dve.e.wait_ge(p.sem("y_sum"), 1)
    for j in range(2):
        dve.e.wait_ge(p.dve_tiles.full, p.dve_tiles.turn(dve))
        bank = shaped(p.dve_tiles.take(dve), 2, S)
        sl = slice(2 * j, 2 * j + 2)
        e_.scalar_tensor_tensor(p.kd[:, sl, :], bank, -1.0 / 64, p.kd[:, sl, :],
                                                       ALU.mult, ALU.add).then_inc(p.dve_tiles.drained, 1)
    dve.e.wait_ge(p.dve_tiles.drained, p.dve_tiles.taken["dve"])
    e_.tensor_tensor(p.kk, p.kd, p.kd, ALU.mult).then_inc(dve.event("y_sum"), 1)
    for j in range(2):
        dve.e.wait_ge(p.dve_tiles.full, p.dve_tiles.turn(dve))
        bank = shaped(p.dve_tiles.take(dve), 2, S)
        e_.tensor_copy(p.kk[:, 2 * j:2 * j + 2, :], bank).then_inc(p.dve_tiles.drained, 1)
    dve.e.wait_ge(p.dve_tiles.drained, p.dve_tiles.taken["dve"])
    e_.tensor_copy(p.small[:, 255:256], p.c("eps")).then_inc(dve.event("variances_in"), 1)
    dve.e.wait_ge(p.sem("y_rstd"), 1)
    e_.tensor_tensor(p.kd, p.kd, p.kk, ALU.mult).then_inc(dve.step(), 1)
    dve.e.wait_ge(dve.steps, dve.n)
    for q in range(PAIRS):
        e_.tensor_scalar(p.kd[:, q, :], p.kd[:, q, :], p.sp("ln_w")[:, q:q + 1], p.sp("ln_b")[:, q:q + 1],
                                 ALU.mult, ALU.add).then_inc(dve.step(), 1)
    dve.e.wait_ge(dve.steps, dve.n)
    e_.tensor_tensor(p.kd, p.kd, p.ksum, ALU.add).then_inc(dve.step(), 1)
    dve.e.wait_ge(dve.steps, dve.n)
    e_.tensor_tensor(p.ksum, p.kd, p.gate, ALU.mult).then_inc(dve.event("y_rwkv"), 1)
    for i in range(12):
        if i % 4 == 0:
            dve.e.wait_ge(p.sem("gates_ready"), i // 4 + 1)
        dve.e.wait_ge(p.dve_tiles.full, p.dve_tiles.turn(dve))
        bank = shaped(p.dve_tiles.take(dve), 2, S)
        d = slice(2 * (i % 4), 2 * (i % 4) + 2)
        g = 4 * BRANCH_ORDER[i // 4] + i % 4
        gates = p.gates[:, 2 * g:2 * g + 2, :]
        if i < 4:
            e_.tensor_tensor(p.merged[:, d, :], bank, gates, ALU.mult).then_inc(p.dve_tiles.drained, 1)
        else:
            e_.tensor_tensor(p.prod, bank, gates, ALU.mult).then_inc(p.dve_tiles.drained, 1)
            dve.e.wait_ge(p.dve_tiles.drained, p.dve_tiles.taken["dve"])
            ins = e_.tensor_tensor(p.merged[:, d, :], p.merged[:, d, :], p.prod, ALU.add)
            if i == 11:
                ins.then_inc(dve.event("merged"), 1)
            else:
                ins.then_inc(dve.step(), 1)
                dve.e.wait_ge(dve.steps, dve.n)
    for half in range(2):
        for b in range(NB):
            dve.e.wait_ge(p.dve_tiles.full, p.dve_tiles.turn(dve))
            bank = p.dve_tiles.take(dve)
            x = p.x[:, b, half * 512:(half + 1) * 512]
            e_.tensor_tensor(x, x, bank, ALU.add).then_inc(p.dve_tiles.drained, 1)
    for b in range(NB):
        diagonal_dve(p, dve, b, b + 1)
    norm_rows(p, dve, p.x, p.pre_rstd, p.hrow, "expert_rows")
    rows_to_columns_evac(p, dve, p.hT, p.sp("g_ffn"), KC, False)
    dve.e.wait_ge(p.dve_tiles.full, p.dve_tiles.turn(dve))
    bank = shaped(p.dve_tiles.take(dve)[:, 0:NB * E_N], NB, E_N)
    e_.tensor_copy(p.aff, bank).then_inc(p.dve_tiles.drained, 1)
    dve.e.wait_ge(p.dve_tiles.drained, p.dve_tiles.taken["dve"])
    e_.tensor_reduce(p.cols[:, 0:2], p.aff, AX, ALU.max).then_inc(dve.step(), 1)
    dve.e.wait_ge(dve.steps, dve.n)
    e_.tensor_scalar(p.cols[:, 2:4], p.cols[:, 0:2], -1.0, None, ALU.mult).then_inc(dve.event("logits"), 1)
    dve.e.wait_ge(p.sem("affinity_exps"), 1)
    e_.reciprocal(p.cols[:, 6:8], p.cols[:, 4:6]).then_inc(dve.step(), 1)
    dve.e.wait_ge(dve.steps, dve.n)
    e_.tensor_tensor(p.aff, p.aff, p.cols[:, 6:8].unsqueeze(2).to_broadcast([P, NB, E_N]), ALU.mult).then_inc(dve.event("affinities"), 1)
    e_.memset(p.ones[0:E_N, :], 1.0).then_inc(dve.step(), 1)
    dve.e.wait_ge(p.dve_tiles.full, p.dve_tiles.turn(dve))
    bank = p.dve_tiles.take(dve)
    e_.tensor_copy(p.affT[0:E_N, :], bank[0:E_N, 0:S]).then_inc(p.dve_tiles.drained, 1)
    dve.e.wait_ge(p.dve_tiles.drained, p.dve_tiles.taken["dve"])
    for _ in range(CAP // 8):
        e_.max(p.top[0:E_N, :], p.affT[0:E_N, :]).then_inc(dve.step(), 1)
        dve.e.wait_ge(dve.steps, dve.n)
        e_.match_replace(p.affT[0:E_N, :], p.top[0:E_N, :], p.affT[0:E_N, :], -1.0).then_inc(dve.step(), 1)
        dve.e.wait_ge(dve.steps, dve.n)
    e_.tensor_scalar(p.mask[0:E_N, :], p.affT[0:E_N, :], 0.0, None, ALU.is_lt).then_inc(dve.step(), 1)
    dve.e.wait_ge(dve.steps, dve.n)
    e_.tensor_tensor_scan(p.cum[0:E_N, :], p.ones[0:E_N, :], p.mask[0:E_N, :], 0.0, ALU.mult, ALU.add).then_inc(dve.step(), 1)
    dve.e.wait_ge(dve.steps, dve.n)
    e_.tensor_tensor(p.cum[0:E_N, :], p.cum[0:E_N, :], p.mask[0:E_N, :], ALU.mult).then_inc(dve.step(), 1)
    dve.e.wait_ge(dve.steps, dve.n)
    e_.tensor_scalar(p.cum[0:E_N, :], p.cum[0:E_N, :], 1.0, None, ALU.subtract).then_inc(dve.event("slots"), 1)
    dve.e.wait_ge(p.dve_tiles.full, p.dve_tiles.turn(dve))
    bank = shaped(p.dve_tiles.take(dve)[:, 0:NB * E_N], NB, E_N)
    e_.tensor_copy(p.posT, bank).then_inc(p.dve_tiles.drained, 1)
    dve.e.wait_ge(p.dve_tiles.drained, p.dve_tiles.taken["dve"])
    for b in range(NB):
        s3 = p.sel[:, b, :].rearrange("p (e c) -> p e c", c=CAP)
        e_.tensor_tensor(s3, spread(p.c("iota"), 1, E_N), p.posT[:, b, :].unsqueeze(2).to_broadcast([P, E_N, CAP]),
                                ALU.is_equal).then_inc(dve.step(), 1)
        dve.e.wait_ge(dve.steps, dve.n)
        e_.tensor_tensor(p.selw[:, b, :].rearrange("p (e c) -> p e c", c=CAP), s3,
                                p.aff[:, b, :].unsqueeze(2).to_broadcast([P, E_N, CAP]), ALU.mult).then_inc(dve.step(), 1)
        dve.e.wait_ge(dve.steps, dve.n)
    dve.finish("second", 0)
    p.reset_rings("dve")
    with dve.e.Fori(0, G_N) as g:
        experts_dve(p, dve, g)
        dve.finish("experts", g)
        p.reset_rings("dve")
    dve.e.wait_ge(p.sem("final_root"), 1)
    e_.reciprocal(p.pre_rstd, p.pre_rstd).then_inc(dve.step(), 1)
    dve.e.wait_ge(dve.steps, dve.n)
    for b in range(NB):
        ins = e_.scalar_tensor_tensor(p.x[:, b, :], p.x[:, b, :], p.pre_rstd[:, b:b + 1], p.sp("g_final"),
                                      ALU.mult, ALU.mult)
        ins.then_inc(dve.event("y_final"), 1)


def second_pool(p, pool):
    pool.e.wait_ge(p.act_tiles.drained, p.mark["raw"])
    e_ = pool.e
    m0 = p.cols[:, 0:15]
    e_.tensor_tensor(m0, p.sp("mu_prev"), p.sp("mu_next"), ALU.add).then_inc(pool.step(), 1)
    pool.e.wait_ge(pool.steps, pool.n)
    e_.tensor_scalar(m0, m0, -1.0, 1.0, ALU.mult, ALU.add).then_inc(pool.step(), 1)
    pool.e.wait_ge(pool.steps, pool.n)
    raw, out = p.raw[:, 0:15, :], p.shifted
    near = p.zp_wide
    for shift, gain in ((0, m0), (1, p.sp("mu_prev")), (-1, p.sp("mu_next"))):
        dst, src = slice(max(shift, 0), S + min(shift, 0)), slice(max(-shift, 0), S + min(-shift, 0))
        g = gain.unsqueeze(2).to_broadcast([P, 15, S - abs(shift)])
        if shift == 0:
            e_.tensor_tensor(out, raw, g, ALU.mult).then_inc(pool.step(), 1)
            pool.e.wait_ge(pool.steps, pool.n)
            continue
        for c0, c1 in ((0, 8), (8, 15)):
            part = near[:, 0:c1 - c0, 0:S - 1]
            e_.tensor_tensor(part, raw[:, c0:c1, src], g[:, c0:c1], ALU.mult).then_inc(pool.step(), 1)
            pool.e.wait_ge(pool.steps, pool.n)
            ins = e_.tensor_tensor(out[:, c0:c1, dst], out[:, c0:c1, dst], part, ALU.add)
            if shift < 0 and c1 == 15:
                ins.then_inc(pool.event("shift_done"), 1)
            else:
                ins.then_inc(pool.step(), 1)
                pool.e.wait_ge(pool.steps, pool.n)
    z, a, b = p.raw[:, 15:19, :], p.zp[0], p.zp[1]
    pool.e.wait_ge(p.sem("shift_done"), 1)
    e_.memset(flat(a), 0.0).then_inc(pool.step(), 1)
    pool.e.wait_ge(pool.steps, pool.n)
    e_.memset(flat(b), 0.0).then_inc(pool.step(), 1)
    pool.e.wait_ge(pool.steps, pool.n)
    e_.tensor_copy(a[:, :, 8:8 + S], z).then_inc(pool.step(), 1)
    pool.e.wait_ge(pool.steps, pool.n)
    src, dst = a, b
    for n in range(4):
        w = 1 << n
        e_.tensor_tensor(dst[:, n:4, 0:272 - w], src[:, n:4, 0:272 - w], src[:, n:4, w:272], ALU.add).then_inc(pool.step(), 1)
        pool.e.wait_ge(pool.steps, pool.n)
        lo = 8 - w
        e_.tensor_tensor(p.pooled[:, n, :], dst[:, n, lo:lo + S], p.c("pool_cnt", 4, S)[:, n, :], ALU.mult).then_inc(pool.step(), 1)
        pool.e.wait_ge(pool.steps, pool.n)
        src, dst = dst, src
    e_.tensor_tensor(p.pooled, p.pooled, z, ALU.subtract).then_inc(pool.event("pooled"), 1)
    pool.e.wait_ge(p.sem("keys_normed"), 1)
    pool.e.wait_ge(p.sem("decays_ready"), 3)
    for e in range(2):
        ins = e_.tensor_tensor(p.sig[:, e], p.sig[:, e], p.kk, ALU.mult)
        if e:
            ins.then_inc(pool.event("alpha_ready"), 1)
        else:
            ins.then_inc(pool.step(), 1)
    pool.finish("second", 0)
    with pool.e.Fori(0, G_N) as g:
        pool.finish("experts", g)


def build(nc, stream, x, mem, pos_row, pos_col, const, layer_par, out):
    from contextlib import ExitStack
    with ExitStack() as ctx:
        p = Program(nc, ctx, None)
        first_buffers(p)
        p.pos = p.sb("positions", 258, I32)
        p.gate_dram = nc.dram_tensor("gate_dram", (12, P, 512), F32, kind="Internal").ap()
        loads = ["const_loaded", "mem_loaded", "x_loaded", "positions_loaded", "layer_params"]
        for name in loads + ["pe_steps", "act_steps", "dve_steps", "pool_steps", "layer_met", "start_met",
                             "second_met", "experts_met", "y_final", "stored", "passed"]:
            p.sem(name)
        block = ctx.enter_context(nc.Block())

        def reset(eng):
            p.reset_rings(eng.name)

        @block.tensor
        def _(e):
            pe = Engine(p, e, "pe")
            w = Weights(p, pe)
            prologue_pe(p, pe, w)
            pe.finish("start", 0)
            reset(pe)
            with e.Fori(0, DEPTH) as l:
                w.start(l * (16 * LAYER_UNITS // SLOTS), p.slots, p.slot_loaded, p.slots_free)
                layer_pe(p, pe, w, l)
                pe.finish("layer", l)
                reset(pe)
            second_buffers(p)
            second_pe(p, pe, w)

        @block.scalar
        def _(e):
            first_buffers(p)
            act = Engine(p, e, "act")
            act.e.dma_start(p.const[:, :], const).then_inc(p.sem("const_loaded"), 16)
            act.e.dma_start(p.x, x.rearrange("(b p) d -> p b d", p=P)).then_inc(p.sem("x_loaded"), 16)
            act.e.dma_start(p.par[:, 0:EARLY_W], layer_par[0:P, 0:EARLY_W]).then_inc(p.sem("layer_params"), 16)
            prologue_act(p, act)
            act.finish("start", 0)
            reset(act)
            with e.Fori(0, DEPTH) as l:
                layer_act(p, act, l, layer_par)
                act.finish("layer", l)
                reset(act)
            second_buffers(p)
            second_act(p, act)

        @block.vector
        def _(e):
            first_buffers(p)
            dve = Engine(p, e, "dve")
            prologue_dve(p, dve)
            dve.finish("start", 0)
            reset(dve)
            with e.Fori(0, DEPTH) as l:
                layer_dve(p, dve, l)
                dve.finish("layer", l)
                reset(dve)
            second_buffers(p)
            second_dve(p, dve)

        @block.gpsimd
        def _(e):
            first_buffers(p)
            pool = Engine(p, e, "pool")
            e.dma_start(p.xv, mem.rearrange("(b p) d -> p b d", p=P)).then_inc(p.sem("mem_loaded"), 16)
            e.dma_start(p.pos[:, 0:256], pos_row).then_inc(p.sem("positions_loaded"), 16)
            e.dma_start(p.pos[:, 256:258], pos_col).then_inc(p.sem("positions_loaded"), 16)
            pool.finish("start", 0)
            with e.Fori(0, DEPTH) as l:
                layer_pool(p, pool, l)
                pool.finish("layer", l)
            second_buffers(p)
            second_pool(p, pool)

        @block.sync
        def _(e):
            e.sem_inc(p.slots_free, SLOTS)
            with e.Fori(0, DENSE_UNITS // SLOTS) as r:
                for s in range(SLOTS):
                    e.wait_ge(p.slots_free, r * SLOTS + (s + 1))
                    e.dma_start(p.slots[s], stream[bass.ds((r * SLOTS + s) * P, P), :]).then_inc(
                        p.slot_loaded[s], 16)
            for s in range(DENSE_UNITS % SLOTS):
                e.wait_ge(p.slots_free, DENSE_UNITS // SLOTS * SLOTS + s + 1)
                u = DENSE_UNITS // SLOTS * SLOTS + s
                e.dma_start(p.slots[s], stream[u * P:(u + 1) * P, :]).then_inc(p.slot_loaded[s], 16)
            e.wait_ge(p.sem("recurrence_left"), 1)
            for s in range(SLOTS, EXPERT_SLOTS - 1):
                e.dma_start(p.expert_slots[s], stream[(DENSE_UNITS + s) * P:(DENSE_UNITS + s + 1) * P, :]).then_inc(
                    p.expert_slot_loaded[s], 16)
            for s in range(SLOTS):
                e.wait_ge(p.slots_free, DENSE_UNITS + s + 1)
                e.dma_start(p.expert_slots[s], stream[(DENSE_UNITS + s) * P:(DENSE_UNITS + s + 1) * P, :]).then_inc(
                    p.expert_slot_loaded[s], 16)
            e.wait_ge(p.sem("second_met"), 8)
            s = EXPERT_SLOTS - 1
            e.dma_start(p.expert_slots[s], stream[(DENSE_UNITS + s) * P:(DENSE_UNITS + s + 1) * P, :]).then_inc(
                p.expert_slot_loaded[s], 16)
            with e.Fori(0, EXPERT_UNITS // EXPERT_SLOTS - 1) as r:
                for s in range(EXPERT_SLOTS):
                    e.wait_ge(p.expert_slots_used, r * EXPERT_SLOTS + (s + 1))
                    e.dma_start(p.expert_slots[s], stream[bass.ds(
                        (r * EXPERT_SLOTS + (DENSE_UNITS + EXPERT_SLOTS + s)) * P, P), :]).then_inc(
                            p.expert_slot_loaded[s], 16)
            e.wait_ge(p.sem("y_final"), NB)
            e.dma_start(out.rearrange("(b p) d -> p b d", p=P), p.x).then_inc(p.sem("stored"), 16)
            e.wait_ge(p.sem("stored"), 16)



def packed(spec, width, values):
    out = np.zeros((P, width), np.float32)
    for name, (a, b) in spec.items():
        v = np.asarray(values[name], np.float32)
        out[:, a:b] = v.reshape(v.shape[0], b - a) if v.shape[0] == P else np.broadcast_to(v.reshape(1, b - a), (P, b - a))
    return out


def by_chunk(v):
    return np.ascontiguousarray(np.asarray(v).reshape(-1, P).T)


def unit(a):
    out = np.zeros((P, UNIT), np.float32)
    a = a.reshape(P, -1)
    out[:, 0:a.shape[1]] = a
    return out


def column_units(w):
    K, n = w.shape
    u = w.reshape(K // P, P, n).transpose(1, 0, 2)
    return [unit(np.concatenate([u[:, :, c:c + P].reshape(P, -1) for c in range(a, min(a + 256, n), P)], axis=1))
            for a in range(0, n, 256)]


def row_units(w, width, split=2):
    K, n = w.shape
    u = w.reshape(K // P, P, n).transpose(1, 0, 2)
    kn = K // P // split
    return [unit(u[:, h * kn:(h + 1) * kn, a:a + width]) for a in range(0, n, width) for h in range(split)]


def constants():
    t = np.arange(P)
    s64 = t % 64
    f = np.arange(64)
    c = {"ident": np.eye(P), "inv": 10000.0 ** (-np.arange(16) / np.float32(16))}
    q = (np.arange(NB)[None, :] * P + t[:, None])[:, :, None]
    c["swa_far"] = np.where(np.abs(q - np.arange(S)) <= 128, 0.0, FAR)
    c["headsum"] = (t[:, None] // 64 == t[None, :] // 64)
    c["eye64"] = s64[:, None] == f
    before = [s64[:, None] < f, s64[:, None] > f]
    upto = [s64[:, None] <= f, s64[:, None] >= f]
    c["causal"] = np.stack([np.stack([before[e], upto[e]], 1) for e in range(2)], 1)
    level = []
    for n in range(6):
        b = 1 << n
        cross = (s64[:, None] // (2 * b) == f // (2 * b)) & (s64[:, None] // b != f // b)
        level.append(np.stack([cross & m for m in before], 1))
    c["level"] = np.stack(level, 1)
    c["scan_keep"] = (np.arange(S) % CH != 0)
    tok = np.arange(S)
    freqs = (np.float32(10000.0) ** (-np.arange(0, 32, 2, dtype=np.float32) / np.float32(32))).astype(np.float32)
    ang = np.concatenate([(tok // 64).astype(np.float32)[:, None] * freqs,
                          (tok % 64).astype(np.float32)[:, None] * freqs], axis=1)
    c["cos"] = np.cos(ang).reshape(NB, P, 32).transpose(1, 0, 2)
    c["sin"] = np.sin(ang).reshape(NB, P, 32).transpose(1, 0, 2)
    cnt = []
    for w in (2, 4, 8, 16):
        lo = w // 2
        hi = w - lo - 1
        cnt.append(1.0 / (np.clip(tok + hi + 1, 0, S) - np.clip(tok - lo, 0, S)))
    c["pool_cnt"] = np.stack(cnt).reshape(1, -1)
    c["iota"] = np.arange(32)
    c["eps"], c["ln_eps"], c["half_pi"] = [EPS], [LN_EPS], [math.pi / 2]
    out = {}
    for k, v in c.items():
        v = np.asarray(v, np.float32)
        out[k] = v if v.shape[0] == P else v.reshape(1, -1)
    return packed(CONST, CONST_W, out)


SWA_ORDER = [h for j in range(4) for h in (j, j + 4)]


def heads(order, size=64, start=0):
    return np.concatenate([start + np.arange(h * size, (h + 1) * size) for h in order])


def layer_arrays(i, l):
    w = i["w_in"][l]
    off = np.cumsum([0, 256, 256, 256, 256, 128, 32, 512, 128, 128])
    aq, ak, av, bq, bkv, bkr, cq, ck, cv = [w[:, off[j]:off[j + 1]] for j in range(9)]
    units = row_units(np.concatenate([bq, bkv, bkr], 1), 416)
    units += row_units(np.concatenate([av, cv], 1), 384)
    units += column_units(np.concatenate([aq, ak, cq[:, heads(SWA_ORDER)], ck], 1))
    units += column_units(i["w_xkv"][l][:, 0:D]) + row_units(i["w_xkv"][l][:, D:], 512)
    wo = i["w_out"][l]
    units += row_units(np.concatenate([wo[0:512], wo[512:][heads(SWA_ORDER)]], 0), 512)
    units += column_units(i["w_xq"][l]) + row_units(i["w_xo"][l], 512)
    wf, wd = i["w_ffn_in"][l], i["w_ffn_out"][l]
    gu = [column_units(np.concatenate([wf[:, f * P:(f + 1) * P], wf[:, FF + f * P:FF + (f + 1) * P]], 1))[0]
          for f in range(FC)]
    down = [unit(wd[j * 256:(j + 1) * 256].reshape(2, P, D).transpose(1, 0, 2)) for j in range(FC // 2)]
    for j in range(FC // 2):
        units += gu[2 * j:2 * j + 2]
        if j:
            units.append(down[j - 1])
    units.append(down[-1])
    units += [np.zeros((P, UNIT), np.float32)] * (LAYER_UNITS - len(units))
    init = 0.8 - 0.6 * math.exp(-0.3 * l)
    par = packed(LAYER, LAYER_W, {
        "g_mix_pre": by_chunk(i["g_mix_pre"][l]), "g_x_pre": by_chunk(i["g_x_pre"][l]),
        "g_x_mem": by_chunk(i["g_x_mem"][l]), "g_ffn_pre": by_chunk(i["g_ffn_pre"][l]),
        "g_q": by_chunk(i["mla_q_norm_g"][l]), "g_kv": by_chunk(i["mla_kv_norm_g"][l]),
        "g_diff": np.concatenate([i["diff_head_g"][l]] * 2).reshape(P, 1), "sinks": i["swa_sinks"][l].reshape(1, -1),
        "lambda": i["diff_lambda"][l].reshape(1, -1), "lam_init": np.array([init]), "lam_rest": np.array([1 - init]),
        "kv_up": i["mla_w_kv_up"][l], "q_up": i["mla_w_q_up"][l].reshape(2, P, 384).transpose(1, 0, 2),
        "g_mix_post": i["g_mix_post"][l].reshape(1, -1), "g_x_post": i["g_x_post"][l].reshape(1, -1),
        "g_ffn_post": i["g_ffn_post"][l].reshape(1, -1),
    })
    return units, par


def second_arrays(i):
    w = i["w_in_2"][0]
    rw, pool, att, gate = np.split(w, [1920, 2432, 3200], axis=1)
    att = np.concatenate([att[:, heads(SWA_ORDER)], att[:, 512:]], 1)
    units = row_units(att, 256, 1) + column_units(np.concatenate([rw, pool], 1)) + column_units(gate)
    for b in ("pool", "attn", "rwkv"):
        wb = i[f"w_branch_{b}_2"][0]
        if b == "attn":
            wb = wb[heads(SWA_ORDER)]
        u = wb.reshape(4, P, D).transpose(1, 0, 2)
        units += [unit(np.concatenate([u[:, :, c:c + P].reshape(P, -1) for c in range(a, a + 512, P)], 1))
                  for a in range(0, D, 512)]
    units += row_units(i["w_out_2"][0], 512)
    assert len(units) == BLOCK2_UNITS
    for g in range(G_N):
        def experts(w, f):
            return [unit(w[g * GE + e].reshape(KC, P, D)[4 * h:4 * h + 4, :, f * 512:(f + 1) * 512].transpose(1, 0, 2))
                    for h in range(2) for e in range(GE)]
        for f in range(2):
            units += experts(i["exp_gate_2"][0], f) + experts(i["exp_up_2"][0], f)
        for f in range(2):
            units += experts(i["exp_down_2"][0], f)
    col = lambda n: by_chunk(i[n + "_2"][0])
    both = lambda n: np.concatenate([by_chunk(i[n + "_2"][0, e]) for e in range(2)], 1)
    row = lambda n: i[n + "_2"][0].reshape(1, -1)
    par = packed(SECOND, LAYER_W, {
        "g_mix": col("norm_mix"), "mu_prev": col("shift_prev"), "mu_next": col("shift_next"),
        "w0": both("rwkv_w0"), "a0": both("rwkv_a0"), "k_k": col("rwkv_k_k"), "k_a": col("rwkv_k_a"),
        "r_k": col("rwkv_r_k"), "ln_w": col("rwkv_ln_w"), "ln_b": col("rwkv_ln_b"), "pool_scale": col("pool_scale"),
        "g_ffn": col("norm_ffn"), "q_norm": row("q_norm"), "k_norm": row("k_norm"),
        "router": i["router_2"][0].reshape(KC, P, E_N).transpose(1, 0, 2),
        "w2": i["rwkv_w2_2"][0].reshape(P, 512), "a2": i["rwkv_a2_2"][0].reshape(P, 512),
        "g2": i["rwkv_g2_2"][0], "pool_w": i["pool_w_2"][0].transpose(1, 0, 2),
        "g_final": i["norm_final_2"].reshape(1, -1),
    })
    return units, par


def kernel(**inputs):
    import concourse.bacc as bacc
    from concourse.bass_utils import run_bass_kernel_spmd

    i = {k: np.asarray(v) for k, v in inputs.items()}
    units, pars = [], []
    for l in range(DEPTH):
        u, par = layer_arrays(i, l)
        units += u
        pars.append(par)
    u2, second = second_arrays(i)
    units += u2
    pos = i["positions"].reshape(-1)
    arrays = {
        "stream": np.concatenate(units, 0), "x": i["x"].reshape(S, D), "mem": i["mem"].reshape(S, D),
        "pos_row": np.ascontiguousarray(np.broadcast_to(pos[None, :], (P, S))),
        "pos_col": np.ascontiguousarray(pos.reshape(NB, P).T),
        "const": constants(), "layer_par": np.concatenate(pars + [second], 0),
    }
    nc = bacc.Bacc("TRN2", target_bir_lowering=False, num_devices=1)
    aps = [nc.dram_tensor("in_" + k, a.shape, mybir.dt.from_np(a.dtype), kind="ExternalInput").ap() for k, a in arrays.items()]
    out = nc.dram_tensor("out", (S, D), F32, kind="ExternalOutput").ap()
    build(nc, *aps, out)
    r = run_bass_kernel_spmd(nc, [{"in_" + k: a for k, a in arrays.items()}], core_ids=[0])
    return r.results[0]["out"].reshape(1, S, D)
```
